# Optimizing a Trainium2 kernel written in Bass

```python
import jax, jax.numpy as jnp
from jax import lax
import numpy as np

D_MODEL = 1024
BATCH = 1
SEQ = 256
DEPTH = 2

CHUNK = 64
HEAD_DIM = 64
ROT_DIM = HEAD_DIM // 4
ROPE_THETA = 500000.0
N_HEADS_A = 6
N_HEADS_B = 5
N_HEADS_C = 5
WIDTH_A = N_HEADS_A * HEAD_DIM
WIDTH_B = N_HEADS_B * HEAD_DIM
WIDTH_C = N_HEADS_C * HEAD_DIM
MIX_WIDTH = WIDTH_A + WIDTH_B + WIDTH_C
IDX_HEADS = 8
IDX_DIM = 64
TOPK_MAX = 256
PREV_CHUNKS = 8
BAND = (PREV_CHUNKS + 1) * CHUNK
REL_CLIP = 128
Q_BLOCK = 128
N_BRANCH = 3
FFN_HIDDEN = -(-8 * D_MODEL // (3 * 256)) * 256
RMS_EPS = 1e-6
FORGET_BIAS_LO = 2.0
FORGET_BIAS_HI = 6.0
SPLIT_SIZES = (WIDTH_A, WIDTH_A, WIDTH_A, IDX_HEADS * IDX_DIM, IDX_DIM, IDX_HEADS,
               3 * WIDTH_B, 3 * WIDTH_C, N_HEADS_C, N_BRANCH * D_MODEL)
IN_WIDTH = sum(SPLIT_SIZES)


def rmsnorm(x, g):
    xf = x.astype(jnp.float32)
    y = xf * lax.rsqrt(jnp.mean(xf * xf, axis=-1, keepdims=True) + RMS_EPS)
    return (y * g.astype(jnp.float32)).astype(x.dtype)

def rope_tables(positions):
    inv = ROPE_THETA ** (-jnp.arange(0, ROT_DIM, 2, dtype=jnp.float32) / ROT_DIM)
    ang = positions.astype(jnp.float32)[..., None] * inv
    return jnp.cos(ang), jnp.sin(ang)

def partial_rope(t, cos, sin):
    half = ROT_DIM // 2
    cs = cos[:, :, None, :].astype(t.dtype)
    sn = sin[:, :, None, :].astype(t.dtype)
    x1 = t[..., :half]
    x2 = t[..., half:ROT_DIM]
    return jnp.concatenate([x1 * cs - x2 * sn, x2 * cs + x1 * sn, t[..., ROT_DIM:]], axis=-1)

def dsa_attention(q, k, v, q_idx, k_idx, w_idx):
    B, S = q.shape[0], q.shape[1]
    topk = min(TOPK_MAX, S // 4)
    n_blk = S // Q_BLOCK
    key_chunk = jnp.arange(S) // CHUNK
    scale = HEAD_DIM ** -0.5
    kf = k_idx.astype(jnp.float32)
    gather = jax.vmap(lambda arr, ix: arr[ix])

    def block(i):
        start = i * Q_BLOCK
        qs = lax.dynamic_slice_in_dim(q, start, Q_BLOCK, axis=1)
        qis = lax.dynamic_slice_in_dim(q_idx, start, Q_BLOCK, axis=1).astype(jnp.float32)
        ws = lax.dynamic_slice_in_dim(w_idx, start, Q_BLOCK, axis=1).astype(jnp.float32)
        q_chunk = (start + jnp.arange(Q_BLOCK)) // CHUNK
        idx_scores = jnp.einsum('bqhs,bqh->bqs',
                                jax.nn.relu(jnp.einsum('bqhd,bsd->bqhs', qis, kf)), ws)
        adm = key_chunk[None, :] <= q_chunk[:, None]
        idx_scores = jnp.where(adm[None], idx_scores, -jnp.inf)
        _, sel = lax.top_k(idx_scores, topk)
        valid = (sel // CHUNK) <= q_chunk[None, :, None]
        k_sel = gather(k, sel)
        v_sel = gather(v, sel)
        logits = jnp.einsum('bqhd,bqkhd->bhqk', qs, k_sel).astype(jnp.float32) * scale
        logits = jnp.where(valid[:, None], logits, -jnp.inf)
        p = jax.nn.softmax(logits, axis=-1).astype(v.dtype)
        return jnp.einsum('bhqk,bqkhd->bqhd', p, v_sel)

    out = lax.map(block, jnp.arange(n_blk))
    return jnp.moveaxis(out, 0, 1).reshape(B, S, -1)

def chunk_band_attention(q, k, v, rel_bias):
    B, S, H, Dh = q.shape
    n_c = S // CHUNK
    pad = PREV_CHUNKS * CHUNK
    qc = q.reshape(B, n_c, CHUNK, H, Dh)
    kp = jnp.pad(k, ((0, 0), (pad, 0), (0, 0), (0, 0))).reshape(B, n_c + PREV_CHUNKS, CHUNK, H, Dh)
    vp = jnp.pad(v, ((0, 0), (pad, 0), (0, 0), (0, 0))).reshape(B, n_c + PREV_CHUNKS, CHUNK, H, Dh)
    kband = jnp.concatenate([kp[:, j:j + n_c] for j in range(PREV_CHUNKS + 1)], axis=2)
    vband = jnp.concatenate([vp[:, j:j + n_c] for j in range(PREV_CHUNKS + 1)], axis=2)
    logits = jnp.einsum('bcqhd,bckhd->bchqk', qc, kband).astype(jnp.float32) * (Dh ** -0.5)
    qi = jnp.arange(CHUNK)
    kj = jnp.arange(BAND)
    dist = jnp.clip(qi[:, None] + pad - kj[None, :], -REL_CLIP, REL_CLIP) + REL_CLIP
    bias = rel_bias[:, dist].astype(jnp.float32)
    band_chunk = jnp.arange(n_c)[:, None] - PREV_CHUNKS + kj[None, :] // CHUNK
    valid = band_chunk >= 0
    logits = jnp.where(valid[None, :, None, None, :], logits + bias[None, None], -jnp.inf)
    p = jax.nn.softmax(logits, axis=-1).astype(v.dtype)
    out = jnp.einsum('bchqk,bckhd->bcqhd', p, vband)
    return out.reshape(B, S, H * Dh)

def forgetting_attention(q, k, v, f_logit):
    B, S, H, Dh = q.shape
    n_blk = S // Q_BLOCK
    log_f = jax.nn.log_sigmoid(f_logit.astype(jnp.float32))
    F = jnp.moveaxis(jnp.cumsum(log_f, axis=1), 1, 2)
    key_pos = jnp.arange(S)
    scale = Dh ** -0.5

    def block(i):
        start = i * Q_BLOCK
        qs = lax.dynamic_slice_in_dim(q, start, Q_BLOCK, axis=1)
        Fq = lax.dynamic_slice_in_dim(F, start, Q_BLOCK, axis=2)
        logits = (jnp.einsum('bqhd,bshd->bhqs', qs, k).astype(jnp.float32) * scale
                  + Fq[..., :, None] - F[:, :, None, :])
        qpos = start + jnp.arange(Q_BLOCK)
        logits = jnp.where((key_pos[None, :] <= qpos[:, None])[None, None], logits, -jnp.inf)
        p = jax.nn.softmax(logits, axis=-1).astype(v.dtype)
        return jnp.einsum('bhqs,bshd->bqhd', p, v)

    out = lax.map(block, jnp.arange(n_blk))
    return jnp.moveaxis(out, 0, 1).reshape(B, S, H * Dh)

def hybrid_mixer(h, cos, sin, w_in, b_in, rel_bias, w_branch, w_out):
    B, S, D = h.shape
    proj = h @ w_in + b_in
    parts = []
    off = 0
    for size in SPLIT_SIZES:
        parts.append(proj[..., off:off + size])
        off += size
    qa, ka, va, qi, ki, wi, qkv_b, qkv_c, f_c, gate_logits = parts
    qa = partial_rope(qa.reshape(B, S, N_HEADS_A, HEAD_DIM), cos, sin)
    ka = partial_rope(ka.reshape(B, S, N_HEADS_A, HEAD_DIM), cos, sin)
    va = va.reshape(B, S, N_HEADS_A, HEAD_DIM)
    qi = partial_rope(qi.reshape(B, S, IDX_HEADS, IDX_DIM), cos, sin)
    ki = partial_rope(ki[:, :, None, :], cos, sin)[:, :, 0, :]
    wi = wi * (IDX_HEADS ** -0.5 * IDX_DIM ** -0.5)
    o_a = dsa_attention(qa, ka, va, qi, ki, wi)
    qkv_b = qkv_b.reshape(B, S, 3, N_HEADS_B, HEAD_DIM)
    o_b = chunk_band_attention(qkv_b[:, :, 0], qkv_b[:, :, 1], qkv_b[:, :, 2], rel_bias)
    qkv_c = qkv_c.reshape(B, S, 3, N_HEADS_C, HEAD_DIM)
    o_c = forgetting_attention(qkv_c[:, :, 0], qkv_c[:, :, 1], qkv_c[:, :, 2], f_c)
    gates = jax.nn.sigmoid(gate_logits.reshape(B, S, N_BRANCH, D))
    y = (gates[:, :, 0] * (o_a @ w_branch[:WIDTH_A])
         + gates[:, :, 1] * (o_b @ w_branch[WIDTH_A:WIDTH_A + WIDTH_B])
         + gates[:, :, 2] * (o_c @ w_branch[WIDTH_A + WIDTH_B:]))
    return y @ w_out

def swiglu(h, w_ffn_in, w_ffn_out):
    gu = h @ w_ffn_in
    g, u = gu[..., :FFN_HIDDEN], gu[..., FFN_HIDDEN:]
    return (jax.nn.silu(g) * u) @ w_ffn_out

def first_inputs(seed: int = 0) -> dict:
    key = jax.random.key(seed)
    ks = jax.random.split(key, 16)
    f32 = jnp.float32
    D = D_MODEL
    nrm = jax.random.normal
    x = nrm(ks[0], (BATCH, SEQ, D), f32)
    c = nrm(ks[1], (BATCH, D), f32)
    offset = jax.random.randint(ks[2], (BATCH, 1), 0, 4096, dtype=jnp.int32)
    positions = offset + jnp.arange(SEQ, dtype=jnp.int32)[None, :]
    ada_w = 0.5 * D ** -0.5 * nrm(ks[3], (DEPTH, D, 6 * D), f32)
    ada_b = 0.01 * nrm(ks[4], (DEPTH, 6 * D), f32)
    norm1_g = 1.0 + 0.05 * nrm(ks[5], (DEPTH, D), f32)
    w_in = D ** -0.5 * nrm(ks[6], (DEPTH, D, IN_WIDTH), f32)
    f_off = sum(SPLIT_SIZES[:8])
    forget_b = jax.random.uniform(ks[7], (DEPTH, N_HEADS_C), f32, FORGET_BIAS_LO, FORGET_BIAS_HI)
    b_in = (0.01 * nrm(ks[8], (DEPTH, IN_WIDTH), f32)).at[:, f_off:f_off + N_HEADS_C].add(forget_b)
    rel_bias = 0.5 * nrm(ks[9], (DEPTH, N_HEADS_B, 2 * REL_CLIP + 1), f32)
    w_branch = WIDTH_B ** -0.5 * nrm(ks[10], (DEPTH, MIX_WIDTH, D), f32)
    w_out = D ** -0.5 * nrm(ks[11], (DEPTH, D, D), f32)
    norm2_g = 1.0 + 0.05 * nrm(ks[12], (DEPTH, D), f32)
    w_ffn_in = D ** -0.5 * nrm(ks[13], (DEPTH, D, 2 * FFN_HIDDEN), f32)
    w_ffn_out = FFN_HIDDEN ** -0.5 * nrm(ks[14], (DEPTH, FFN_HIDDEN, D), f32)
    final_g = 1.0 + 0.05 * nrm(ks[15], (D,), f32)
    return {'x': x, 'c': c, 'positions': positions, 'ada_w': ada_w, 'ada_b': ada_b,
            'norm1_g': norm1_g, 'w_in': w_in, 'b_in': b_in, 'rel_bias': rel_bias,
            'w_branch': w_branch, 'w_out': w_out, 'norm2_g': norm2_g,
            'w_ffn_in': w_ffn_in, 'w_ffn_out': w_ffn_out, 'final_g': final_g}

def first_block(x, c, positions, ada_w, ada_b, norm1_g, w_in, b_in, rel_bias,
              w_branch, w_out, norm2_g, w_ffn_in, w_ffn_out, final_g):
    cos, sin = rope_tables(positions)
    cond = jax.nn.silu(c)
    for l in range(DEPTH):
        mod = (cond @ ada_w[l] + ada_b[l])[:, None, :]
        sh1, sc1, g1, sh2, sc2, g2 = jnp.split(mod, 6, axis=-1)
        h = rmsnorm(x, norm1_g[l]) * (1 + sc1) + sh1
        x = x + g1 * hybrid_mixer(h, cos, sin, w_in[l], b_in[l], rel_bias[l], w_branch[l], w_out[l])
        h = rmsnorm(x, norm2_g[l]) * (1 + sc2) + sh2
        x = x + g2 * swiglu(h, w_ffn_in[l], w_ffn_out[l])
    return rmsnorm(x, final_g)


N_MIXERS = 2
MOBA_HEADS = 16
MOBA_BLOCK = 256
MOBA_TOPK = 3
MOBA_Q_CHUNK = 32
DIL_GROUPS = ((128, 1), (512, 4), (2048, 16))
DIL_HEADS_PER_GROUP = 4
DIL_HEADS = DIL_HEADS_PER_GROUP * len(DIL_GROUPS)
DIL_BLOCK = 128
D_FF = 4 * D_MODEL
ROPE_THETA_2 = 10000.0
LN_EPS = 1e-5
DEEPNORM_ALPHA = (2.0 * DEPTH) ** 0.25
DEEPNORM_BETA = (8.0 * DEPTH) ** -0.25
N_LAYERS_A = (DEPTH + N_MIXERS - 1) // N_MIXERS
N_LAYERS_B = DEPTH // N_MIXERS


def layer_norm(x, g, b):
    xf = x.astype(jnp.float32)
    mu = jnp.mean(xf, axis=-1, keepdims=True)
    var = jnp.mean(jnp.square(xf - mu), axis=-1, keepdims=True)
    y = (xf - mu) * lax.rsqrt(var + LN_EPS)
    return (y * g.astype(jnp.float32) + b.astype(jnp.float32)).astype(x.dtype)

def rotary_tables(seq, dtype):
    inv = 1.0 / (ROPE_THETA_2 ** (jnp.arange(0, HEAD_DIM, 2, dtype=jnp.float32) / HEAD_DIM))
    ang = jnp.arange(seq, dtype=jnp.float32)[:, None] * inv[None, :]
    return jnp.cos(ang).astype(dtype), jnp.sin(ang).astype(dtype)

def apply_rotary(t, cos, sin):
    t1, t2 = jnp.split(t, 2, axis=-1)
    c = cos[None, :, None, :]
    s = sin[None, :, None, :]
    return jnp.concatenate([t1 * c - t2 * s, t2 * c + t1 * s], axis=-1)

def moba_attention(x, w_qkv, w_o, cos, sin):
    B, S, _ = x.shape
    H, dh, BLK, QC = MOBA_HEADS, HEAD_DIM, MOBA_BLOCK, MOBA_Q_CHUNK
    qkv = (x @ w_qkv).reshape(B, S, 3, H, dh)
    q = apply_rotary(qkv[:, :, 0], cos, sin) * (dh ** -0.5)
    k = apply_rotary(qkv[:, :, 1], cos, sin)
    v = qkv[:, :, 2]
    pad = (-S) % BLK
    Sp = S + pad
    nb = Sp // BLK
    padw = ((0, 0), (0, pad), (0, 0), (0, 0))
    q = jnp.pad(q, padw).transpose(0, 2, 1, 3)
    k = jnp.pad(k, padw).transpose(0, 2, 1, 3)
    v = jnp.pad(v, padw).transpose(0, 2, 1, 3)
    k_blk = k.reshape(B, H, nb, BLK, dh)
    v_blk = v.reshape(B, H, nb, BLK, dh)
    k_mean = jnp.mean(k_blk.astype(jnp.float32), axis=3).astype(k.dtype)

    gate = jnp.einsum('bhsd,bhnd->bhsn', q, k_mean).astype(jnp.float32)
    q_block = jnp.arange(Sp) // BLK
    past = jnp.arange(nb)[None, :] < q_block[:, None]
    gate = jnp.where(past[None, None], gate, -jnp.inf)
    kk = min(MOBA_TOPK, nb)
    sel_score, sel_idx = lax.top_k(gate, kk)
    sel_valid = jnp.isfinite(sel_score)

    nc = Sp // QC
    q_c = q.reshape(B, H, nc, QC, dh).transpose(2, 0, 1, 3, 4)
    idx_c = sel_idx.reshape(B, H, nc, QC, kk).transpose(2, 0, 1, 3, 4)
    val_c = sel_valid.reshape(B, H, nc, QC, kk).transpose(2, 0, 1, 3, 4)
    b_ix = jnp.arange(B)[:, None, None, None]
    h_ix = jnp.arange(H)[None, :, None, None]
    key_off = jnp.arange(BLK)

    def one_chunk(args):
        c, qc, idx, valid = args
        kg = k_blk[b_ix, h_ix, idx]
        vg = v_blk[b_ix, h_ix, idx]
        s_past = jnp.einsum('bhqd,bhqnkd->bhqnk', qc, kg).astype(jnp.float32)
        s_past = jnp.where(valid[..., None], s_past, -jnp.inf).reshape(B, H, QC, kk * BLK)
        start = c * QC
        blk = start // BLK
        k_own = lax.dynamic_index_in_dim(k_blk, blk, axis=2, keepdims=False)
        v_own = lax.dynamic_index_in_dim(v_blk, blk, axis=2, keepdims=False)
        s_own = jnp.einsum('bhqd,bhkd->bhqk', qc, k_own).astype(jnp.float32)
        q_off = start % BLK + jnp.arange(QC)
        causal = key_off[None, :] <= q_off[:, None]
        s_own = jnp.where(causal[None, None], s_own, -jnp.inf)
        p = jax.nn.softmax(jnp.concatenate([s_past, s_own], axis=-1), axis=-1).astype(v.dtype)
        p_past = p[..., :kk * BLK].reshape(B, H, QC, kk, BLK)
        p_own = p[..., kk * BLK:]
        return (jnp.einsum('bhqnk,bhqnkd->bhqd', p_past, vg)
                + jnp.einsum('bhqk,bhkd->bhqd', p_own, v_own))

    out = lax.map(one_chunk, (jnp.arange(nc, dtype=jnp.int32), q_c, idx_c, val_c))
    out = out.transpose(1, 0, 3, 2, 4).reshape(B, Sp, H * dh)[:, :S]
    return out @ w_o

def dilated_group(q, k, v, window, dilation):
    B, S, Hg, dh = q.shape
    span = window // dilation
    WB = DIL_BLOCK
    assert span <= WB
    L = S // dilation
    Lp = -(-L // WB) * WB
    nblk = Lp // WB

    def to_blocks(t):
        t = t.reshape(B, L, dilation, Hg, dh).transpose(0, 2, 1, 3, 4)
        t = jnp.pad(t, ((0, 0), (0, 0), (0, Lp - L), (0, 0), (0, 0)))
        return t.reshape(B, dilation, nblk, WB, Hg, dh)

    def with_prev(t):
        prev = jnp.pad(t, ((0, 0), (0, 0), (1, 0), (0, 0), (0, 0), (0, 0)))[:, :, :-1]
        return jnp.concatenate([prev, t], axis=3)

    qb = to_blocks(q)
    kw = with_prev(to_blocks(k))
    vw = with_prev(to_blocks(v))
    s = jnp.einsum('brnqhd,brnkhd->brnhqk', qb, kw).astype(jnp.float32)
    qi = jnp.arange(nblk)[:, None, None] * WB + jnp.arange(WB)[None, :, None]
    ki = jnp.arange(nblk)[:, None, None] * WB - WB + jnp.arange(2 * WB)[None, None, :]
    dist = qi - ki
    mask = (dist >= 0) & (dist <= span) & (ki >= 0)
    s = jnp.where(mask[None, None, :, None], s, -jnp.inf)
    lse = jax.nn.logsumexp(s, axis=-1)
    p = jnp.exp(s - lse[..., None]).astype(v.dtype)
    o = jnp.einsum('brnhqk,brnkhd->brnqhd', p, vw)
    o = o.reshape(B, dilation, Lp, Hg, dh)[:, :, :L].transpose(0, 2, 1, 3, 4).reshape(B, S, Hg, dh)
    lse = lse.transpose(0, 1, 2, 4, 3).reshape(B, dilation, Lp, Hg)[:, :, :L]
    lse = lse.transpose(0, 2, 1, 3).reshape(B, S, Hg)
    return o, lse

def dilated_attention(x, w_qkv, w_o, cos, sin):
    B, S, _ = x.shape
    G, Hg, dh = len(DIL_GROUPS), DIL_HEADS_PER_GROUP, HEAD_DIM
    qkv = (x @ w_qkv).reshape(B, S, 3, DIL_HEADS, dh)
    q = apply_rotary(qkv[:, :, 0], cos, sin) * (dh ** -0.5)
    k = apply_rotary(qkv[:, :, 1], cos, sin)
    v = qkv[:, :, 2]
    outs, lses = [], []
    for g, (window, dilation) in enumerate(DIL_GROUPS):
        hs = slice(g * Hg, (g + 1) * Hg)
        o_g, lse_g = dilated_group(q[:, :, hs], k[:, :, hs], v[:, :, hs], window, dilation)
        outs.append(o_g)
        lses.append(lse_g)
    alpha = jax.nn.softmax(jnp.stack(lses, axis=0), axis=0).astype(x.dtype)
    o = jnp.stack(outs, axis=0) * alpha[..., None]
    o = o.transpose(1, 2, 0, 3, 4).reshape(B, S, G * Hg * dh)
    return o @ w_o

def sq_relu_mlp(x, w_in, w_out):
    return jnp.square(jax.nn.relu(x @ w_in)) @ w_out

def second_inputs(seed: int = 0) -> dict:
    key = jax.random.key(seed)
    ks = jax.random.split(key, 12)
    f32 = jnp.float32
    moba_w = MOBA_HEADS * HEAD_DIM
    dil_w = DIL_HEADS * HEAD_DIM
    x = jax.random.normal(ks[0], (BATCH, SEQ, D_MODEL), f32)
    moba_w_qkv = jax.random.normal(ks[1], (N_LAYERS_A, D_MODEL, 3 * moba_w), f32) * D_MODEL ** -0.5
    moba_w_o = jax.random.normal(ks[2], (N_LAYERS_A, moba_w, D_MODEL), f32) * (moba_w ** -0.5 * DEEPNORM_BETA)
    dil_w_qkv = jax.random.normal(ks[3], (N_LAYERS_B, D_MODEL, 3 * dil_w), f32) * D_MODEL ** -0.5
    dil_w_o = jax.random.normal(ks[4], (N_LAYERS_B, dil_w, D_MODEL), f32) * (dil_w ** -0.5 * DEEPNORM_BETA)
    mlp_w_in = jax.random.normal(ks[5], (DEPTH, D_MODEL, D_FF), f32) * D_MODEL ** -0.5
    mlp_w_out = jax.random.normal(ks[6], (DEPTH, D_FF, D_MODEL), f32) * (D_FF ** -0.5 * DEEPNORM_BETA)
    ln_mix_g = 1.0 + 0.02 * jax.random.normal(ks[7], (DEPTH, D_MODEL), f32)
    ln_mix_b = 0.02 * jax.random.normal(ks[8], (DEPTH, D_MODEL), f32)
    ln_mlp_g = 1.0 + 0.02 * jax.random.normal(ks[9], (DEPTH, D_MODEL), f32)
    ln_mlp_b = 0.02 * jax.random.normal(ks[10], (DEPTH, D_MODEL), f32)
    return {"x": x, "moba_w_qkv": moba_w_qkv, "moba_w_o": moba_w_o,
            "dil_w_qkv": dil_w_qkv, "dil_w_o": dil_w_o,
            "mlp_w_in": mlp_w_in, "mlp_w_out": mlp_w_out,
            "ln_mix_g": ln_mix_g, "ln_mix_b": ln_mix_b,
            "ln_mlp_g": ln_mlp_g, "ln_mlp_b": ln_mlp_b}

def second_block(x, moba_w_qkv, moba_w_o, dil_w_qkv, dil_w_o, mlp_w_in, mlp_w_out,
              ln_mix_g, ln_mix_b, ln_mlp_g, ln_mlp_b):
    S = x.shape[1]
    cos, sin = rotary_tables(S, x.dtype)
    h = x
    for i in range(DEPTH):
        j = i // N_MIXERS
        if i % N_MIXERS == 0:
            mix = moba_attention(h, moba_w_qkv[j], moba_w_o[j], cos, sin)
        else:
            mix = dilated_attention(h, dil_w_qkv[j], dil_w_o[j], cos, sin)
        h = layer_norm(DEEPNORM_ALPHA * h + mix, ln_mix_g[i], ln_mix_b[i])
        h = layer_norm(DEEPNORM_ALPHA * h + sq_relu_mlp(h, mlp_w_in[i], mlp_w_out[i]),
                       ln_mlp_g[i], ln_mlp_b[i])
    return h


def setup_inputs(seed=0):
    out = dict(first_inputs(seed))
    for name, value in second_inputs(seed + 1).items():
        if name != "x":
            out[name + "_2"] = value
    return out


def reference(
    x, c, positions, ada_w, ada_b, norm1_g, w_in, b_in, rel_bias, w_branch, w_out, norm2_g,
    w_ffn_in, w_ffn_out, final_g, moba_w_qkv_2, moba_w_o_2, dil_w_qkv_2, dil_w_o_2, mlp_w_in_2,
    mlp_w_out_2, ln_mix_g_2, ln_mix_b_2, ln_mlp_g_2, ln_mlp_b_2,
):
    x = first_block(
        x, c, positions, ada_w, ada_b, norm1_g, w_in, b_in, rel_bias, w_branch, w_out, norm2_g,
        w_ffn_in, w_ffn_out, final_g,
    )
    return second_block(
        x, moba_w_qkv_2, moba_w_o_2, dil_w_qkv_2, dil_w_o_2, mlp_w_in_2, mlp_w_out_2,
        ln_mix_g_2, ln_mix_b_2, ln_mlp_g_2, ln_mlp_b_2,
    )


_drawn_inputs = setup_inputs


def setup_inputs(seed=0):
    import zlib

    import numpy as np

    out = dict(_drawn_inputs(seed))
    spreads = {}
    factors = {'ada_b': 3.32, 'norm1_g': 3.155}
    for name, (base, spread) in spreads.items():
        noise = np.random.default_rng([zlib.crc32(name.encode()), seed]).standard_normal(out[name].shape)
        drawn = base * np.exp(spread * noise) if base else spread * noise
        out[name] = __import__('jax').numpy.asarray(drawn.astype(out[name].dtype))
    for name, factor in factors.items():
        out[name] = (out[name] * factor).astype(out[name].dtype)
    return out
```

```python
from contextlib import ExitStack

import numpy as np

import concourse.bass as bass
from concourse import mybir

F32 = mybir.dt.float32
F32R = mybir.dt.float32r
I32 = mybir.dt.int32
ALU = mybir.AluOpType
ACT = mybir.ActivationFunctionType
AX_X = mybir.AxisListType.X

P = 128
S = 256
NT = S // P
D = 1024
KT = D // P
CW = 512
DEPTH = 2
DH = 64
CHUNK = 64
HA, HB, HC, HI = 6, 5, 5, 8
FFN = 2816
DFF = 4096
REL = 128
MOBA_H, DIL_H = 16, 12
DIL = ((128, 1), (512, 4), (2048, 16))
TOPK = S // 4
ALPHA = (2.0 * DEPTH) ** 0.25
RMS_EPS, LN_EPS = 1e-6, 1e-5
SCALE = DH ** -0.5
NEG = -1e30
IDX_OUT = -1e38
PICKED = -3e38

QA, KA, VA = 0, HA * DH, 2 * HA * DH
QI = 3 * HA * DH
KI = QI + HI * DH
WI = KI + DH
QB = WI + HI
KB, VB = QB + HB * DH, QB + 2 * HB * DH
QC = QB + 3 * HB * DH
KC, VC = QC + HC * DH, QC + 2 * HC * DH
FC = QC + 3 * HC * DH
GATE = FC + HC
PROJ_W = GATE + 1
IN_W = GATE + 3 * D
N_PROJ = -(-PROJ_W // CW)
N_GATE = 3 * D // CW

NR = 5
NH = 4
NV = 5
UNIT_K = 2


def constants():
    p = np.arange(P)[:, None]
    k = np.arange(S)[None, :]
    d = P + p - k
    parts = [("ident", np.eye(P)), ("ones", np.ones((P, P)))]
    parts += [("causal", np.where(d >= 0, 0.0, NEG))]
    parts += [("band", np.where(k // CHUNK <= (P + p) // CHUNK, 0.0, NEG))]
    for t in range(NT):
        parts.append((f"tri{t}", np.where(t * P + p <= k, 1 / SCALE, 0.0)))
    rot = DH // 4
    inv = np.float32(500000.0) ** (-np.arange(0, rot, 2, dtype=np.float32) / np.float32(rot))
    parts.append(("inv", np.tile(inv.astype(np.float32)[None], (P, 1))))
    inv2 = (1.0 / (np.float32(10000.0) ** (np.arange(0, DH, 2, dtype=np.float32) / np.float32(DH)))).astype(np.float32)
    for t in range(NT):
        ang = ((t * P + p).astype(np.float32) * inv2[None]).astype(np.float32).astype(np.float64)
        parts.append((f"cc{t}", np.concatenate([np.cos(ang), np.cos(ang)], 1)))
        parts.append((f"ss{t}", np.concatenate([-np.sin(ang), np.sin(ang)], 1)))
    parts.append(("eps", np.tile(np.array([[RMS_EPS, LN_EPS]]), (P, 1))))
    for g, (window, dil) in enumerate(DIL):
        parts.append((f"dil{g}", np.where((d >= 0) & (d <= window) & (d % dil == 0), 0.0, NEG)))
    at, cols = {}, 0
    for name, a in parts:
        at[name] = (cols, cols + a.shape[1])
        cols += a.shape[1]
    return np.concatenate([a for _, a in parts], 1).astype(np.float32), at


class Signal:

    def __init__(self, sem, name, book):
        self.sem, self.name, self.known, self.new = sem, name, book[0], book[1]
        self.count = 0

    def mark(self, event):
        self.count += 1
        self.new[self.name, event] = self.count
        return 1

    def at(self, event):
        return self.known[self.name, event] if self.known else 1


def plan():
    chunks, stream = [], []
    count = {"w": 0, "ada": 0, "vec": 0}
    pair = [0]

    def chunk(key, src, row0, ktiles, col0, ncols, steps=None):
        c = dict(key=key, kind="gemm", pair=pair[0] % 2, ncols=ncols, units=[])
        pair[0] += 1
        for k0 in range(0, ktiles, UNIT_K):
            n = min(UNIT_K, ktiles - k0)
            u = dict(kind="w", index=count["w"], n=n, ncols=ncols, src=(src, row0 + k0 * P, n, col0, ncols))
            u["tiles"] = [[(k0 + i, i)] for i in range(n)] if steps is None else steps[k0 // UNIT_K]
            count["w"] += 1
            c["units"].append(u)
        chunks.append(c)
        return c

    def vec(name, src, col0, ncols=CW):
        v = dict(kind="vec", index=count["vec"], name=name, src=(src, col0, ncols), ncols=ncols)
        count["vec"] += 1
        return v

    def ada(l, c):
        units = []
        for i in range(KT // UNIT_K):
            units.append(dict(kind="ada", index=count["ada"], l=l, c=c, i=i))
            count["ada"] += 1
        ch = dict(key=("ada", l, c), kind="ada", pair=pair[0] % 2, units=units)
        pair[0] += 1
        vs = [vec(("ada_b", l, c), ("ada_b", l), c * CW)]
        if c in (2, 3):
            vs.append(vec(("norm1_g", l, c - 2), ("norm1_g", l), (c - 2) * CW))
        if c in (8, 9):
            vs.append(vec(("norm2_g", l, c - 8), ("norm2_g", l), (c - 8) * CW))
        return ch, vs, units

    def put_ada(l, c):
        ch, vs, units = ada(l, c)
        chunks.append(ch)
        stream.extend(vs)
        stream.extend(units)

    def put(vs, *args, **kw):
        c = chunk(*args, **kw)
        stream.extend(vs)
        stream.extend(c["units"])

    for c in range(4):
        put_ada(0, c)
    for l in range(DEPTH):
        for j in range(N_PROJ):
            n = min(CW, PROJ_W - j * CW)
            put([vec(("b_in", l, j), ("b_in", l), j * CW, n)], ("proj", l, j), ("w_in", l), 0, KT, j * CW, n)
            if j % 2 == 1:
                put_ada(l, 4 + j // 2)
        for j in range(N_GATE):
            put([vec(("b_gate", l, j), ("b_in", l), GATE + j * CW)], ("gate", l, j), ("w_in", l), 0, KT, GATE + j * CW, CW)
            if j % 2 == 0 or j == 3:
                put_ada(l, {0: 8, 2: 9, 3: 10, 4: 11}[j])
        steps = {"A": [[[(0, 0)], [(1, 1)]], [[(2, 0)], []], None, None],
                 "B": [None, [[], [(3, 1)]], [[(4, 0)], [(5, 1)]], None],
                 "C": [None, None, [[], [(8, 1)]], [[(6, 0)], [(7, 1)]]]}
        for cc in range(D // CW):
            for b, k0, kn, st in (("A", 0, 3, [[[(0, 0)], [(1, 1)]], [[(2, 0)]]]),
                                  ("B", 3, 3, [[[(3, 0)], [(4, 1)]], [[(5, 0)]]]),
                                  ("C", 5, 3, [[[(8, 0)], [(6, 1)]], [[(7, 0)]]])):
                put([], ("branch", l, cc, b), ("w_branch", l), k0 * P, kn, cc * CW, CW, steps=st)
        for cc in range(D // CW):
            put([], ("wout", l, cc), ("w_out", l), 0, KT, cc * CW, CW)
        for j in range(-(-FFN // CW)):
            n = min(CW, FFN - j * CW)
            put([], ("ffg", l, j), ("w_ffn_in", l), 0, KT, j * CW, n)
            put([], ("ffu", l, j), ("w_ffn_in", l), 0, KT, FFN + j * CW, n)
            if l + 1 < DEPTH and 1 <= j <= 4:
                put_ada(l + 1, j - 1)
        for cc in range(D // CW):
            put([], ("ffo", l, cc), ("w_ffn_out", l), 0, FFN // P, cc * CW, CW)
    stream.extend(vec(("final_g", h), ("final_g",), h * CW) for h in range(2))
    for i in range(2):
        heads = (MOBA_H, DIL_H)[i]
        w = 3 * heads * DH
        for j in range(-(-w // CW)):
            n = min(CW, w - j * CW)
            put([], ("qkv", i, j), (("moba_w_qkv", "dil_w_qkv")[i],), 0, KT, j * CW, n)
        for cc in range(2):
            put([], ("wo", i, cc), (("moba_w_o", "dil_w_o")[i],), 0, heads * DH // P, cc * CW, CW)
        for v in ("ln_mix_g", "ln_mix_b"):
            stream.extend(vec((v, i, h), (v, i), h * CW) for h in range(2))
        for j in range(DFF // CW):
            put([], ("mi", i, j), ("mlp_w_in", i), 0, KT, j * CW, CW)
        for cc in range(2):
            put([], ("mo", i, cc), ("mlp_w_out", i), 0, DFF // P, cc * CW, CW)
        for v in ("ln_mlp_g", "ln_mlp_b"):
            stream.extend(vec((v, i, h), (v, i), h * CW) for h in range(2))
    last = {}
    for c in chunks:
        c["before"] = last.get(c["pair"])
        last[c["pair"]] = c["key"]
    return chunks, stream


def heads_one():
    out = [dict(kind="I", h=h, q=QI + h * DH, k=KI) for h in range(HI)]
    out += [dict(kind="B", h=h, q=QB + h * DH, k=KB + h * DH, v=VB + h * DH, o=(HA + h) * DH) for h in range(HB)]
    out += [dict(kind="C", h=h, q=QC + h * DH, k=KC + h * DH, v=VC + h * DH, o=(HA + HB + h) * DH) for h in range(HC)]
    out += [dict(kind="A", h=h, q=QA + h * DH, k=KA + h * DH, v=VA + h * DH, o=h * DH) for h in range(HA)]
    return out


def heads_two(i):
    n = (MOBA_H, DIL_H)[i]
    kind = "MD"[i]
    return [dict(kind=kind, h=h, q=h * DH, k=(n + h) * DH, v=(2 * n + h) * DH, o=h * DH) for h in range(n)]


def build(nc, dram, out, cat, book):
    with ExitStack() as ctx:
        program(nc, ctx, dram, out, cat, book)


def program(nc, ctx, dram, out, cat, book):
    chunks, stream = plan()
    by_key = {c["key"]: c for c in chunks}
    vec_of = {i["name"]: i for i in stream if i["kind"] == "vec"}
    ring = [i for i in stream if i["kind"] != "vec"]
    for n, i in enumerate(ring):
        i["slot"], i["turn"] = n % NR, n // NR
        i["evicts"] = ring[n - NR] if n >= NR else None

    plan_at = [-(-nc.sbuf_base // 64) * 64]
    top = []

    def place(name, shape, dt=F32, at=None):
        size = int(np.prod(shape[1:])) * 4
        offset = plan_at[0] if at is None else at
        if at is None:
            plan_at[0] += -(-size // 32) * 32
        top.append(offset + size)
        t = nc.alloc_sbuf_tensor_at(name, list(shape), dt, offset=offset)
        return t, offset

    X, _ = place("x_rows", [P, NT, D])
    O, _ = place("o_rows", [P, NT, D])
    HT, _ = place("turned", [P, KT + 1, 2, S], F32R)
    RAW, _ = place("raw_units", [P, NR, UNIT_K, CW])
    HI_, _ = place("hi_units", [P, NH, UNIT_K, CW], F32R)
    LO, _ = place("lo_units", [P, NH, UNIT_K, CW], F32R)
    VEC, _ = place("row_vectors", [P, NV, CW])
    PROJ, union = place("proj_rows", [P, NT, PROJ_W])
    GATES, _ = place("gate_rows", [P, NT, 3 * D])
    MOD, _ = place("mod_rows", [P, 6 * D])
    AT, _ = place("turned_wide", [P, DFF // P, 2, S], F32R, at=union)
    TG, _ = place("ffn_tanh", [P, 2, NT, CW], at=union + FFN // P * 2 * S * 4)
    RT, _ = place("mlp_relu", [P, 2, NT, CW], at=union + DFF // P * 2 * S * 4)
    QKV, _ = place("qkv_rows", [P, NT, 3 * D], at=union)
    RTMP, _ = place("rotary_tmp", [P, 2, CW], at=union + DFF // P * 2 * S * 4)
    LNT, _ = place("norm_tmp", [P, D], at=union)
    SM, _ = place("scores", [P, 2, 3 * P])
    PT, _ = place("probs_turned", [P, 2, 3 * P])
    QKT, _ = place("qk_turned", [DH, 2, 2 * S])
    KIT, _ = place("idx_keys_turned", [DH, S])
    IDX, _ = place("idx_scores", [P, 3 * P])
    MB, _ = place("bias_masks", [P, HB, S])
    CM, cm_at = place("forget_masks", [P, HC, 3 * P])
    LB, _ = place("logf_wide", [P, NT, P])
    n_const = cat["eps"][1]
    CON, _ = place("constants", [P, n_const])
    DILM, _ = place("dilated_masks", [P, 3, S], at=cm_at)
    SMALL, _ = place("small", [P, 440])
    POS, _ = place("positions_int", [P, NT], I32)
    RB, _ = place("rel_rows", [DEPTH * HB, 2 * REL + 1], at=cm_at)
    RE, _ = place("rel_extended", [DEPTH * HB, 3 * P], at=cm_at + 2048)
    assert max(top) <= nc.sbuf_usable_end, (max(top), nc.sbuf_usable_end)
    scratch = nc.dram_tensor("rel_scratch", [DEPTH * HB, 3 * P], F32)

    def con(name):
        a, b = cat[name]
        return CON[:, a:b]

    used = [0]

    def small(n):
        used[0] += n
        assert used[0] <= 440
        return SMALL[:, used[0] - n:used[0]]

    COND, CT = small(KT), small(KT)
    POSF, ANG, KR, RED, COS, SIN = (small(NT), *(small(NT * 8) for _ in range(5)))
    MAX8 = small(16)
    ZN, ZA, ZE, ZU, ZL, ZD, LF, F8 = (small(NT * HC) for _ in range(8))
    MX, NM, RS, RR = (small(48) for _ in range(4))
    STAT = small(24)
    MV, RSTD, NMR = small(4), small(2), small(2)

    BANK = [ctx.enter_context(nc.psum_tensor(f"bank{i}", [P, CW], F32)) for i in range(8)]
    SB_ = (4, 5)
    TQ, TP = 6, 7

    def sem(name):
        return ctx.enter_context(nc.semaphore(name))

    def signal(name):
        return Signal(sem(name), name, book)

    raw_in = [sem(f"raw_in{i}") for i in range(NR)]
    vec_in = [sem(f"vec_in{i}") for i in range(NV)]
    x_in, c_in, pos_in, const_in, rel_in = (sem(n) for n in ("x_in", "c_in", "pos_in", "const_in", "rel_in"))
    scratch_in, dil_in, out_in = sem("scratch_in"), sem("dil_in"), sem("out_in")
    bias_in = [sem(f"bias_in{h}") for h in range(HB)]
    hi_ready = signal("hi_ready")
    lo_ready = signal("lo_ready")
    unit_used = signal("unit_used")
    ada_used = signal("ada_used")
    vec_used = signal("vec_used")
    product = signal("product")
    drained = signal("drained")
    turned = signal("turned")
    turned_hi = signal("turned_hi")
    turned_lo = signal("turned_lo")
    rows = signal("rows")
    act_side = signal("act_side")
    qk_in_psum = signal("qk_in_psum")
    qk_turned = signal("qk_turned")
    scored = signal("scored")
    masked = signal("masked")
    exped = signal("exped")
    p_in_psum = signal("p_in_psum")
    p_turned = signal("p_turned")
    headed = signal("headed")
    head_out = signal("head_out")
    forget = signal("forget")
    chain = signal("chain")
    act_chain = signal("act_chain")

    def tile_rows(src):
        name, *ix = src
        a = dram[name]
        return a[ix[0]] if ix else (a[0] if len(a.shape) == 3 else a)

    def raw_ready(e, u):
        e.wait_ge(raw_in[u["slot"]], 16 * (u["turn"] + 1))

    def vec_ready(e, name):
        v = vec_of[name]
        e.wait_ge(vec_in[v["index"] % NV], 16 * (v["index"] // NV + 1))
        return VEC[:, v["index"] % NV, 0:v["ncols"]]

    vectors = [i for i in stream if i["kind"] == "vec"]

    def freed_by(vec):
        what, *ix = vec["name"]
        if what in ("ada_b", "b_in", "b_gate"):
            return drained, ({"ada_b": "ada", "b_in": "proj", "b_gate": "gate"}[what], *ix)
        return vec_used, vec["name"]

    block = ctx.enter_context(nc.Block())

    @block.sync
    def _(sp):
        sp.dma_start(COND, dram["c"].rearrange("b (p k) -> (b p) k", p=P)).then_inc(c_in, 16)
        sp.dma_start(CON[:, :], dram["constants"][:, 0:n_const]).then_inc(const_in, 16)
        sp.dma_start(RB[:, :], dram["rel_bias"].rearrange("l h r -> (l h) r")).then_inc(rel_in, 16)
        sp.dma_start(POS[:, :], dram["positions"].rearrange("b (t p) -> (b p) t", p=P),
                     allow_slow_non_contiguous=True).then_inc(pos_in, 16)
        first_w = True
        for item in stream:
            if item["kind"] == "vec":
                n = item["index"]
                if n >= NV:
                    signal_, event = freed_by(vectors[n - NV])
                    sp.wait_ge(signal_.sem, signal_.at(event))
                (name, *ix), col0, ncols = item["src"]
                a = dram[name]
                row = (a[ix[0]:ix[0] + 1, :] if ix else a.rearrange("(a n) -> a n", a=1))[:, col0:col0 + ncols]
                sp.dma_start(VEC[:, n % NV, 0:ncols], row.to_broadcast([P, ncols])).then_inc(vec_in[n % NV], 16)
                continue
            old = item["evicts"]
            if old is not None and old["kind"] == "w":
                sp.wait_ge(lo_ready.sem, lo_ready.at(old["index"]))
            elif old is not None:
                sp.wait_ge(ada_used.sem, ada_used.at(old["index"]))
            if item["kind"] == "ada":
                l, c, i = item["l"], item["c"], item["i"]
                src = dram["ada_w"][l].rearrange("(p k) n -> p k n", p=P)[:, i * UNIT_K:(i + 1) * UNIT_K, c * CW:(c + 1) * CW]
                sp.dma_start(RAW[:, item["slot"], :, :], src).then_inc(raw_in[item["slot"]], 16)
            else:
                src, row0, n, col0, ncols = item["src"]
                a = tile_rows(src)[row0:row0 + n * P, col0:col0 + ncols].rearrange("(k p) n -> p k n", p=P)
                if first_w:
                    first_w = False
                    sp.dma_start(X[:, :, :], dram["x"][0].rearrange("(t p) d -> p t d", p=P)).then_inc(x_in, 16)
                    sp.wait_ge(rows.sem, rows.at("rel"))
                    sp.dma_start(scratch[:, :], RE[:, :]).then_inc(scratch_in, 16)
                    sp.wait_ge(scratch_in, 16)
                key = item["index"]
                if key in bias_at:
                    l = bias_at[key]
                    for h in range(HB):
                        if l:
                            sp.wait_ge(masked.sem, masked.at((l - 1, HI + HB - 1)))
                        rel = bass.AP(scratch, (l * HB + h) * 3 * P, [[1, P], [1, S]])
                        sp.dma_start(MB[:, h, :], rel).then_inc(bias_in[h], 16)
                if key == dil_at:
                    sp.wait_ge(masked.sem, masked.at((DEPTH - 1, HI + HB + HC - 1)))
                    a0, b0 = cat["dil0"][0], cat["dil2"][1]
                    sp.dma_start(DILM[:, :, :], dram["constants"][:, a0:b0].rearrange("p (g k) -> p g k", g=3)).then_inc(dil_in, 16)
                sp.dma_start(RAW[:, item["slot"], 0:n, 0:ncols], a).then_inc(raw_in[item["slot"]], 16)
        for t in range(NT):
            sp.wait_ge(vec_used.sem, vec_used.at(("ln_mlp_b", 1, 1)))
            sp.dma_start(out[0, t * P:(t + 1) * P, :], X[:, t, :]).then_inc(out_in, 16)
        sp.wait_ge(out_in, 16 * NT)

    @block.gpsimd
    def _(pool):
        for u in (i for i in ring if i["kind"] == "w"):
            s, n, w = u["index"] % NH, u["n"], u["ncols"]
            pool.wait_ge(hi_ready.sem, hi_ready.at(u["index"]))
            pool.tensor_tensor(LO[:, s, 0:n, 0:w], RAW[:, u["slot"], 0:n, 0:w], HI_[:, s, 0:n, 0:w].bitcast(F32),
                               ALU.subtract).then_inc(lo_ready.sem, lo_ready.mark(u["index"]))

    @block.tensor
    def _(pe):
        todo = [c for c in chunks]

        def pair_free(c):
            if c["before"][0] == "mi":
                pe.wait_ge(act_side.sem, act_side.at(("relu", *c["before"][1:])))
            else:
                pe.wait_ge(drained.sem, drained.at(c["before"]))

        def unit(c, i, A):
            u = c["units"][i]
            if i == 0 and c["before"] is not None:
                pair_free(c)
            pe.wait_ge(lo_ready.sem, lo_ready.at(u["index"]))
            s, w = u["index"] % NH, u["ncols"]
            nt = [(a, b) for tile in u["tiles"] for a, b in tile]
            for t in range(NT):
                for m, (a, b) in enumerate(nt):
                    xs = A[:, a, :, t * P:(t + 1) * P]
                    passes = ((0, HI_), (0, LO), (1, HI_))
                    for q, (part, W) in enumerate(passes):
                        ins = pe.matmul(BANK[2 * c["pair"] + t][:, 0:w], xs[:, part, :], W[:, s, b, 0:w],
                                        start=(i == 0 and m == 0 and q == 0),
                                        stop=(i == len(c["units"]) - 1 and m == len(nt) - 1 and q == 2))
            ins.then_inc(unit_used.sem, unit_used.mark(u["index"]))

        def ada_sum(c):
            _, l, n = c["key"]
            if c["before"] is not None:
                pair_free(c)
            pe.wait_ge(ada_used.sem, ada_used.at(c["units"][-1]["index"]))
            pe.matmul(BANK[2 * c["pair"]][:, :], con("ones"), MOD[:, n * CW:(n + 1) * CW],
                      start=True, stop=True).then_inc(product.sem, product.mark(c["key"]))

        def gemms(A, n=None, until=None):
            while todo and (todo[0]["key"][0] in until or todo[0]["kind"] == "ada"):
                c = todo.pop(0)
                if c["kind"] == "ada":
                    ada_sum(c)
                else:
                    for i in range(len(c["units"])):
                        unit(c, i, A)

        def turn(tag, src, ntiles, ready):
            for g in range(-(-ntiles // 2)):
                n = min(2, ntiles - 2 * g)
                if g >= 2:
                    pe.wait_ge(turned_lo.sem, turned_lo.at((tag, g - 2)))
                for t in range(NT):
                    if g == 0:
                        signal_, event = ready(t)
                        pe.wait_ge(signal_.sem, signal_.at(event))
                    for j in range(n):
                        ins = pe.transpose(BANK[(TQ, TP)[g % 2]][:, (j * NT + t) * P:(j * NT + t + 1) * P],
                                           src[:, t, (2 * g + j) * P:(2 * g + j + 1) * P], con("ident"))
                ins.then_inc(turned.sem, turned.mark((tag, g)))

        def wait_turned(tag, ntiles):
            pe.wait_ge(turned_lo.sem, turned_lo.at((tag, -(-ntiles // 2) - 1)))

        def attention(tag, heads, src, weave, pt_banks):
            lag = 2 if len(pt_banks) == 1 else 3
            for k in range(len(heads) + lag):
                if 0 <= k - 1 < len(heads):
                    h, hd = k - 1, heads[k - 1]
                    pe.wait_ge(qk_turned.sem, qk_turned.at((tag, h)))
                    if h >= 2:
                        prev = heads[h - 2]
                        if prev["kind"] == "I":
                            pe.wait_ge(exped.sem, exped.at((tag, h - 2)))
                        else:
                            pe.wait_ge(masked.sem, masked.at((tag, h - 2)))
                    bank = BANK[SB_[h % 2]]
                    q = QKT[:, h % 2, 0:S]
                    kk = KIT[:, :] if hd["kind"] == "I" else QKT[:, h % 2, S:2 * S]
                    pe.matmul(bank[:, 0:S], q[:, P:S], kk, start=True, stop=True)
                    pe.matmul(bank[:, S:S + P], q[:, 0:P], kk[:, 0:P], start=True, stop=True)\
                        .then_inc(scored.sem, scored.mark((tag, h)))
                if k < len(heads):
                    hd = heads[k]
                    if k >= 1:
                        pe.wait_ge(qk_turned.sem, qk_turned.at((tag, k - 1)))
                    with_k = hd["kind"] != "I" or hd["h"] == 0
                    for col, at in ((hd["q"], 0), (hd["k"], S))[:2 if with_k else 1]:
                        for t in range(NT):
                            ins = pe.transpose(BANK[TQ][0:DH, at + t * P:at + (t + 1) * P], src[:, t, col:col + DH], con("ident"))
                    ins.then_inc(qk_in_psum.sem, qk_in_psum.mark((tag, k)))
                h = k - 2
                if 0 <= h < len(heads) and heads[h]["kind"] != "I":
                    pe.wait_ge(exped.sem, exped.at((tag, h)))
                    prior = h - len(pt_banks)
                    if prior >= 0 and heads[prior]["kind"] != "I":
                        pe.wait_ge(head_out.sem, head_out.at((tag, prior)))
                    bank = BANK[pt_banks[h % len(pt_banks)]]
                    for at, cols in ((0, slice(S, S + P)), (P, slice(0, P)), (2 * P, slice(P, S))):
                        ins = pe.transpose(bank[:, at:at + P], SM[:, h % 2, cols], con("ident"))
                    ins.then_inc(p_in_psum.sem, p_in_psum.mark((tag, h)))
                weave(k)
                h = k - lag
                if 0 <= h < len(heads) and heads[h]["kind"] != "I":
                    hd = heads[h]
                    bank = BANK[pt_banks[h % len(pt_banks)]]
                    pe.wait_ge(p_turned.sem, p_turned.at((tag, h)))
                    v = hd["v"]
                    pt = PT[:, h % 2, :]
                    pe.matmul(bank[:, 384:448], pt[:, 0:P], src[:, 0, v:v + DH], start=True, stop=True)
                    pe.matmul(bank[:, 448:512], pt[:, P:2 * P], src[:, 0, v:v + DH], start=True, stop=False)
                    pe.matmul(bank[:, 448:512], pt[:, 2 * P:3 * P], src[:, 1, v:v + DH], start=False, stop=True)\
                        .then_inc(headed.sem, headed.mark((tag, h)))

        pe.wait_ge(const_in, 16)
        gemms(None, until=())
        for l in range(DEPTH):
            turn(("n1", l), O, KT, lambda t: (rows, ("h", ("n1", l), t)))
            wait_turned(("n1", l), KT)
            gemms(HT, until=("proj",))
            heads = heads_one()
            gates = [c for c in todo if c["key"][0] == "gate"][:N_GATE]
            pe.wait_ge(drained.sem, drained.at(("proj", l, N_PROJ - 1)))

            def weave(k, l=l):
                if k >= 1 and 2 <= k < 2 + HC + 1:
                    forget_products(l, k - 2)
                if todo[0]["key"][0] == "gate" and todo[0]["key"][1] == l:
                    c = todo[0]
                    unit(c, k % 4, HT)
                    if k % 4 == 3:
                        todo.pop(0)
                        while todo[0]["kind"] == "ada":
                            ada_sum(todo.pop(0))

            def forget_products(l, c):
                if c == 0:
                    pe.wait_ge(rows.sem, rows.at(("logf", l)))
                    lf = LF.rearrange("p (t h) -> p t h", t=NT)
                    pe.matmul(BANK[TP][:, 0:HC], con("tri0")[:, 0:P], lf[:, 0, :], start=True, stop=True)
                    pe.matmul(BANK[TP][:, HC:2 * HC], con("tri0")[:, P:S], lf[:, 0, :], start=True, stop=False)
                    pe.matmul(BANK[TP][:, HC:2 * HC], con("tri1")[:, P:S], lf[:, 1, :], start=False, stop=True)\
                        .then_inc(forget.sem, forget.mark((l, "cols")))
                    return
                pe.wait_ge(rows.sem, rows.at(("logf_wide", l, c - 1)))
                pe.matmul(BANK[TP][:, 0:S], LB[:, 0, :], con("tri0"), start=True, stop=False)
                pe.matmul(BANK[TP][:, 0:S], LB[:, 1, :], con("tri1"), start=False, stop=True)\
                    .then_inc(forget.sem, forget.mark((l, c - 1)))

            attention(l, heads, PROJ, weave, (TP,))
            turn(("o", l), O, KT, lambda t: (head_out, (l, len(heads) - 1)))
            pe.wait_ge(rows.sem, rows.at(("halves", l)))
            gemms(HT, until=("branch",))
            turn(("y", l), O, KT, lambda t: (rows, ("y", l)))
            wait_turned(("y", l), KT)
            gemms(AT, until=("wout",))
            turn(("n2", l), O, KT, lambda t: (rows, ("h", ("n2", l), t)))
            wait_turned(("n2", l), KT)
            n_ff = -(-FFN // CW)
            for j in range(n_ff + 1):
                if j < n_ff:
                    for what in ("ffg", "ffu"):
                        c = todo.pop(0)
                        assert c["key"] == (what, l, j)
                        for i in range(len(c["units"])):
                            unit(c, i, HT)
                        if what == "ffg" and j:
                            turn_ffn(pe, turned, turned_lo, rows, drained, ("a", l), j - 1, min(CW, FFN - (j - 1) * CW) // P, BANK, TQ, TP, O, con)
                    while todo[0]["kind"] == "ada":
                        ada_sum(todo.pop(0))
                else:
                    turn_ffn(pe, turned, turned_lo, rows, drained, ("a", l), j - 1, min(CW, FFN - (j - 1) * CW) // P, BANK, TQ, TP, O, con)
            pe.wait_ge(turned_lo.sem, turned_lo.at((("a", l), n_ff - 1, 1)))
            gemms(AT, until=("ffo",))
        for i in range(2):
            heads = heads_two(i)
            turn(("x", i), X, KT, lambda t: (vec_used, ("final_g", 1) if i == 0 else ("ln_mlp_b", 0, 1)))
            wait_turned(("x", i), KT)
            gemms(HT, until=("qkv",))
            pe.wait_ge(drained.sem, drained.at(("qkv", i, -(-3 * len(heads) * DH // CW) - 1)))
            attention(("two", i), heads, QKV, lambda k: None, (TP, 3))
            nk = len(heads) * DH // P
            turn(("o2", i), O, nk, lambda t: (rows, "weighted") if i else (head_out, (("two", 0), len(heads) - 1)))
            wait_turned(("o2", i), nk)
            gemms(HT, until=("wo",))
            turn(("m", i), X, KT, lambda t: (vec_used, ("ln_mix_b", i, 1)))
            wait_turned(("m", i), KT)
            for j in range(DFF // CW + 1):
                if j < DFF // CW:
                    c = todo.pop(0)
                    for u in range(len(c["units"])):
                        unit(c, u, HT)
                if j:
                    turn_ffn(pe, turned, turned_lo, rows, drained, ("a2", i), j - 1, CW // P, BANK, TQ, TP, O, con)
            pe.wait_ge(turned_lo.sem, turned_lo.at((("a2", i), DFF // CW - 1, 1)))
            gemms(AT, until=("mo",))
        assert not todo

    last_unit = {c["key"]: c["units"][-1]["index"] for c in chunks if c["kind"] == "gemm"}

    def product_ready(e, key):
        c = by_key[key]
        if c["kind"] == "ada":
            e.wait_ge(product.sem, product.at(key))
        else:
            e.wait_ge(unit_used.sem, unit_used.at(last_unit[key]))
        return [BANK[2 * c["pair"] + t] for t in range(NT)]

    @block.scalar
    def _(act):
        w_units = [i for i in ring if i["kind"] == "w"]
        done = [0]

        def prep(upto):
            while done[0] < min(upto, len(w_units)):
                u = w_units[done[0]]
                s, n, w = u["index"] % NH, u["n"], u["ncols"]
                raw_ready(act, u)
                if u["index"] >= NH:
                    act.wait_ge(unit_used.sem, unit_used.at(u["index"] - NH))
                act.activation(HI_[:, s, 0:n, 0:w], RAW[:, u["slot"], 0:n, 0:w], ACT.Copy)\
                    .then_inc(hi_ready.sem, hi_ready.mark(u["index"]))
                done[0] += 1

        def prep_chunk(key, ahead=NH):
            prep(last_unit[key] + 1 + ahead)

        def turn_hi(tag, A, ntiles):
            for g in range(-(-ntiles // 2)):
                n = min(2, ntiles - 2 * g)
                act.wait_ge(turned.sem, turned.at((tag, g)))
                act.activation(A[:, 2 * g:2 * g + n, 0, :], BANK[(TQ, TP)[g % 2]][:, 0:n * S].rearrange("p (k s) -> p k s", k=n),
                               ACT.Copy).then_inc(turned_hi.sem, turned_hi.mark((tag, g)))

        def turn_hi_ffn(tag, j, n):
            for t in range(NT):
                act.wait_ge(turned.sem, turned.at((tag, j, t)))
                act.activation(AT[:, 4 * j:4 * j + n, 0, t * P:(t + 1) * P], BANK[(TQ, TP)[t]][:, 0:n * P].rearrange("p (k s) -> p k s", k=n),
                               ACT.Copy).then_inc(turned_hi.sem, turned_hi.mark((tag, j, t)))

        def rms(tag, ready):
            for t in range(NT):
                ready(t)
                act.activation(O[:, t, :], X[:, t, :], ACT.Square, accum_out=STAT[:, t:t + 1])\
                    .then_inc(act_chain.sem, act_chain.mark(("sq", tag, t)))
            act.wait_ge(act_chain.sem, act_chain.at(("sq", tag, NT - 1)))
            act.activation(RSTD, STAT[:, 0:NT], ACT.Sqrt, scale=1.0 / D, bias=con("eps")[:, 0:1])\
                .then_inc(act_side.sem, act_side.mark(("rms", tag)))

        def attention(tag, heads, weave):
            for k in range(len(heads) + 1):
                weave(k)
                if k < len(heads):
                    hd = heads[k]
                    act.wait_ge(qk_in_psum.sem, qk_in_psum.at((tag, k)))
                    if k >= 2:
                        act.wait_ge(scored.sem, scored.at((tag, k - 2)))
                    if hd["kind"] == "I":
                        if hd["h"] == 0:
                            act.activation(KIT[:, :], BANK[TQ][0:DH, S:2 * S], ACT.Copy)\
                                .then_inc(act_chain.sem, act_chain.mark(("kit", tag)))
                        act.activation(QKT[:, k % 2, 0:S], BANK[TQ][0:DH, 0:S], ACT.Copy)\
                            .then_inc(qk_turned.sem, qk_turned.mark((tag, k)))
                    else:
                        act.activation(QKT[:, k % 2, :], BANK[TQ][0:DH, :], ACT.Copy)\
                            .then_inc(qk_turned.sem, qk_turned.mark((tag, k)))
                h = k - 1
                if h >= 0 and heads[h]["kind"] == "I":
                    act.wait_ge(scored.sem, scored.at((tag, h)))
                    if h >= 2:
                        act.wait_ge(masked.sem, masked.at((tag, h - 2)))
                    act.activation(SM[:, h % 2, :], BANK[SB_[h % 2]][:, 0:3 * P], ACT.Relu)\
                        .then_inc(exped.sem, exped.mark((tag, h)))
                elif h >= 0:
                    act.wait_ge(masked.sem, masked.at((tag, h)))
                    m = 2 * h
                    act.activation(SM[:, h % 2, S:S + P], SM[:, h % 2, S:S + P], ACT.Exp, bias=NM[:, m:m + 1],
                                   accum_out=RS[:, m:m + 1])
                    act.activation(SM[:, h % 2, 0:S], SM[:, h % 2, 0:S], ACT.Exp, bias=NM[:, m + 1:m + 2],
                                   accum_out=RS[:, m + 1:m + 2]).then_inc(exped.sem, exped.mark((tag, h)))

        act.wait_ge(c_in, 16)
        act.activation(CT, COND, ACT.Tanh, scale=0.5).then_inc(act_side.sem, act_side.mark("cond"))
        for what, dst in (("sin", SIN), ("cos", COS)):
            act.wait_ge(rows.sem, rows.at(what))
            act.activation(dst, dst, ACT.Sin).then_inc(act_side.sem, act_side.mark(what))
        prep(NH)
        for l in range(DEPTH):
            rms(("n1", l), lambda t: act.wait_ge(x_in, 16) if l == 0 else act.wait_ge(rows.sem, rows.at(("x", ("end", l - 1), t))))
            turn_hi(("n1", l), HT, KT)
            for j in range(N_PROJ):
                prep_chunk(("proj", l, j))
            act.wait_ge(rows.sem, rows.at(("nabs", l)))
            act.activation(ZE, ZA, ACT.Exp).then_inc(act_side.sem, act_side.mark(("ze", l)))
            act.wait_ge(rows.sem, rows.at(("zu", l)))
            act.activation(ZL, ZU, ACT.Ln).then_inc(act_side.sem, act_side.mark(("zl", l)))
            first = by_key[("gate", l, 0)]["units"][0]["index"]

            def gate_tanh(j, l=l):
                act.wait_ge(drained.sem, drained.at(("gate", l, j)))
                act.activation(GATES[:, :, j * CW:(j + 1) * CW], GATES[:, :, j * CW:(j + 1) * CW], ACT.Tanh, scale=0.5)\
                    .then_inc(act_side.sem, act_side.mark(("gate", l, j)))

            def weave(k, l=l):
                prep(first + min(k + 1, 4 * N_GATE) + 3)
                if k >= 6 and (k - 6) % 4 == 0:
                    gate_tanh((k - 6) // 4)

            attention(l, heads_one(), weave)
            gate_tanh(N_GATE - 1)
            prep_chunk(("gate", l, N_GATE - 1))
            turn_hi(("o", l), HT, KT)
            for cc in range(2):
                for b in "ABC":
                    prep_chunk(("branch", l, cc, b), 2)
            turn_hi(("y", l), AT, KT)
            for cc in range(2):
                prep_chunk(("wout", l, cc))
            rms(("n2", l), lambda t: act.wait_ge(rows.sem, rows.at(("x", ("mid1", l), t))))
            turn_hi(("n2", l), HT, KT)
            n_ff = -(-FFN // CW)
            for j in range(n_ff):
                n = min(CW, FFN - j * CW)
                prep_chunk(("ffg", l, j))
                banks = product_ready(act, ("ffg", l, j))
                for t in range(NT):
                    if j >= 2:
                        act.wait_ge(drained.sem, drained.at(("ffu", l, j - 2)))
                    ins = act.activation(TG[:, j % 2, t, 0:n], banks[t][:, 0:n], ACT.Tanh, scale=0.5)
                ins.then_inc(act_side.sem, act_side.mark(("tg", l, j)))
                if j:
                    turn_hi_ffn(("a", l), j - 1, CW // P)
                prep_chunk(("ffu", l, j))
            turn_hi_ffn(("a", l), n_ff - 1, (FFN - (n_ff - 1) * CW) // P)
            for cc in range(2):
                prep_chunk(("ffo", l, cc))
        rms("final", lambda t: act.wait_ge(rows.sem, rows.at(("x", ("end", DEPTH - 1), t))))

        def root(tag):
            act.wait_ge(rows.sem, rows.at(("var", tag)))
            act.activation(RSTD, MV.rearrange("p (t m) -> p t m", t=NT)[:, :, 1], ACT.Sqrt, bias=con("eps")[:, 1:2])\
                .then_inc(act_side.sem, act_side.mark(("root", tag)))

        for i in range(2):
            heads = heads_two(i)
            turn_hi(("x", i), HT, KT)
            w = 3 * len(heads) * DH
            for j in range(-(-w // CW)):
                prep_chunk(("qkv", i, j))
                n = min(CW, w - j * CW)
                if j * CW >= 2 * len(heads) * DH:
                    pass
            attention(("two", i), heads, lambda k: None)
            if i == 1:
                act.wait_ge(rows.sem, rows.at("group_max"))
                act.activation(NM[:, 0:3 * 4 * NT], MX[:, 0:3 * 4 * NT], ACT.Exp)\
                    .then_inc(act_side.sem, act_side.mark("group_exp"))
            turn_hi(("o2", i), HT, len(heads) * DH // P)
            for cc in range(2):
                prep_chunk(("wo", i, cc))
            root(("mid", i))
            turn_hi(("m", i), HT, KT)
            for j in range(DFF // CW):
                prep_chunk(("mi", i, j))
                banks = product_ready(act, ("mi", i, j))
                if j >= 2:
                    act.wait_ge(rows.sem, rows.at(("a2", i, j - 2)))
                for t in range(NT):
                    ins = act.activation(RT[:, j % 2, t, :], banks[t][:, :], ACT.Relu)
                ins.then_inc(act_side.sem, act_side.mark(("relu", i, j)))
                if j:
                    turn_hi_ffn(("a2", i), j - 1, CW // P)
            turn_hi_ffn(("a2", i), DFF // CW - 1, CW // P)
            for cc in range(2):
                prep_chunk(("mo", i, cc))
            root(("end2", i))

    @block.vector
    def _(dve):
        v = nc.vector
        step = [0]

        def link(ins):
            step[0] += 1
            ins.then_inc(chain.sem, chain.mark(step[0]))
            dve.wait_ge(chain.sem, step[0])

        def tell(ins, signal_, event):
            ins.then_inc(signal_.sem, signal_.mark(event))
            dve.wait_ge(signal_.sem, signal_.at(event))

        def say(ins, event):
            tell(ins, rows, event)

        pos_in_stream = {}
        for n, i in enumerate(ring):
            if i["kind"] == "w":
                pos_in_stream[i["index"]] = n
        ada_units = [(n, i) for n, i in enumerate(ring) if i["kind"] == "ada"]
        ada_done = [0]
        ada_pending = []

        def ada_upto(n):
            while ada_done[0] < len(ada_units) and ada_units[ada_done[0]][0] < n:
                _, u = ada_units[ada_done[0]]
                ada_done[0] += 1
                cols = slice(u["c"] * CW, (u["c"] + 1) * CW)
                raw_ready(dve, u)
                for k in range(UNIT_K):
                    kt = u["i"] * UNIT_K + k
                    if kt == 0:
                        link(v.tensor_scalar(MOD[:, cols], RAW[:, u["slot"], k, :], COND[:, kt:kt + 1], None, ALU.mult))
                        continue
                    ins = v.scalar_tensor_tensor(MOD[:, cols], RAW[:, u["slot"], k, :], COND[:, kt:kt + 1], MOD[:, cols], ALU.mult, ALU.add)
                    if k < UNIT_K - 1:
                        link(ins)
                tell(ins, ada_used, u["index"])

        def ada_drain(key):
            _, l, c = key
            cols = slice(c * CW, (c + 1) * CW)
            b = vec_ready(dve, ("ada_b", l, c))
            bank = product_ready(dve, key)[0]
            tell(v.tensor_tensor(MOD[:, cols], bank[:, :], b, ALU.add), drained, key)
            name = {2: "norm1_g", 3: "norm1_g", 8: "norm2_g", 9: "norm2_g"}.get(c)
            if name:
                name = (name, l, c - 2 if c < 6 else c - 8)
                g = vec_ready(dve, name)
                tell(v.scalar_tensor_tensor(MOD[:, cols], MOD[:, cols], 1.0, g, ALU.add, ALU.mult), vec_used, name)

        order = [c["key"] for c in chunks]

        def before(key):
            i = order.index(key)
            nxt = next((c for c in chunks[i + 1:] if c["kind"] == "gemm"), None)
            if nxt is not None:
                ada_upto(pos_in_stream[nxt["units"][-1]["index"]])

        def after(key):
            i = order.index(key) + 1
            while i < len(order) and order[i][0] == "ada":
                ada_upto(len(ring) if False else 1 + max(n for n, u in ada_units if (u["l"], u["c"]) == order[i][1:]))
                ada_drain(order[i])
                i += 1

        def turn_lo(tag, A, ntiles):
            for g in range(-(-ntiles // 2)):
                n = min(2, ntiles - 2 * g)
                dve.wait_ge(turned_hi.sem, turned_hi.at((tag, g)))
                tell(v.tensor_tensor(A[:, 2 * g:2 * g + n, 1, :], BANK[(TQ, TP)[g % 2]][:, 0:n * S].rearrange("p (k s) -> p k s", k=n),
                                A[:, 2 * g:2 * g + n, 0, :].bitcast(F32), ALU.subtract),
                    turned_lo, (tag, g))

        def turn_lo_ffn(tag, j, n):
            for t in range(NT):
                dve.wait_ge(turned_hi.sem, turned_hi.at((tag, j, t)))
                tell(v.tensor_tensor(AT[:, 4 * j:4 * j + n, 1, t * P:(t + 1) * P], BANK[(TQ, TP)[t]][:, 0:n * P].rearrange("p (k s) -> p k s", k=n),
                                AT[:, 4 * j:4 * j + n, 0, t * P:(t + 1) * P].bitcast(F32), ALU.subtract),
                    turned_lo, (tag, j, t))

        def h_rows(tag, shift, coef):
            dve.wait_ge(act_side.sem, act_side.at(("rms", tag)))
            link(v.reciprocal(RR[:, 0:NT], RSTD))
            for t in range(NT):
                link(v.scalar_tensor_tensor(O[:, t, :], X[:, t, :], RR[:, t:t + 1], MOD[:, coef:coef + D], ALU.mult, ALU.mult))
                say(v.tensor_tensor(O[:, t, :], O[:, t, :], MOD[:, shift:shift + D], ALU.add), ("h", tag, t))

        def attention(tag, heads, mask_of, weave, pt_banks, outputs, late=None):
            lag = 2 if len(pt_banks) == 1 else 3
            for k in range(len(heads) + lag):
                weave(k)
                h = k - 1
                if 0 <= h < len(heads):
                    hd = heads[h]
                    if hd["kind"] == "I":
                        dve.wait_ge(exped.sem, exped.at((tag, h)))
                        for t, cols in ((1, slice(0, S)), (0, slice(S, S + P))):
                            acc = IDX[:, cols]
                            if h == 0:
                                prev = con("band")[:, 0:S] if t else con("band")[:, P:S]
                            else:
                                prev = acc
                            ins = v.scalar_tensor_tensor(acc, SM[:, h % 2, cols], PROJ[:, t, WI + h:WI + h + 1], prev, ALU.mult, ALU.add)
                        tell(ins, masked, (tag, h))
                    else:
                        dve.wait_ge(scored.sem, scored.at((tag, h)))
                        if h >= 2 and heads[h - 2]["kind"] != "I":
                            dve.wait_ge(p_in_psum.sem, p_in_psum.at((tag, h - 2)))
                        m1, m0 = mask_of(hd)
                        m = 2 * h
                        bank = BANK[SB_[h % 2]]
                        v.tensor_tensor_reduce(SM[:, h % 2, S:S + P], bank[:, S:S + P], m0, SCALE, PICKED, ALU.add, ALU.max, MX[:, m:m + 1])
                        link(v.tensor_tensor_reduce(SM[:, h % 2, 0:S], bank[:, 0:S], m1, SCALE, PICKED, ALU.add, ALU.max, MX[:, m + 1:m + 2]))
                        tell(v.tensor_scalar(NM[:, m:m + 2], MX[:, m:m + 2], -1.0, None, ALU.mult),
                    masked, (tag, h))
                h = k - 2
                if 0 <= h < len(heads) and heads[h]["kind"] != "I":
                    dve.wait_ge(p_in_psum.sem, p_in_psum.at((tag, h)))
                    if h >= 2 and heads[h - 2]["kind"] != "I":
                        dve.wait_ge(headed.sem, headed.at((tag, h - 2)))
                    bank = BANK[pt_banks[h % len(pt_banks)]]
                    tell(v.tensor_copy(PT[:, h % 2, :], bank[:, 0:3 * P]), p_turned, (tag, h))
                if late:
                    late(k)
                h = k - lag
                if 0 <= h < len(heads) and heads[h]["kind"] != "I":
                    outputs(h, heads[h], BANK[pt_banks[h % len(pt_banks)]])

        def scaled_output(tag):
            def put(h, hd, bank):
                m = 2 * h
                dve.wait_ge(exped.sem, exped.at((tag, h)))
                link(v.reciprocal(RR[:, m:m + 2], RS[:, m:m + 2]))
                dve.wait_ge(headed.sem, headed.at((tag, h)))
                tell(v.tensor_tensor(O[:, :, hd["o"]:hd["o"] + DH], bank[:, 384:512].rearrange("p (t d) -> p t d", t=NT),
                                RR[:, m:m + 2].unsqueeze(2).to_broadcast([P, NT, DH]), ALU.mult),
                    head_out, (tag, h))
            return put

        dve.wait_ge(c_in, 16)
        dve.wait_ge(act_side.sem, act_side.at("cond"))
        link(v.scalar_tensor_tensor(COND, CT, 1.0, COND, ALU.add, ALU.mult))
        link(v.tensor_scalar(COND, COND, 0.5, None, ALU.mult))
        dve.wait_ge(rel_in, 16)
        link(v.tensor_copy(RE[:, 0:S], RB[:, 1:S + 1]))
        say(v.tensor_copy(RE[:, S:3 * P], RB[:, 2 * REL:2 * REL + 1].to_broadcast([DEPTH * HB, P])), "rel")
        dve.wait_ge(pos_in, 16)
        dve.wait_ge(const_in, 16)
        link(v.tensor_copy(POSF, POS[:, :]))
        for t in range(NT):
            link(v.tensor_scalar(ANG[:, 8 * t:8 * t + 8], con("inv"), POSF[:, t:t + 1], None, ALU.mult))
        magic = float(1.5 * 2 ** 23)
        two_pi = 2 * np.pi
        c1 = float(np.float32(6.28125))
        c2 = float(np.float32(round((two_pi - c1) * 2 ** 21) / 2 ** 21))
        c3 = float(np.float32(two_pi - c1 - c2))
        link(v.tensor_scalar(KR, ANG, float(1 / two_pi), magic, ALU.mult, ALU.add))
        link(v.tensor_scalar(KR, KR, -magic, None, ALU.add))
        link(v.scalar_tensor_tensor(RED, KR, -c1, ANG, ALU.mult, ALU.add))
        link(v.scalar_tensor_tensor(RED, KR, -c2, RED, ALU.mult, ALU.add))
        link(v.scalar_tensor_tensor(RED, KR, -c3, RED, ALU.mult, ALU.add))
        pi_in = float(np.nextafter(np.float32(np.pi), np.float32(0)))
        say(v.tensor_scalar(SIN, RED, pi_in, -pi_in, ALU.min, ALU.max), "sin")
        link(v.tensor_scalar(KR, RED, float(np.pi / 2), -float(two_pi), ALU.is_gt, ALU.mult))
        link(v.scalar_tensor_tensor(RED, RED, float(np.pi / 2), KR, ALU.add, ALU.add))
        say(v.tensor_scalar(COS, RED, pi_in, -pi_in, ALU.min, ALU.max), "cos")
        v.memset(HT[0:64, KT, :, :].bitcast(F32), 0.0)
        for c in range(4):
            ada_upto(KT // UNIT_K * (c + 1))
            if c:
                ada_drain(("ada", 0, c - 1))
        ada_drain(("ada", 0, 3))
        dve.wait_ge(x_in, 16)

        for l in range(DEPTH):
            h_rows(("n1", l), 0, D)
            turn_lo(("n1", l), HT, KT)
            if l == 0:
                dve.wait_ge(act_side.sem, act_side.at("cos"))
            tmp = SM[:, :, :].rearrange("p a b -> p (a b)")

            def rope(col, n, l):
                for t in range(NT):
                    hv = PROJ[:, t, col:col + n * DH].rearrange("p (h d) -> p h d", d=DH)
                    x1, x2 = hv[:, :, 0:8], hv[:, :, 8:16]
                    cs = COS[:, 8 * t:8 * t + 8].unsqueeze(1).to_broadcast([P, n, 8])
                    sn = SIN[:, 8 * t:8 * t + 8].unsqueeze(1).to_broadcast([P, n, 8])
                    a, b, c, d = (tmp[:, 96 * i:96 * i + 8 * n].rearrange("p (h d) -> p h d", d=8) for i in range(4))
                    v.tensor_tensor(a, x1, cs, ALU.mult)
                    v.tensor_tensor(b, x2, sn, ALU.mult)
                    v.tensor_tensor(c, x2, cs, ALU.mult)
                    link(v.tensor_tensor(d, x1, sn, ALU.mult))
                    v.tensor_tensor(x1, a, b, ALU.subtract)
                    link(v.tensor_tensor(x2, c, d, ALU.add))

            for j in range(N_PROJ):
                key = ("proj", l, j)
                n = min(CW, PROJ_W - j * CW)
                before(key)
                b = vec_ready(dve, ("b_in", l, j))
                banks = product_ready(dve, key)
                v.tensor_tensor(PROJ[:, 0, j * CW:j * CW + n], banks[0][:, 0:n], b, ALU.add)
                tell(v.tensor_tensor(PROJ[:, 1, j * CW:j * CW + n], banks[1][:, 0:n], b, ALU.add), drained, key)
                if j == 1:
                    rope(QA, 2 * HA, l)
                if j == 3:
                    rope(QI, HI + 1, l)
                    wi = PROJ[:, :, WI:WI + HI]
                    link(v.tensor_scalar(wi, wi, float(np.float32(HI ** -0.5 * DH ** -0.5)), None, ALU.mult))
                after(key)
            z = PROJ[:, :, FC:FC + HC]
            as2 = lambda a: a.rearrange("p (t h) -> p t h", t=NT)
            link(v.tensor_scalar(as2(ZN), z, -1.0, None, ALU.mult))
            say(v.tensor_tensor(as2(ZA), as2(ZN), z, ALU.min), ("nabs", l))
            dve.wait_ge(act_side.sem, act_side.at(("ze", l)))
            say(v.tensor_scalar(ZU, ZE, 1.0, None, ALU.add), ("zu", l))
            dve.wait_ge(rows.sem, rows.at(("zu", l)))
            link(v.scalar_tensor_tensor(ZD, ZU, -1.0, ZE, ALU.add, ALU.subtract))
            link(v.reciprocal(ZA, ZU))
            link(v.tensor_tensor(ZD, ZD, ZA, ALU.mult))
            dve.wait_ge(act_side.sem, act_side.at(("zl", l)))
            link(v.tensor_tensor(ZL, ZL, ZD, ALU.subtract))
            say(v.scalar_tensor_tensor(LF, ZN, 0.0, ZL, ALU.max, ALU.add), ("logf", l))
            dve.wait_ge(rows.sem, rows.at(("logf", l)))

            def logf_wide(c, l=l):
                for t in range(NT):
                    ins = v.tensor_scalar(LB[:, t, :], con("ones"), LF[:, t * HC + c:t * HC + c + 1], None, ALU.mult)
                say(ins, ("logf_wide", l, c))

            def mask_of(hd, l=l):
                if hd["kind"] == "B":
                    return MB[:, hd["h"], ::-1], MB[:, hd["h"], 0:P][:, ::-1]
                if hd["kind"] == "C":
                    return CM[:, hd["h"], 0:S], CM[:, hd["h"], S:S + P]
                return IDX[:, 0:S], IDX[:, S:S + P]

            first = by_key[("gate", l, 0)]["units"][0]["index"]

            def weave(k, l=l, first=first):
                ada_upto(pos_in_stream[first + min(k + 4, 4 * N_GATE - 1)])
                if k == 2:
                    dve.wait_ge(forget.sem, forget.at((l, "cols")))
                    link(v.tensor_copy(F8, BANK[TP][:, 0:2 * HC]))
                    logf_wide(0)
                elif 3 <= k < 3 + HC:
                    c = k - 3
                    dve.wait_ge(forget.sem, forget.at((l, c)))
                    v.scalar_tensor_tensor(CM[:, c, 0:S], BANK[TP][:, 0:S], F8[:, HC + c:HC + c + 1], con("causal"), ALU.subtract, ALU.add)
                    link(v.scalar_tensor_tensor(CM[:, c, S:S + P], BANK[TP][:, 0:P], F8[:, c:c + 1], con("causal")[:, P:S], ALU.subtract, ALU.add))
                    if c + 1 < HC:
                        logf_wide(c + 1)
                if HI - HB <= k < HI:
                    h = k - (HI - HB)
                    dve.wait_ge(bias_in[h], 16 * (l + 1))
                    link(v.scalar_tensor_tensor(MB[:, h, :], MB[:, h, :], 1 / SCALE, con("band")[:, ::-1], ALU.mult, ALU.add))

            def late(k, l=l):
                if k % 4 == 0 and k:
                    key = ("gate", l, k // 4 - 1)
                    before(key)
                    b = vec_ready(dve, ("b_gate", l, k // 4 - 1))
                    banks = product_ready(dve, key)
                    j = k // 4 - 1
                    v.tensor_tensor(GATES[:, 0, j * CW:(j + 1) * CW], banks[0][:, :], b, ALU.add)
                    tell(v.tensor_tensor(GATES[:, 1, j * CW:(j + 1) * CW], banks[1][:, :], b, ALU.add), drained, key)
                    after(key)
                r = k - (HI + 2)
                if 0 <= r < TOPK // 8:
                    for a, cols in ((0, slice(0, S)), (8, slice(S, S + P))):
                        ins = v.max(MAX8[:, a:a + 8], IDX[:, cols])
                    link(ins)
                    for a, cols in ((0, slice(0, S)), (8, slice(S, S + P))):
                        ins = v.match_replace(IDX[:, cols], MAX8[:, a:a + 8], IDX[:, cols], PICKED)
                    link(ins)
                    if r == TOPK // 8 - 1:
                        link(v.tensor_scalar(IDX[:, :], IDX[:, :], PICKED, NEG, ALU.not_equal, ALU.mult))

            attention(l, heads_one(), mask_of, weave, (TP,), scaled_output(l), late)
            last = len(heads_one()) - 1
            dve.wait_ge(head_out.sem, head_out.at((l, last)))
            turn_lo(("o", l), HT, KT)
            dve.wait_ge(turned_lo.sem, turned_lo.at((("o", l), KT // 2 - 1)))
            link(v.tensor_copy(HT[64:128, KT, :, :], HT[64:128, 5, :, :].bitcast(F32)))
            say(v.memset(HT[64:128, 5, :, :].bitcast(F32), 0.0), ("halves", l))
            for cc in range(2):
                for n, b in enumerate("ABC"):
                    key = ("branch", l, cc, b)
                    banks = product_ready(dve, key)
                    j = (n * D + cc * CW) // CW
                    dve.wait_ge(act_side.sem, act_side.at(("gate", l, j)))
                    for t in range(NT):
                        g = GATES[:, t, j * CW:(j + 1) * CW]
                        ins = v.scalar_tensor_tensor(O[:, t, cc * CW:(cc + 1) * CW] if n == 0 else g, g, 1.0, banks[t][:, :], ALU.add, ALU.mult)
                    tell(ins, drained, key)
                    if n:
                        for t in range(NT):
                            ins = v.tensor_tensor(O[:, t, cc * CW:(cc + 1) * CW], O[:, t, cc * CW:(cc + 1) * CW],
                                                  GATES[:, t, j * CW:(j + 1) * CW], ALU.add)
                        if cc == 1 and n == 2:
                            say(ins, ("y", l))
                        else:
                            link(ins)
            turn_lo(("y", l), AT, KT)

            def add_to_x(key, gain, factor, tmp_of, event, l=l):
                cc = key[-1]
                before(key)
                banks = product_ready(dve, key)
                for t in range(NT):
                    ins = v.scalar_tensor_tensor(tmp_of(t), banks[t][:, :], factor, MOD[:, gain + cc * CW:gain + (cc + 1) * CW], ALU.mult, ALU.mult)
                tell(ins, drained, key)
                for t in range(NT):
                    xs = X[:, t, cc * CW:(cc + 1) * CW]
                    ins = v.tensor_tensor(xs, xs, tmp_of(t), ALU.add)
                    if cc == 1:
                        say(ins, ("x", event, t))
                if cc == 0:
                    link(ins)
                after(key)

            for cc in range(2):
                add_to_x(("wout", l, cc), 2 * D, 0.5, lambda t: GATES[:, t, D:D + CW], ("mid1", l))
            dve.wait_ge(rows.sem, rows.at(("x", ("mid1", l), 1)))
            h_rows(("n2", l), 3 * D, 4 * D)
            turn_lo(("n2", l), HT, KT)
            n_ff = -(-FFN // CW)
            for j in range(n_ff):
                n = min(CW, FFN - j * CW)
                kg, ku = ("ffg", l, j), ("ffu", l, j)
                before(kg)
                banks = product_ready(dve, kg)
                dve.wait_ge(act_side.sem, act_side.at(("tg", l, j)))
                for t in range(NT):
                    ins = v.scalar_tensor_tensor(TG[:, j % 2, t, 0:n], TG[:, j % 2, t, 0:n], 1.0, banks[t][:, 0:n], ALU.add, ALU.mult)
                tell(ins, drained, kg)
                if j:
                    turn_lo_ffn(("a", l), j - 1, CW // P)
                before(ku)
                banks = product_ready(dve, ku)
                for t in range(NT):
                    ins = v.scalar_tensor_tensor(O[:, t, (j % 2) * CW:(j % 2) * CW + n], TG[:, j % 2, t, 0:n], 0.5, banks[t][:, 0:n], ALU.mult, ALU.mult)
                tell(ins, drained, ku)
                after(ku)
            turn_lo_ffn(("a", l), n_ff - 1, (FFN - (n_ff - 1) * CW) // P)
            for cc in range(2):
                add_to_x(("ffo", l, cc), 5 * D, 1.0, lambda t: TG[:, 0, t, :], ("end", l))
            dve.wait_ge(rows.sem, rows.at(("x", ("end", l), 1)))

        def vec_free(name, ins):
            tell(ins, vec_used, name)

        dve.wait_ge(act_side.sem, act_side.at(("rms", "final")))
        link(v.reciprocal(RR[:, 0:NT], RSTD))
        for half in range(2):
            g = vec_ready(dve, ("final_g", half))
            for t in range(NT):
                xs = X[:, t, half * CW:(half + 1) * CW]
                ins = v.scalar_tensor_tensor(xs, xs, RR[:, t:t + 1], g, ALU.mult, ALU.mult)
            vec_free(("final_g", half), ins)

        def layer_norm(tag, names):
            g_name, b_name, i = names
            st = STAT.rearrange("p (t c s) -> p t c s", t=NT, c=2)
            for t in range(NT):
                for c in range(2):
                    ins = v.bn_stats(st[:, t, c, :], X[:, t, c * CW:(c + 1) * CW])
            link(ins)
            for t in range(NT):
                ins = v.bn_aggr(MV[:, 2 * t:2 * t + 2], STAT[:, 12 * t:12 * t + 12])
            say(ins, ("var", tag))
            dve.wait_ge(act_side.sem, act_side.at(("root", tag)))
            link(v.reciprocal(RR[:, 0:NT], RSTD))
            for t in range(NT):
                link(v.tensor_scalar(X[:, t, :], X[:, t, :], MV[:, 2 * t:2 * t + 1], RR[:, t:t + 1], ALU.subtract, ALU.mult))
            for name, op in ((g_name, ALU.mult), (b_name, ALU.add)):
                for half in range(2):
                    g = vec_ready(dve, (name, i, half))
                    for t in range(NT):
                        xs = X[:, t, half * CW:(half + 1) * CW]
                        ins = v.tensor_tensor(xs, xs, g, op)
                    vec_free((name, i, half), ins)

        def residual(key):
            cc = key[-1]
            banks = product_ready(dve, key)
            for t in range(NT):
                xs = X[:, t, cc * CW:(cc + 1) * CW]
                ins = v.scalar_tensor_tensor(xs, xs, ALPHA, banks[t][:, :], ALU.mult, ALU.add)
            tell(ins, drained, key)

        for i in range(2):
            heads = heads_two(i)
            nh = len(heads)
            turn_lo(("x", i), HT, KT)
            w = 3 * nh * DH
            for j in range(-(-w // CW)):
                key = ("qkv", i, j)
                n = min(CW, w - j * CW)
                banks = product_ready(dve, key)
                rot = max(0, min(n, 2 * nh * DH - j * CW))
                for t in range(NT):
                    if rot:
                        r = rot // DH
                        four = lambda a: a.rearrange("p (h two d) -> p h two d", two=2, d=DH // 2)
                        wide = lambda name: con(name).rearrange("p (two d) -> p two d", two=2).unsqueeze(1).to_broadcast([P, r, 2, DH // 2])
                        px = banks[t][:, 0:rot]
                        v.tensor_tensor(four(RTMP[:, 0, 0:rot]), four(px), wide(f"cc{t}"), ALU.mult)
                        link(v.tensor_tensor(four(RTMP[:, 1, 0:rot]), four(px)[:, :, ::-1, :], wide(f"ss{t}"), ALU.mult))
                        ins = v.tensor_tensor(QKV[:, t, j * CW:j * CW + rot], RTMP[:, 0, 0:rot], RTMP[:, 1, 0:rot], ALU.add)
                    if rot < n:
                        if rot:
                            link(ins)
                        ins = v.tensor_copy(QKV[:, t, j * CW + rot:j * CW + n], banks[t][:, rot:n])
                    if t < NT - 1:
                        link(ins)
                tell(ins, drained, key)
            if i == 0:
                attention(("two", i), heads, lambda hd: (con("causal"), con("causal")[:, P:S]), lambda k: None, (TP, 3),
                          scaled_output(("two", i)))
                dve.wait_ge(head_out.sem, head_out.at((("two", i), nh - 1)))
            else:
                dve.wait_ge(dil_in, 16)

                def raw_output(h, hd, bank):
                    dve.wait_ge(headed.sem, headed.at((("two", 1), h)))
                    tell(v.tensor_copy(O[:, :, hd["o"]:hd["o"] + DH], bank[:, 384:512].rearrange("p (t d) -> p t d", t=NT)),
                    head_out, (("two", 1), h))

                attention(("two", i), heads, lambda hd: (DILM[:, hd["h"] // 4, :], DILM[:, hd["h"] // 4, P:S]), lambda k: None,
                          (TP, 3), raw_output)
                dve.wait_ge(head_out.sem, head_out.at((("two", i), nh - 1)))
                n2 = 4 * NT
                mx, rs, ww = MX[:, 0:3 * n2], RS[:, 0:3 * n2], NM[:, 0:3 * n2]
                gm = RR[:, 0:n2]
                link(v.tensor_tensor(gm, mx[:, 0:n2], mx[:, n2:2 * n2], ALU.max))
                link(v.tensor_tensor(gm, gm, mx[:, 2 * n2:3 * n2], ALU.max))
                for g in range(3):
                    ins = v.tensor_tensor(mx[:, g * n2:(g + 1) * n2], mx[:, g * n2:(g + 1) * n2], gm, ALU.subtract)
                say(ins, "group_max")
                dve.wait_ge(act_side.sem, act_side.at("group_exp"))
                link(v.tensor_tensor(rs, rs, ww, ALU.mult))
                link(v.tensor_tensor(gm, rs[:, 0:n2], rs[:, n2:2 * n2], ALU.add))
                link(v.tensor_tensor(gm, gm, rs[:, 2 * n2:3 * n2], ALU.add))
                link(v.reciprocal(gm, gm))
                for g in range(3):
                    ins = v.tensor_tensor(ww[:, g * n2:(g + 1) * n2], ww[:, g * n2:(g + 1) * n2], gm, ALU.mult)
                link(ins)
                for t in range(NT):
                    ot = O[:, t, 0:nh * DH].rearrange("p (h d) -> p h d", d=DH)
                    say(v.tensor_tensor(ot, ot, ww.rearrange("p (h t) -> p h t", t=NT)[:, :, t:t + 1].to_broadcast([P, nh, DH]), ALU.mult),
                        "weighted" if t == NT - 1 else "weighting")
            turn_lo(("o2", i), HT, nh * DH // P)
            for cc in range(2):
                residual(("wo", i, cc))
            layer_norm(("mid", i), ("ln_mix_g", "ln_mix_b", i))
            turn_lo(("m", i), HT, KT)
            for j in range(DFF // CW):
                key = ("mi", i, j)
                dve.wait_ge(act_side.sem, act_side.at(("relu", i, j)))
                if j >= 2:
                    dve.wait_ge(turned.sem, turned.at((("a2", i), j - 2, 1)))
                for t in range(NT):
                    ins = v.tensor_tensor(O[:, t, (j % 2) * CW:(j % 2 + 1) * CW], RT[:, j % 2, t, :], RT[:, j % 2, t, :], ALU.mult)
                say(ins, ("a2", i, j))
                if j:
                    turn_lo_ffn(("a2", i), j - 1, CW // P)
            turn_lo_ffn(("a2", i), DFF // CW - 1, CW // P)
            for cc in range(2):
                residual(("mo", i, cc))
            layer_norm(("end2", i), ("ln_mlp_g", "ln_mlp_b", i))


def turn_ffn(pe, turned, turned_lo, rows, drained, tag, j, n, BANK, TQ, TP, O, con):
    signal_, event = (drained, ("ffu", tag[1], j)) if tag[0] == "a" else (rows, (*tag, j))
    pe.wait_ge(signal_.sem, signal_.at(event))
    for t in range(NT):
        if j:
            pe.wait_ge(turned_lo.sem, turned_lo.at((tag, j - 1, t)))
        for k in range(n):
            ins = pe.transpose(BANK[(TQ, TP)[t]][:, k * P:(k + 1) * P],
                               O[:, t, (j % 2) * CW + k * P:(j % 2) * CW + (k + 1) * P], con("ident"))
        ins.then_inc(turned.sem, turned.mark((tag, j, t)))


def unit_index(key):
    chunks, _ = plan()
    return next(c for c in chunks if c["key"] == key)["units"][0]["index"]


bias_at = {unit_index(("proj", l, 0)): l for l in range(DEPTH)}
dil_at = unit_index(("mi", 0, 0))

_INS = ["x", "c", "positions", "ada_w", "ada_b", "norm1_g", "w_in", "b_in", "rel_bias", "w_branch", "w_out",
        "norm2_g", "w_ffn_in", "w_ffn_out", "final_g", "moba_w_qkv_2", "moba_w_o_2", "dil_w_qkv_2", "dil_w_o_2",
        "mlp_w_in_2", "mlp_w_out_2", "ln_mix_g_2", "ln_mix_b_2", "ln_mlp_g_2", "ln_mlp_b_2"]


def traced(nc, arrays, cat, book):
    dram = {}
    for name, a in arrays.items():
        short = name.removeprefix("in_").removesuffix("_2")
        dram[short] = nc.dram_tensor(name, a.shape, mybir.dt.from_np(a.dtype), kind="ExternalInput").ap()
    out = nc.dram_tensor("out_0_dram", (1, S, D), F32, kind="ExternalOutput").ap()
    build(nc, dram, out, cat, book)
    return nc


def kernel(**inputs):
    import concourse.bacc as bacc
    from concourse.bass_utils import run_bass_kernel_spmd

    const, cat = constants()
    arrays = {f"in_{name}": np.ascontiguousarray(inputs[name]) for name in _INS}
    arrays["in_constants"] = const
    values = {}
    traced(bacc.Bacc("TRN2", target_bir_lowering=False, num_devices=1), arrays, cat, ({}, values))
    nc = traced(bacc.Bacc("TRN2", target_bir_lowering=False, num_devices=1), arrays, cat, (values, {}))
    return run_bass_kernel_spmd(nc, [arrays], core_ids=[0]).results[0]["out_0_dram"]
```

```python
from contextlib import ExitStack

import numpy as np

import concourse.bass as bass
from concourse import mybir

F32 = mybir.dt.float32
F32R = mybir.dt.float32r
I32 = mybir.dt.int32
ALU = mybir.AluOpType
ACT = mybir.ActivationFunctionType
AX_X = mybir.AxisListType.X

P = 128
S = 256
NT = S // P
D = 1024
KT = D // P
CW = 512
DEPTH = 2
DH = 64
CHUNK = 64
HA, HB, HC, HI = 6, 5, 5, 8
FFN = 2816
DFF = 4096
REL = 128
MOBA_H, DIL_H = 16, 12
DIL = ((128, 1), (512, 4), (2048, 16))
TOPK = S // 4
ALPHA = (2.0 * DEPTH) ** 0.25
RMS_EPS, LN_EPS = 1e-6, 1e-5
SCALE = DH ** -0.5
NEG = -1e30
IDX_OUT = -1e38
PICKED = -3e38

QA, KA, VA = 0, HA * DH, 2 * HA * DH
QI = 3 * HA * DH
KI = QI + HI * DH
WI = KI + DH
QB = WI + HI
KB, VB = QB + HB * DH, QB + 2 * HB * DH
QC = QB + 3 * HB * DH
KC, VC = QC + HC * DH, QC + 2 * HC * DH
FC = QC + 3 * HC * DH
GATE = FC + HC
PROJ_W = GATE + 1
IN_W = GATE + 3 * D
N_PROJ = -(-PROJ_W // CW)
N_GATE = 3 * D // CW

NR = 5
NH = 4
NV = 5
UNIT_K = 2


def constants():
    p = np.arange(P)[:, None]
    k = np.arange(S)[None, :]
    d = P + p - k
    parts = [("ident", np.eye(P)), ("ones", np.ones((P, P)))]
    parts += [("causal", np.where(d >= 0, 0.0, NEG))]
    parts += [("band", np.where(k // CHUNK <= (P + p) // CHUNK, 0.0, NEG))]
    for t in range(NT):
        parts.append((f"tri{t}", np.where(t * P + p <= k, 1 / SCALE, 0.0)))
    rot = DH // 4
    inv = np.float32(500000.0) ** (-np.arange(0, rot, 2, dtype=np.float32) / np.float32(rot))
    parts.append(("inv", np.tile(inv.astype(np.float32)[None], (P, 1))))
    inv2 = (1.0 / (np.float32(10000.0) ** (np.arange(0, DH, 2, dtype=np.float32) / np.float32(DH)))).astype(np.float32)
    for t in range(NT):
        ang = ((t * P + p).astype(np.float32) * inv2[None]).astype(np.float32).astype(np.float64)
        parts.append((f"cc{t}", np.concatenate([np.cos(ang), np.cos(ang)], 1)))
        parts.append((f"ss{t}", np.concatenate([-np.sin(ang), np.sin(ang)], 1)))
    parts.append(("eps", np.tile(np.array([[RMS_EPS, LN_EPS]]), (P, 1))))
    for g, (window, dil) in enumerate(DIL):
        parts.append((f"dil{g}", np.where((d >= 0) & (d <= window) & (d % dil == 0), 0.0, NEG)))
    at, cols = {}, 0
    for name, a in parts:
        at[name] = (cols, cols + a.shape[1])
        cols += a.shape[1]
    return np.concatenate([a for _, a in parts], 1).astype(np.float32), at


class Signal:

    def __init__(self, sem, name, book):
        self.sem, self.name, self.known, self.new = sem, name, book[0], book[1]
        self.count = 0

    def mark(self, event):
        self.count += 1
        self.new[self.name, event] = self.count
        return 1

    def at(self, event):
        return self.known[self.name, event] if self.known else 1


def plan():
    chunks, stream = [], []
    count = {"w": 0, "ada": 0, "vec": 0}
    pair = [0]

    def chunk(key, src, row0, ktiles, col0, ncols, steps=None):
        c = dict(key=key, kind="gemm", pair=pair[0] % 2, ncols=ncols, units=[])
        pair[0] += 1
        for k0 in range(0, ktiles, UNIT_K):
            n = min(UNIT_K, ktiles - k0)
            u = dict(kind="w", index=count["w"], n=n, ncols=ncols, src=(src, row0 + k0 * P, n, col0, ncols))
            u["tiles"] = [[(k0 + i, i)] for i in range(n)] if steps is None else steps[k0 // UNIT_K]
            count["w"] += 1
            c["units"].append(u)
        chunks.append(c)
        return c

    def vec(name, src, col0, ncols=CW):
        v = dict(kind="vec", index=count["vec"], name=name, src=(src, col0, ncols), ncols=ncols)
        count["vec"] += 1
        return v

    def ada(l, c):
        units = []
        for i in range(KT // UNIT_K):
            units.append(dict(kind="ada", index=count["ada"], l=l, c=c, i=i))
            count["ada"] += 1
        return dict(key=("ada", l, c), kind="ada", units=units)

    def ada_vecs(l, c):
        vs = [vec(("ada_b", l, c), ("ada_b", l), c * CW)]
        if c in (2, 3):
            vs.append(vec(("norm1_g", l, c - 2), ("norm1_g", l), (c - 2) * CW))
        if c in (8, 9):
            vs.append(vec(("norm2_g", l, c - 8), ("norm2_g", l), (c - 8) * CW))
        return vs

    def put(c, vec_args=None):
        stream.extend(c["units"][:-1])
        if vec_args:
            stream.append(vec(*vec_args))
        stream.append(c["units"][-1])

    def phase(parts, adas, summed=True):
        units = [(l, c, n) for l, c in adas for n in range(KT // UNIT_K)]
        made = {}
        total = sum(-(-args[3] // UNIT_K) for _, args in parts)
        seen = sent = 0
        for vec_args, args in parts:
            done = []
            c = chunk(*args)
            for n, u in enumerate(c["units"]):
                if vec_args and n == len(c["units"]) - 1:
                    stream.append(vec(*vec_args))
                stream.append(u)
                seen += 1
                while sent * total < seen * len(units) and sent < len(units):
                    l, a, i = units[sent]
                    if i == 0:
                        made[l, a] = ada(l, a)
                    last_ = i == KT // UNIT_K - 1
                    if last_ and summed:
                        stream.extend(ada_vecs(l, a))
                    stream.append(made[l, a]["units"][i])
                    if last_:
                        done.append(made[l, a])
                    sent += 1
            if summed:
                chunks.extend(done)
        return list(made.values())

    for c in (2, 3, 0):
        a = ada(0, c)
        chunks.append(a)
        stream.extend(a["units"])
        stream.extend(ada_vecs(0, c))
    last_shift = ada(0, 1)
    chunks.append(last_shift)
    for l in range(DEPTH):
        start = len(stream)
        parts = []
        for j in range(N_PROJ):
            n = min(CW, PROJ_W - j * CW)
            parts.append(((("b_in", l, j), ("b_in", l), j * CW, n), (("proj", l, j), ("w_in", l), 0, KT, j * CW, n)))
        phase(parts, [(l, c) for c in ((4, 5, 6, 7), (8, 9, 10, 11))[l]])
        if l == 0:
            at = [n for n in range(start, len(stream)) if stream[n]["kind"] == "w"][1] + 1
            stream[at:at] = last_shift["units"] + ada_vecs(0, 1)
        parts = []
        for j in range(N_GATE):
            parts.append(((("b_gate", l, j), ("b_in", l), GATE + j * CW), (("gate", l, j), ("w_in", l), 0, KT, GATE + j * CW, CW)))
        late = phase(parts, [(0, 8), (0, 9)] if l == 0 else [], summed=False)
        for cc in range(D // CW):
            for b, k0, kn, st in (("C", 5, 3, [[[(8, 0)], [(6, 1)]], [[(7, 0)]]]),
                                  ("B", 3, 3, [[[(3, 0)], [(4, 1)]], [[(5, 0)]]]),
                                  ("A", 0, 3, [[[(0, 0)], [(1, 1)]], [[(2, 0)]]])):
                put(chunk(("branch", l, cc, b), ("w_branch", l), k0 * P, kn, cc * CW, CW, steps=st))
        for a in late:
            stream.extend(ada_vecs(*a["key"][1:]))
        for cc in range(D // CW):
            put(chunk(("wout", l, cc), ("w_out", l), 0, KT, cc * CW, CW))
            if cc == 0:
                chunks.extend(late)
        parts = []
        for j in range(-(-FFN // CW)):
            n = min(CW, FFN - j * CW)
            parts.append((None, (("ffg", l, j), ("w_ffn_in", l), 0, KT, j * CW, n)))
            parts.append((None, (("ffu", l, j), ("w_ffn_in", l), 0, KT, FFN + j * CW, n)))
        phase(parts, [(0, 10), (0, 11)] + [(1, c) for c in range(8)] if l == 0 else [])
        for cc in range(D // CW):
            put(chunk(("ffo", l, cc), ("w_ffn_out", l), 0, FFN // P, cc * CW, CW))
    stream.extend(vec(("final_g", h), ("final_g",), h * CW) for h in range(2))
    for i in range(2):
        heads = (MOBA_H, DIL_H)[i]
        w = 3 * heads * DH
        for j in range(-(-w // CW)):
            n = min(CW, w - j * CW)
            put(chunk(("qkv", i, j), (("moba_w_qkv", "dil_w_qkv")[i],), 0, KT, j * CW, n))
        for cc in range(2):
            put(chunk(("wo", i, cc), (("moba_w_o", "dil_w_o")[i],), 0, heads * DH // P, cc * CW, CW))
        stream.extend(vec((v, i, h), (v, i), h * CW) for h in range(2) for v in ("ln_mix_g", "ln_mix_b"))
        for j in range(DFF // CW):
            put(chunk(("mi", i, j), ("mlp_w_in", i), 0, KT, j * CW, CW))
        for cc in range(2):
            put(chunk(("mo", i, cc), ("mlp_w_out", i), 0, DFF // P, cc * CW, CW))
        stream.extend(vec((v, i, h), (v, i), h * CW) for h in range(2) for v in ("ln_mlp_g", "ln_mlp_b"))
    for n, v in enumerate(v for v in stream if v["kind"] == "vec"):
        v["index"] = n
    for kind in ("ada", "w"):
        for n, u in enumerate(u for u in stream if u["kind"] == kind):
            u["index"] = n
    last = {}
    for c in chunks:
        place = c["pair"] if c["kind"] == "gemm" else ("ada", c["key"][2] % 2)
        c["before"] = last.get(place)
        last[place] = c["key"]
    return chunks, stream


def heads_one():
    out = [dict(kind="I", h=h, q=QI + h * DH, k=KI) for h in range(HI)]
    out += [dict(kind="B", h=h, q=QB + h * DH, k=KB + h * DH, v=VB + h * DH, o=(HA + h) * DH) for h in range(HB)]
    out += [dict(kind="C", h=h, q=QC + h * DH, k=KC + h * DH, v=VC + h * DH, o=(HA + HB + h) * DH) for h in range(HC)]
    out += [dict(kind="A", h=h, q=QA + h * DH, k=KA + h * DH, v=VA + h * DH, o=h * DH) for h in range(HA)]
    return out


def heads_two(i):
    n = (MOBA_H, DIL_H)[i]
    kind = "MD"[i]
    return [dict(kind=kind, h=h, q=h * DH, k=(n + h) * DH, v=(2 * n + h) * DH, o=h * DH) for h in range(n)]


def build(nc, dram, out, cat, book):
    with ExitStack() as ctx:
        program(nc, ctx, dram, out, cat, book)


def program(nc, ctx, dram, out, cat, book):
    chunks, stream = plan()
    by_key = {c["key"]: c for c in chunks}
    vec_of = {i["name"]: i for i in stream if i["kind"] == "vec"}
    ring = [i for i in stream if i["kind"] != "vec"]
    for n, i in enumerate(ring):
        i["slot"], i["turn"] = n % NR, n // NR
        i["evicts"] = ring[n - NR] if n >= NR else None

    plan_at = [-(-nc.sbuf_base // 64) * 64]
    top = []

    def place(name, shape, dt=F32, at=None):
        size = int(np.prod(shape[1:])) * 4
        offset = plan_at[0] if at is None else at
        if at is None:
            plan_at[0] += -(-size // 32) * 32
        top.append(offset + size)
        t = nc.alloc_sbuf_tensor_at(name, list(shape), dt, offset=offset)
        return t, offset

    X, _ = place("x_rows", [P, NT, D])
    O, _ = place("o_rows", [P, NT, D])
    HT, _ = place("turned", [P, KT + 1, 2, S], F32R)
    RAW, _ = place("raw_units", [P, NR, UNIT_K, CW])
    HI_, _ = place("hi_units", [P, NH, UNIT_K, CW], F32R)
    LO, _ = place("lo_units", [P, NH, UNIT_K, CW], F32R)
    VEC, _ = place("row_vectors", [P, NV, CW])
    PROJ, union = place("proj_rows", [P, NT, PROJ_W])
    GATES, _ = place("gate_rows", [P, NT, 3 * D])
    MOD, _ = place("mod_rows", [P, 6 * D])
    AT, _ = place("turned_wide", [P, DFF // P, 2, S], F32R, at=union)
    TG, _ = place("ffn_tanh", [P, 2, NT, CW], at=union + FFN // P * 2 * S * 4)
    RT, _ = place("mlp_relu", [P, 2, NT, CW], at=union + DFF // P * 2 * S * 4)
    QKV, _ = place("qkv_rows", [P, NT, 3 * D], at=union)
    RTMP, _ = place("rotary_tmp", [P, 2, CW], at=union + DFF // P * 2 * S * 4)
    QKV_END = union + NT * 3 * D * 4
    QKT2, _ = place("qk_turned_2", [DH, 3, 2 * S], at=QKV_END)
    PT2, _ = place("probs_turned_2", [P, 3, 3 * P], at=QKV_END + 3 * 2 * S * 4)
    SM, _ = place("scores", [P, 3, 3 * P])
    PT, _ = place("probs_turned", [P, 2, 3 * P])
    QKT, _ = place("qk_turned", [DH, 2, 2 * S])
    KIT, _ = place("idx_keys_turned", [DH, S])
    IDX, _ = place("idx_scores", [P, 3 * P])
    MB, _ = place("bias_masks", [P, HB, S])
    CM, cm_at = place("forget_masks", [P, HC, 3 * P])
    LB, _ = place("logf_wide", [P, NT, P])
    n_const = cat["eps"][1]
    CON, _ = place("constants", [P, n_const])
    DILM, _ = place("dilated_masks", [P, 3, S], at=cm_at)
    SMALL, _ = place("small", [P, 420])
    SQ = SM[:, :, :].rearrange("p a b -> p (a b)")[:, 0:NT * CW].rearrange("p (t n) -> p t n", t=NT)
    POS, _ = place("positions_int", [P, NT], I32)
    RB, _ = place("rel_rows", [DEPTH * HB, 2 * REL + 1], at=cm_at)
    RE, _ = place("rel_extended", [DEPTH * HB, 3 * P], at=cm_at + 2048)
    assert max(top) <= nc.sbuf_usable_end, (max(top), nc.sbuf_usable_end)
    scratch = nc.dram_tensor("rel_scratch", [DEPTH * HB, 3 * P], F32)

    def con(name):
        a, b = cat[name]
        return CON[:, a:b]

    used = [0]

    def small(n):
        used[0] += n
        assert used[0] <= 420
        return SMALL[:, used[0] - n:used[0]]

    COND, CT = small(KT), small(KT)
    POSF, ANG, KR, RED, COS, SIN = (small(NT), *(small(NT * 8) for _ in range(5)))
    MAX8 = small(16)
    ZN, ZA, ZE, ZU, ZL, ZD, LF, F8 = (small(NT * HC) for _ in range(8))
    MX, NM, RS, RR = (small(48) for _ in range(4))
    STAT = small(24)
    MV, RSTD, NMR = small(4), small(2), small(2)

    BANK = [ctx.enter_context(nc.psum_tensor(f"bank{i}", [P, CW], F32)) for i in range(8)]
    SB_ = (4, 5)
    TQ, TP = 6, 7

    ONE = dict(score=1, turn=3, weigh=4, qk=QKT, pt=PT, n_pt=2, n_qk=2, tq=(TQ,), tp=(TP,))
    TWO = dict(score=2, turn=4, weigh=6, qk=QKT2, pt=PT2, n_pt=3, n_qk=3, tq=(TQ, 2), tp=(TP, 3, 1))
    N_SM = 3
    GATE_STEP = 2

    def sem(name):
        return ctx.enter_context(nc.semaphore(name))

    def signal(name):
        return Signal(sem(name), name, book)

    raw_in = [sem(f"raw_in{i}") for i in range(NR)]
    vec_in = [sem(f"vec_in{i}") for i in range(NV)]
    x_in, c_in, pos_in, const_in, rel_in = (sem(n) for n in ("x_in", "c_in", "pos_in", "const_in", "rel_in"))
    scratch_in, dil_in, out_in = sem("scratch_in"), sem("dil_in"), sem("out_in")
    bias_in = [sem(f"bias_in{h}") for h in range(HB)]
    hi_ready = signal("hi_ready")
    lo_ready = signal("lo_ready")
    unit_used = signal("unit_used")
    ada_used = signal("ada_used")
    vec_used = signal("vec_used")
    product = signal("product")
    drained = signal("drained")
    turned = signal("turned")
    turned_hi = signal("turned_hi")
    turned_lo = signal("turned_lo")
    rows = signal("rows")
    act_side = signal("act_side")
    qk_in_psum = signal("qk_in_psum")
    qk_turned = signal("qk_turned")
    scored = signal("scored")
    masked = signal("masked")
    exped = signal("exped")
    p_in_psum = signal("p_in_psum")
    p_turned = signal("p_turned")
    headed = signal("headed")
    head_out = signal("head_out")
    forget = signal("forget")
    chain = signal("chain")
    act_chain = signal("act_chain")

    def tile_rows(src):
        name, *ix = src
        a = dram[name]
        return a[ix[0]] if ix else (a[0] if len(a.shape) == 3 else a)

    def raw_ready(e, u):
        e.wait_ge(raw_in[u["slot"]], 16 * (u["turn"] + 1))

    def vec_ready(e, name):
        v = vec_of[name]
        e.wait_ge(vec_in[v["index"] % NV], 16 * (v["index"] // NV + 1))
        return VEC[:, v["index"] % NV, 0:v["ncols"]]

    vectors = [i for i in stream if i["kind"] == "vec"]

    def freed_by(vec):
        what, *ix = vec["name"]
        if what in ("ada_b", "b_in", "b_gate"):
            return drained, ({"ada_b": "ada", "b_in": "proj", "b_gate": "gate"}[what], *ix)
        return vec_used, vec["name"]

    block = ctx.enter_context(nc.Block())

    @block.sync
    def _(sp):
        sp.dma_start(COND, dram["c"].rearrange("b (p k) -> (b p) k", p=P)).then_inc(c_in, 16)
        sp.dma_start(CON[:, :], dram["constants"][:, 0:n_const]).then_inc(const_in, 16)
        ada_seen = 0
        for item in stream:
            if item["kind"] == "vec":
                n = item["index"]
                if n >= NV:
                    signal_, event = freed_by(vectors[n - NV])
                    sp.wait_ge(signal_.sem, signal_.at(event))
                (name, *ix), col0, ncols = item["src"]
                a = dram[name]
                row = (a[ix[0]:ix[0] + 1, :] if ix else a.rearrange("(a n) -> a n", a=1))[:, col0:col0 + ncols]
                sp.dma_start(VEC[:, n % NV, 0:ncols], row.to_broadcast([P, ncols])).then_inc(vec_in[n % NV], 16)
                continue
            old = item["evicts"]
            if old is not None and old["kind"] == "w":
                sp.wait_ge(lo_ready.sem, lo_ready.at(old["index"]))
            elif old is not None:
                sp.wait_ge(ada_used.sem, ada_used.at(old["index"]))
            if item["kind"] == "ada":
                l, c, i = item["l"], item["c"], item["i"]
                ada_seen += 1
                if ada_seen == KT:
                    sp.dma_start(X[:, :, :], dram["x"][0].rearrange("(t p) d -> p t d", p=P)).then_inc(x_in, 16)
                src = dram["ada_w"][l].rearrange("(p k) n -> p k n", p=P)[:, i * UNIT_K:(i + 1) * UNIT_K, c * CW:(c + 1) * CW]
                sp.dma_start(RAW[:, item["slot"], :, :], src).then_inc(raw_in[item["slot"]], 16)
            else:
                src, row0, n, col0, ncols = item["src"]
                a = tile_rows(src)[row0:row0 + n * P, col0:col0 + ncols].rearrange("(k p) n -> p k n", p=P)
                key = item["index"]
                if key == dil_at:
                    sp.wait_ge(masked.sem, masked.at((DEPTH - 1, HI + HB + HC - 1)))
                    a0, b0 = cat["dil0"][0], cat["dil2"][1]
                    sp.dma_start(DILM[:, :, :], dram["constants"][:, a0:b0].rearrange("p (g k) -> p g k", g=3)).then_inc(dil_in, 16)
                sp.dma_start(RAW[:, item["slot"], 0:n, 0:ncols], a).then_inc(raw_in[item["slot"]], 16)
        for t in range(NT):
            sp.wait_ge(vec_used.sem, vec_used.at(("ln_mlp_b", 1, 1)))
            sp.dma_start(out[0, t * P:(t + 1) * P, :], X[:, t, :]).then_inc(out_in, 16)
        sp.wait_ge(out_in, 16 * NT)

    @block.gpsimd
    def _(pool):
        for u in (i for i in ring if i["kind"] == "w"):
            s, n, w = u["index"] % NH, u["n"], u["ncols"]
            pool.wait_ge(hi_ready.sem, hi_ready.at(u["index"]))
            pool.tensor_tensor(LO[:, s, 0:n, 0:w], RAW[:, u["slot"], 0:n, 0:w], HI_[:, s, 0:n, 0:w].bitcast(F32),
                               ALU.subtract).then_inc(lo_ready.sem, lo_ready.mark(u["index"]))

    @block.tensor
    def _(pe):
        todo = [c for c in chunks]

        def pair_free(c):
            if c["before"][0] == "mi":
                pe.wait_ge(act_side.sem, act_side.at(("relu", *c["before"][1:])))
            else:
                pe.wait_ge(drained.sem, drained.at(c["before"]))

        def unit(c, i, A):
            u = c["units"][i]
            if i == 0 and c["before"] is not None:
                pair_free(c)
            pe.wait_ge(lo_ready.sem, lo_ready.at(u["index"]))
            s, w = u["index"] % NH, u["ncols"]
            nt = [(a, b) for tile in u["tiles"] for a, b in tile]
            for t in range(NT):
                for m, (a, b) in enumerate(nt):
                    xs = A[:, a, :, t * P:(t + 1) * P]
                    passes = ((0, HI_), (0, LO), (1, HI_))
                    for q, (part, W) in enumerate(passes):
                        ins = pe.matmul(BANK[2 * c["pair"] + t][:, 0:w], xs[:, part, :], W[:, s, b, 0:w],
                                        start=(i == 0 and m == 0 and q == 0),
                                        stop=(i == len(c["units"]) - 1 and m == len(nt) - 1 and q == 2))
            ins.then_inc(unit_used.sem, unit_used.mark(u["index"]))

        def ada_sum(c):
            _, l, n = c["key"]
            if c["before"] is not None:
                pair_free(c)
            pe.wait_ge(ada_used.sem, ada_used.at(c["units"][-1]["index"]))
            pe.matmul(BANK[SB_[n % 2]][:, :], con("ones"), MOD[:, n * CW:(n + 1) * CW],
                      start=True, stop=True).then_inc(product.sem, product.mark(c["key"]))

        def gemms(A, n=None, until=None):
            while todo and (todo[0]["key"][0] in until or todo[0]["kind"] == "ada"):
                c = todo.pop(0)
                if c["kind"] == "ada":
                    ada_sum(c)
                else:
                    for i in range(len(c["units"])):
                        unit(c, i, A)

        def turn(tag, src, groups, n, ready, ntiles=KT):
            g = groups[n]
            if n >= 2:
                pe.wait_ge(turned_lo.sem, turned_lo.at((tag, groups[n - 2])))
            signal_, event = ready(g)
            pe.wait_ge(signal_.sem, signal_.at(event))
            for t in range(NT):
                for j in range(min(2, ntiles - 2 * g)):
                    ins = pe.transpose(BANK[(TQ, TP)[n % 2]][:, (j * NT + t) * P:(j * NT + t + 1) * P],
                                       src[:, t, (2 * g + j) * P:(2 * g + j + 1) * P], con("ident"))
            ins.then_inc(turned.sem, turned.mark((tag, g)))

        def sums():
            while todo and todo[0]["kind"] == "ada":
                ada_sum(todo.pop(0))

        def turn_and_start(tag, src, ready, A, ntiles=KT, turned_before=0, between=None):
            n_groups = -(-ntiles // 2)
            c = todo.pop(0)
            for n in range(n_groups + 1):
                if between and n == 2:
                    ada_sum(between)
                if turned_before <= n < n_groups:
                    turn(tag, src, range(n_groups), n, ready, ntiles)
                if n:
                    pe.wait_ge(turned_lo.sem, turned_lo.at((tag, n - 1)))
                    unit(c, n - 1, A)

        def wide(tag, n, name):
            c = todo.pop(0)
            last = n - 1
            width = (FFN - last * CW if name == "ffo" else CW) // P
            for i in range(len(c["units"])):
                if i == 2 * last - 2:
                    turn_ffn(pe, turned, turned_lo, rows, drained, tag, last, width, BANK, TQ, TP, O, con)
                pe.wait_ge(turned_lo.sem, turned_lo.at((tag, i // 2, 1)))
                unit(c, i, AT)
            gemms(AT, until=(name,))

        def attention(tag, heads, src, weave, pipe):
            real = lambda h: 0 <= h < len(heads) and heads[h]["kind"] != "I"
            for k in range(len(heads) + pipe["weigh"]):
                h = k - pipe["score"]
                if 0 <= h < len(heads):
                    hd = heads[h]
                    pe.wait_ge(qk_turned.sem, qk_turned.at((tag, h)))
                    if h >= 2:
                        by = exped if heads[h - 2]["kind"] == "I" else masked
                        pe.wait_ge(by.sem, by.at((tag, h - 2)))
                    bank = BANK[SB_[h % 2]]
                    slot = h % pipe["n_qk"]
                    q = pipe["qk"][:, slot, 0:S]
                    kk = KIT[:, :] if hd["kind"] == "I" else pipe["qk"][:, slot, S:2 * S]
                    pe.matmul(bank[:, 0:S], q[:, P:S], kk, start=True, stop=True)
                    pe.matmul(bank[:, S:S + P], q[:, 0:P], kk[:, 0:P], start=True, stop=True)\
                        .then_inc(scored.sem, scored.mark((tag, h)))
                if k < len(heads):
                    hd = heads[k]
                    n_tq = len(pipe["tq"])
                    if k >= n_tq:
                        pe.wait_ge(qk_turned.sem, qk_turned.at((tag, k - n_tq)))
                    with_k = hd["kind"] != "I" or hd["h"] == 0
                    for col, at in ((hd["q"], 0), (hd["k"], S))[:2 if with_k else 1]:
                        for t in range(NT):
                            ins = pe.transpose(BANK[pipe["tq"][k % n_tq]][0:DH, at + t * P:at + (t + 1) * P],
                                               src[:, t, col:col + DH], con("ident"))
                    ins.then_inc(qk_in_psum.sem, qk_in_psum.mark((tag, k)))
                n_tp = len(pipe["tp"])
                h = k - pipe["weigh"]
                if real(h):
                    bank = BANK[pipe["tp"][h % n_tp]]
                    pe.wait_ge(p_turned.sem, p_turned.at((tag, h)))
                    v = heads[h]["v"]
                    pt = pipe["pt"][:, h % pipe["n_pt"], :]
                    pe.matmul(bank[:, 384:448], pt[:, 0:P], src[:, 0, v:v + DH], start=True, stop=True)
                    pe.matmul(bank[:, 448:512], pt[:, P:2 * P], src[:, 0, v:v + DH], start=True, stop=False)
                    pe.matmul(bank[:, 448:512], pt[:, 2 * P:3 * P], src[:, 1, v:v + DH], start=False, stop=True)\
                        .then_inc(headed.sem, headed.mark((tag, h)))
                weave(k)
                h = k - pipe["turn"]
                if real(h):
                    pe.wait_ge(exped.sem, exped.at((tag, h)))
                    if real(h - n_tp):
                        pe.wait_ge(head_out.sem, head_out.at((tag, h - n_tp)))
                    bank = BANK[pipe["tp"][h % n_tp]]
                    for at, cols in ((0, slice(S, S + P)), (P, slice(0, P)), (2 * P, slice(P, S))):
                        ins = pe.transpose(bank[:, at:at + P], SM[:, h % N_SM, cols], con("ident"))
                    ins.then_inc(p_in_psum.sem, p_in_psum.mark((tag, h)))

        pe.wait_ge(const_in, 16)
        for c in range(3):
            ada_sum(todo.pop(0))
        for l in range(DEPTH):
            turn_and_start(("n1", l), O, lambda g: (rows, ("h", ("n1", l), g // 2)), HT, between=todo.pop(0) if l == 0 else None)
            gemms(HT, until=("proj",))
            heads = heads_one()
            pe.wait_ge(drained.sem, drained.at(("proj", l, N_PROJ - 1)))

            def weave(k, l=l):
                if k >= 1 and 2 <= k < 2 + HC + 1:
                    forget_products(l, k - 2)
                if k >= GATE_STEP and todo[0]["key"][0:2] == ("gate", l):
                    c = todo[0]
                    unit(c, (k - GATE_STEP) % 4, HT)
                    if (k - GATE_STEP) % 4 == 3:
                        todo.pop(0)

            def forget_products(l, c):
                if c == 0:
                    pe.wait_ge(rows.sem, rows.at(("logf", l)))
                    lf = LF.rearrange("p (t h) -> p t h", t=NT)
                    pe.matmul(BANK[TP][:, 0:HC], con("tri0")[:, 0:P], lf[:, 0, :], start=True, stop=True)
                    pe.matmul(BANK[TP][:, HC:2 * HC], con("tri0")[:, P:S], lf[:, 0, :], start=True, stop=False)
                    pe.matmul(BANK[TP][:, HC:2 * HC], con("tri1")[:, P:S], lf[:, 1, :], start=False, stop=True)\
                        .then_inc(forget.sem, forget.mark((l, "cols")))
                    return
                pe.wait_ge(rows.sem, rows.at(("logf_wide", l, c - 1)))
                pe.matmul(BANK[TP][:, 0:S], LB[:, 0, :], con("tri0"), start=True, stop=False)
                pe.matmul(BANK[TP][:, 0:S], LB[:, 1, :], con("tri1"), start=False, stop=True)\
                    .then_inc(forget.sem, forget.mark((l, c - 1)))

            attention(l, heads, PROJ, weave, ONE)

            def branch(cc, b):
                assert todo[0]["key"] == ("branch", l, cc, b)
                c = todo.pop(0)
                for i in range(len(c["units"])):
                    unit(c, i, HT)

            tag, order = ("o", l), (3, 2, 1, 0)
            kinds = {3: HI + HB + HC - 1, 2: len(heads) - 1, 1: len(heads) - 1, 0: len(heads) - 1}
            ready = lambda g: (head_out, (l, kinds[g]))
            turn(tag, O, order, 0, ready)
            turn(tag, O, order, 1, ready)
            turn(tag, O, order, 2, ready)
            pe.wait_ge(rows.sem, rows.at(("halves", l)))
            branch(0, "C")
            turn(tag, O, order, 3, ready)
            pe.wait_ge(turned_lo.sem, turned_lo.at((tag, 1)))
            branch(0, "B")
            pe.wait_ge(turned_lo.sem, turned_lo.at((tag, 0)))
            branch(0, "A")
            branch(1, "C")
            ready = lambda g: (rows, ("y", l, g // 2))
            turn(("y", l), O, range(4), 0, ready)
            turn(("y", l), O, range(4), 1, ready)
            branch(1, "B")
            branch(1, "A")
            turn_and_start(("y", l), O, ready, AT, turned_before=2)
            gemms(AT, until=("wout",))
            turn_and_start(("n2", l), O, lambda g: (rows, ("h", ("n2", l), g // 2)), HT)
            n_ff = -(-FFN // CW)
            for j in range(n_ff):
                if j < n_ff:
                    for what in ("ffg", "ffu"):
                        if (what, j) != ("ffg", 0):
                            c = todo.pop(0)
                            assert c["key"] == (what, l, j)
                            for i in range(len(c["units"])):
                                unit(c, i, HT)
                        sums()
                        if what == "ffg" and j:
                            turn_ffn(pe, turned, turned_lo, rows, drained, ("a", l), j - 1, min(CW, FFN - (j - 1) * CW) // P, BANK, TQ, TP, O, con)
            wide(("a", l), n_ff, "ffo")
        for i in range(2):
            heads = heads_two(i)
            start = (lambda g: (vec_used, ("final_g", g // 2))) if i == 0 else (lambda g: (vec_used, ("ln_mlp_b", 0, g // 2)))
            turn_and_start(("x", i), X, start, HT)
            gemms(HT, until=("qkv",))
            pe.wait_ge(drained.sem, drained.at(("qkv", i, -(-3 * len(heads) * DH // CW) - 1)))
            attention(("two", i), heads, QKV, lambda k: None, TWO)
            turn_and_start(("o2", i), O, lambda g: (rows, "weighted") if i else (head_out, (("two", 0), len(heads) - 1 if g else 3)),
                           HT, len(heads) * DH // P)
            gemms(HT, until=("wo",))
            turn_and_start(("m", i), X, lambda g: (vec_used, ("ln_mix_b", i, g // 2)), HT)
            for j in range(DFF // CW):
                if j:
                    c = todo.pop(0)
                    for u in range(len(c["units"])):
                        unit(c, u, HT)
                    turn_ffn(pe, turned, turned_lo, rows, drained, ("a2", i), j - 1, CW // P, BANK, TQ, TP, O, con)
            wide(("a2", i), DFF // CW, "mo")
        assert not todo

    last_unit = {c["key"]: c["units"][-1]["index"] for c in chunks if c["kind"] == "gemm"}

    def product_ready(e, key):
        c = by_key[key]
        if c["kind"] == "ada":
            e.wait_ge(product.sem, product.at(key))
            return [BANK[SB_[key[2] % 2]]]
        e.wait_ge(unit_used.sem, unit_used.at(last_unit[key]))
        return [BANK[2 * c["pair"] + t] for t in range(NT)]

    @block.scalar
    def _(act):
        w_units = [i for i in ring if i["kind"] == "w"]
        done = [0]

        def prep(upto):
            while done[0] < min(upto, len(w_units)):
                u = w_units[done[0]]
                s, n, w = u["index"] % NH, u["n"], u["ncols"]
                raw_ready(act, u)
                if u["index"] >= NH:
                    act.wait_ge(unit_used.sem, unit_used.at(u["index"] - NH))
                act.activation(HI_[:, s, 0:n, 0:w], RAW[:, u["slot"], 0:n, 0:w], ACT.Copy)\
                    .then_inc(hi_ready.sem, hi_ready.mark(u["index"]))
                done[0] += 1

        def prep_chunk(key, ahead=NH):
            prep(last_unit[key] + 1 + ahead)

        def turn_hi(tag, A, ntiles=KT, order=None, part=slice(None)):
            for m, g in list(enumerate(order or range(-(-ntiles // 2))))[part]:
                n = min(2, ntiles - 2 * g)
                act.wait_ge(turned.sem, turned.at((tag, g)))
                act.activation(A[:, 2 * g:2 * g + n, 0, :], BANK[(TQ, TP)[m % 2]][:, 0:n * S].rearrange("p (k s) -> p k s", k=n),
                               ACT.Copy).then_inc(turned_hi.sem, turned_hi.mark((tag, g)))

        def turn_hi_ffn(tag, j, n):
            for t in range(NT):
                act.wait_ge(turned.sem, turned.at((tag, j, t)))
                act.activation(AT[:, 4 * j:4 * j + n, 0, t * P:(t + 1) * P], BANK[(TQ, TP)[t]][:, 0:n * P].rearrange("p (k s) -> p k s", k=n),
                               ACT.Copy).then_inc(turned_hi.sem, turned_hi.mark((tag, j, t)))

        def squares(tag, half, event):
            signal_, name = event
            act.wait_ge(signal_.sem, signal_.at(name))
            if half:
                act.wait_ge(act_side.sem, act_side.at(("squares", tag, 0)))
            for t in range(NT):
                ins = act.activation(SQ[:, t, :], X[:, t, half * CW:(half + 1) * CW], ACT.Square,
                                     accum_out=STAT[:, 2 * half + t:2 * half + t + 1])
            ins.then_inc(act_side.sem, act_side.mark(("squares", tag, half)))

        def root(tag, eps, scale, src):
            act.activation(NMR[:, 0:1], con("eps")[:, 0:1], ACT.Sqrt).then_inc(act_chain.sem, act_chain.mark(("table", tag)))
            act.wait_ge(rows.sem, rows.at(("var", tag)))
            act.activation(RSTD, src, ACT.Sqrt, scale=scale, bias=con("eps")[:, eps:eps + 1])\
                .then_inc(act_side.sem, act_side.mark(("root", tag)))

        def rms_root(tag):
            root(tag, 0, 1.0 / D, STAT[:, 0:NT])

        def attention(tag, heads, weave, pipe):
            for k in range(len(heads) + pipe["score"]):
                weave(k)
                if k < len(heads):
                    hd = heads[k]
                    bank = BANK[pipe["tq"][k % len(pipe["tq"])]]
                    slot = pipe["qk"][:, k % pipe["n_qk"], :]
                    act.wait_ge(qk_in_psum.sem, qk_in_psum.at((tag, k)))
                    if k >= pipe["n_qk"]:
                        act.wait_ge(scored.sem, scored.at((tag, k - pipe["n_qk"])))
                    if hd["kind"] == "I":
                        if hd["h"] == 0:
                            act.activation(KIT[:, :], bank[0:DH, S:2 * S], ACT.Copy)\
                                .then_inc(act_chain.sem, act_chain.mark(("kit", tag)))
                        act.activation(slot[:, 0:S], bank[0:DH, 0:S], ACT.Copy)\
                            .then_inc(qk_turned.sem, qk_turned.mark((tag, k)))
                    else:
                        act.activation(slot, bank[0:DH, :], ACT.Copy)\
                            .then_inc(qk_turned.sem, qk_turned.mark((tag, k)))
                h = k - pipe["score"]
                if h >= 0 and heads[h]["kind"] == "I":
                    act.wait_ge(scored.sem, scored.at((tag, h)))
                    if h >= N_SM:
                        act.wait_ge(masked.sem, masked.at((tag, h - N_SM)))
                    act.activation(SM[:, h % N_SM, :], BANK[SB_[h % 2]][:, 0:3 * P], ACT.Relu)\
                        .then_inc(exped.sem, exped.mark((tag, h)))
                elif h >= 0:
                    act.wait_ge(masked.sem, masked.at((tag, h)))
                    m = 2 * h
                    act.activation(SM[:, h % N_SM, S:S + P], SM[:, h % N_SM, S:S + P], ACT.Exp, bias=NM[:, m:m + 1],
                                   accum_out=RS[:, m:m + 1])
                    act.activation(SM[:, h % N_SM, 0:S], SM[:, h % N_SM, 0:S], ACT.Exp, bias=NM[:, m + 1:m + 2],
                                   accum_out=RS[:, m + 1:m + 2]).then_inc(exped.sem, exped.mark((tag, h)))

        def bias_rows(l):
            for h in range(HB):
                rel = bass.AP(scratch, (l * HB + h) * 3 * P, [[1, P], [1, S]])
                act.dma_start(MB[:, h, :], rel).then_inc(bias_in[h], 16)

        act.dma_start(RB[:, :], dram["rel_bias"].rearrange("l h r -> (l h) r")).then_inc(rel_in, 16)
        act.dma_start(POS[:, :], dram["positions"].rearrange("b (t p) -> (b p) t", p=P),
                      allow_slow_non_contiguous=True).then_inc(pos_in, 16)
        act.wait_ge(c_in, 16)
        act.activation(CT, COND, ACT.Tanh, scale=0.5).then_inc(act_side.sem, act_side.mark("cond"))
        for what, dst in (("sin", SIN), ("cos", COS)):
            act.wait_ge(rows.sem, rows.at(what))
            act.activation(dst, dst, ACT.Sin).then_inc(act_side.sem, act_side.mark(what))
        act.wait_ge(rows.sem, rows.at("rel"))
        act.dma_start(scratch[:, :], RE[:, :]).then_inc(scratch_in, 16)
        act.wait_ge(x_in, 16)
        for half in range(2):
            squares(("n1", 0), half, (act_side, "cond"))
        prep(2)
        for l in range(DEPTH):
            rms_root(("n1", l))
            turn_hi(("n1", l), HT, part=slice(0, 2))
            if l == 0:
                prep(3)
            turn_hi(("n1", l), HT, part=slice(2, 4))
            if l == 0:
                prep(NH)
                act.wait_ge(scratch_in, 16)
                bias_rows(0)
            for j in range(N_PROJ):
                prep_chunk(("proj", l, j))
            act.wait_ge(rows.sem, rows.at(("nabs", l)))
            act.activation(ZE, ZA, ACT.Exp).then_inc(act_side.sem, act_side.mark(("ze", l)))
            act.wait_ge(rows.sem, rows.at(("zu", l)))
            act.activation(ZL, ZU, ACT.Ln).then_inc(act_side.sem, act_side.mark(("zl", l)))
            first = by_key[("gate", l, 0)]["units"][0]["index"]

            def gate_tanh(j, l=l):
                act.wait_ge(drained.sem, drained.at(("gate", l, j)))
                act.activation(GATES[:, :, j * CW:(j + 1) * CW], GATES[:, :, j * CW:(j + 1) * CW], ACT.Tanh, scale=0.5)\
                    .then_inc(act_side.sem, act_side.mark(("gate", l, j)))

            def weave(k, l=l):
                prep(first + min(max(k - GATE_STEP, 0) + 1, 4 * N_GATE) + 3)
                if k >= 6 + GATE_STEP and (k - 6 - GATE_STEP) % 4 == 0:
                    gate_tanh((k - 6 - GATE_STEP) // 4)

            attention(l, heads_one(), weave, ONE)
            prep_chunk(("gate", l, N_GATE - 1))
            if (len(heads_one()) + ONE["score"] - 1 - 6 - GATE_STEP) // 4 < N_GATE - 1:
                gate_tanh(N_GATE - 1)
            if l + 1 < DEPTH:
                act.wait_ge(masked.sem, masked.at((l, HI + HB - 1)))
                bias_rows(l + 1)
            turn_hi(("o", l), HT, order=(3, 2, 1, 0))
            for cc in range(2):
                for b in "CBA":
                    prep_chunk(("branch", l, cc, b), 3)
                    if (cc, b) == (1, "C"):
                        turn_hi(("y", l), AT, part=slice(0, 2))
            turn_hi(("y", l), AT, part=slice(2, 4))
            for cc in range(2):
                prep_chunk(("wout", l, cc))
                squares(("n2", l), cc, (rows, ("x", ("mid1", l), cc)))
            rms_root(("n2", l))
            turn_hi(("n2", l), HT)
            n_ff = -(-FFN // CW)
            for j in range(n_ff):
                n = min(CW, FFN - j * CW)
                prep_chunk(("ffg", l, j))
                banks = product_ready(act, ("ffg", l, j))
                for t in range(NT):
                    if j >= 2:
                        act.wait_ge(drained.sem, drained.at(("ffu", l, j - 2)))
                    ins = act.activation(TG[:, j % 2, t, 0:n], banks[t][:, 0:n], ACT.Tanh, scale=0.5)
                ins.then_inc(act_side.sem, act_side.mark(("tg", l, j)))
                if j:
                    turn_hi_ffn(("a", l), j - 1, CW // P)
                prep_chunk(("ffu", l, j))
            first = by_key[("ffo", l, 0)]["units"][0]["index"]
            prep(first + 2 * n_ff - 4 + NH)
            turn_hi_ffn(("a", l), n_ff - 1, (FFN - (n_ff - 1) * CW) // P)
            following = ("n1", l + 1) if l + 1 < DEPTH else "final"
            for cc in range(2):
                prep_chunk(("ffo", l, cc))
                squares(following, cc, (rows, ("x", ("end", l), cc)))
        rms_root("final")

        def ln_root(tag):
            root(tag, 1, 1.0, MV.rearrange("p (t m) -> p t m", t=NT)[:, :, 1])

        for i in range(2):
            heads = heads_two(i)
            turn_hi(("x", i), HT)
            for j in range(-(-3 * len(heads) * DH // CW)):
                prep_chunk(("qkv", i, j))
            attention(("two", i), heads, lambda k: None, TWO)
            if i == 1:
                act.wait_ge(rows.sem, rows.at("group_max"))
                act.activation(NM[:, 0:3 * 4 * NT], MX[:, 0:3 * 4 * NT], ACT.Exp)\
                    .then_inc(act_side.sem, act_side.mark("group_exp"))
            turn_hi(("o2", i), HT, len(heads) * DH // P)
            for cc in range(2):
                prep_chunk(("wo", i, cc))
            ln_root(("mid", i))
            turn_hi(("m", i), HT)
            for j in range(DFF // CW):
                prep_chunk(("mi", i, j))
                banks = product_ready(act, ("mi", i, j))
                if j >= 2:
                    act.wait_ge(rows.sem, rows.at(("a2", i, j - 2)))
                for t in range(NT):
                    ins = act.activation(RT[:, j % 2, t, :], banks[t][:, :], ACT.Relu)
                ins.then_inc(act_side.sem, act_side.mark(("relu", i, j)))
                if j:
                    turn_hi_ffn(("a2", i), j - 1, CW // P)
            first = by_key[("mo", i, 0)]["units"][0]["index"]
            prep(first + 2 * (DFF // CW) - 4 + NH)
            turn_hi_ffn(("a2", i), DFF // CW - 1, CW // P)
            for cc in range(2):
                prep_chunk(("mo", i, cc))
            ln_root(("end2", i))

    @block.vector
    def _(dve):
        v = nc.vector
        step = [0]

        def link(ins):
            step[0] += 1
            ins.then_inc(chain.sem, chain.mark(step[0]))
            dve.wait_ge(chain.sem, step[0])

        def tell(ins, signal_, event):
            ins.then_inc(signal_.sem, signal_.mark(event))
            dve.wait_ge(signal_.sem, signal_.at(event))

        def say(ins, event):
            tell(ins, rows, event)

        pos_in_stream = {}
        for n, i in enumerate(ring):
            if i["kind"] == "w":
                pos_in_stream[i["index"]] = n
        ada_units = [(n, i) for n, i in enumerate(ring) if i["kind"] == "ada"]
        ada_done = [0]
        ada_pending = []

        def ada_upto(n):
            while ada_done[0] < len(ada_units) and ada_units[ada_done[0]][0] < n:
                _, u = ada_units[ada_done[0]]
                ada_done[0] += 1
                cols = slice(u["c"] * CW, (u["c"] + 1) * CW)
                raw_ready(dve, u)
                for k in range(UNIT_K):
                    kt = u["i"] * UNIT_K + k
                    if kt == 0:
                        link(v.tensor_scalar(MOD[:, cols], RAW[:, u["slot"], k, :], COND[:, kt:kt + 1], None, ALU.mult))
                        continue
                    ins = v.scalar_tensor_tensor(MOD[:, cols], RAW[:, u["slot"], k, :], COND[:, kt:kt + 1], MOD[:, cols], ALU.mult, ALU.add)
                    if k < UNIT_K - 1:
                        link(ins)
                tell(ins, ada_used, u["index"])

        def ada_drain(key):
            _, l, c = key
            cols = slice(c * CW, (c + 1) * CW)
            b = vec_ready(dve, ("ada_b", l, c))
            bank = product_ready(dve, key)[0]
            tell(v.tensor_tensor(MOD[:, cols], bank[:, :], b, ALU.add), drained, key)
            name = {2: "norm1_g", 3: "norm1_g", 8: "norm2_g", 9: "norm2_g"}.get(c)
            if name:
                name = (name, l, c - 2 if c < 6 else c - 8)
                g = vec_ready(dve, name)
                tell(v.scalar_tensor_tensor(MOD[:, cols], MOD[:, cols], 1.0, g, ALU.add, ALU.mult), vec_used, name)

        order = [c["key"] for c in chunks]

        def before(key):
            i = order.index(key)
            nxt = next((c for c in chunks[i + 1:] if c["kind"] == "gemm"), None)
            if nxt is not None:
                ada_upto(pos_in_stream[nxt["units"][-1]["index"]])

        def after(key):
            i = order.index(key) + 1
            while i < len(order) and order[i][0] == "ada":
                ada_upto(1 + max(n for n, u in ada_units if (u["l"], u["c"]) == order[i][1:]))
                ada_drain(order[i])
                i += 1

        def turn_lo(tag, A, ntiles=KT, order=None, part=slice(None)):
            for m, g in list(enumerate(order or range(-(-ntiles // 2))))[part]:
                n = min(2, ntiles - 2 * g)
                dve.wait_ge(turned_hi.sem, turned_hi.at((tag, g)))
                tell(v.tensor_tensor(A[:, 2 * g:2 * g + n, 1, :], BANK[(TQ, TP)[m % 2]][:, 0:n * S].rearrange("p (k s) -> p k s", k=n),
                                A[:, 2 * g:2 * g + n, 0, :].bitcast(F32), ALU.subtract),
                    turned_lo, (tag, g))

        def turn_lo_ffn(tag, j, n):
            for t in range(NT):
                dve.wait_ge(turned_hi.sem, turned_hi.at((tag, j, t)))
                tell(v.tensor_tensor(AT[:, 4 * j:4 * j + n, 1, t * P:(t + 1) * P], BANK[(TQ, TP)[t]][:, 0:n * P].rearrange("p (k s) -> p k s", k=n),
                                AT[:, 4 * j:4 * j + n, 0, t * P:(t + 1) * P].bitcast(F32), ALU.subtract),
                    turned_lo, (tag, j, t))

        def scaled(half, coef):
            for t in range(NT):
                cols = slice(half * CW, (half + 1) * CW)
                ins = v.tensor_tensor(O[:, t, cols], X[:, t, cols], MOD[:, coef + half * CW:coef + (half + 1) * CW], ALU.mult)
            link(ins)

        def root_of_squares(tag):
            for half in range(2):
                dve.wait_ge(act_side.sem, act_side.at(("squares", tag, half)))
            say(v.tensor_tensor(STAT[:, 0:NT], STAT[:, 0:NT], STAT[:, 2:2 + NT], ALU.add), ("var", tag))
            dve.wait_ge(act_side.sem, act_side.at(("root", tag)))
            link(v.reciprocal(RR[:, 0:NT], RSTD))

        def h_rows(tag, shift, halves=range(2)):
            for half in halves:
                for t in range(NT):
                    cols = slice(half * CW, (half + 1) * CW)
                    ins = v.scalar_tensor_tensor(O[:, t, cols], O[:, t, cols], RR[:, t:t + 1],
                                                 MOD[:, shift + half * CW:shift + (half + 1) * CW], ALU.mult, ALU.add)
                say(ins, ("h", tag, half))

        def attention(tag, heads, mask_of, weave, pipe, outputs, late=None):
            for k in range(len(heads) + pipe["weigh"]):
                weave(k)
                h = k - pipe["score"]
                if 0 <= h < len(heads):
                    hd = heads[h]
                    if hd["kind"] == "I":
                        dve.wait_ge(exped.sem, exped.at((tag, h)))
                        for t, cols in ((1, slice(0, S)), (0, slice(S, S + P))):
                            acc = IDX[:, cols]
                            if h == 0:
                                prev = con("band")[:, 0:S] if t else con("band")[:, P:S]
                            else:
                                prev = acc
                            ins = v.scalar_tensor_tensor(acc, SM[:, h % N_SM, cols], PROJ[:, t, WI + h:WI + h + 1], prev, ALU.mult, ALU.add)
                        tell(ins, masked, (tag, h))
                    else:
                        dve.wait_ge(scored.sem, scored.at((tag, h)))
                        if h >= N_SM and heads[h - N_SM]["kind"] != "I":
                            dve.wait_ge(p_in_psum.sem, p_in_psum.at((tag, h - N_SM)))
                        m1, m0 = mask_of(hd)
                        m = 2 * h
                        bank = BANK[SB_[h % 2]]
                        v.tensor_tensor_reduce(SM[:, h % N_SM, S:S + P], bank[:, S:S + P], m0, SCALE, PICKED, ALU.add, ALU.max, MX[:, m:m + 1])
                        link(v.tensor_tensor_reduce(SM[:, h % N_SM, 0:S], bank[:, 0:S], m1, SCALE, PICKED, ALU.add, ALU.max, MX[:, m + 1:m + 2]))
                        tell(v.tensor_scalar(NM[:, m:m + 2], MX[:, m:m + 2], -1.0, None, ALU.mult), masked, (tag, h))
                n_tp = len(pipe["tp"])
                h = k - pipe["weigh"]
                if 0 <= h < len(heads) and heads[h]["kind"] != "I":
                    outputs(h, heads[h], BANK[pipe["tp"][h % n_tp]])
                if late:
                    late(k)
                h = k - pipe["turn"]
                if 0 <= h < len(heads) and heads[h]["kind"] != "I":
                    dve.wait_ge(p_in_psum.sem, p_in_psum.at((tag, h)))
                    if h >= pipe["n_pt"] and heads[h - pipe["n_pt"]]["kind"] != "I":
                        dve.wait_ge(headed.sem, headed.at((tag, h - pipe["n_pt"])))
                    tell(v.tensor_copy(pipe["pt"][:, h % pipe["n_pt"], :], BANK[pipe["tp"][h % n_tp]][:, 0:3 * P]), p_turned, (tag, h))

        def scaled_output(tag):
            def put(h, hd, bank):
                m = 2 * h
                dve.wait_ge(exped.sem, exped.at((tag, h)))
                link(v.reciprocal(RR[:, m:m + 2], RS[:, m:m + 2]))
                dve.wait_ge(headed.sem, headed.at((tag, h)))
                tell(v.tensor_tensor(O[:, :, hd["o"]:hd["o"] + DH], bank[:, 384:512].rearrange("p (t d) -> p t d", t=NT),
                                RR[:, m:m + 2].unsqueeze(2).to_broadcast([P, NT, DH]), ALU.mult),
                    head_out, (tag, h))
            return put

        dve.wait_ge(c_in, 16)
        dve.wait_ge(act_side.sem, act_side.at("cond"))
        link(v.scalar_tensor_tensor(COND, CT, 1.0, COND, ALU.add, ALU.mult))
        link(v.tensor_scalar(COND, COND, 0.5, None, ALU.mult))
        dve.wait_ge(rel_in, 16)
        link(v.tensor_copy(RE[:, 0:S], RB[:, 1:S + 1]))
        say(v.tensor_copy(RE[:, S:3 * P], RB[:, 2 * REL:2 * REL + 1].to_broadcast([DEPTH * HB, P])), "rel")
        dve.wait_ge(pos_in, 16)
        dve.wait_ge(const_in, 16)
        link(v.tensor_copy(POSF, POS[:, :]))
        for t in range(NT):
            link(v.tensor_scalar(ANG[:, 8 * t:8 * t + 8], con("inv"), POSF[:, t:t + 1], None, ALU.mult))
        magic = float(1.5 * 2 ** 23)
        two_pi = 2 * np.pi
        c1 = float(np.float32(6.28125))
        c2 = float(np.float32(round((two_pi - c1) * 2 ** 21) / 2 ** 21))
        c3 = float(np.float32(two_pi - c1 - c2))
        link(v.tensor_scalar(KR, ANG, float(1 / two_pi), magic, ALU.mult, ALU.add))
        link(v.tensor_scalar(KR, KR, -magic, None, ALU.add))
        link(v.scalar_tensor_tensor(RED, KR, -c1, ANG, ALU.mult, ALU.add))
        link(v.scalar_tensor_tensor(RED, KR, -c2, RED, ALU.mult, ALU.add))
        link(v.scalar_tensor_tensor(RED, KR, -c3, RED, ALU.mult, ALU.add))
        pi_in = float(np.nextafter(np.float32(np.pi), np.float32(0)))
        say(v.tensor_scalar(SIN, RED, pi_in, -pi_in, ALU.min, ALU.max), "sin")
        link(v.tensor_scalar(KR, RED, float(np.pi / 2), -float(two_pi), ALU.is_gt, ALU.mult))
        link(v.scalar_tensor_tensor(RED, RED, float(np.pi / 2), KR, ALU.add, ALU.add))
        say(v.tensor_scalar(COS, RED, pi_in, -pi_in, ALU.min, ALU.max), "cos")
        v.memset(HT[0:64, KT, :, :].bitcast(F32), 0.0)
        for n, c in enumerate((2, 3, 0)):
            ada_upto(KT // UNIT_K * (n + 1))
            if n:
                ada_drain(("ada", 0, (2, 3, 0)[n - 1]))
                if n == 1:
                    dve.wait_ge(x_in, 16)
                scaled(n - 1, D)
        root_of_squares(("n1", 0))
        ada_drain(("ada", 0, 0))

        for l in range(DEPTH):
            if l == 0:
                h_rows(("n1", l), 0, (0,))
                turn_lo(("n1", l), HT, part=slice(0, 2))
                ada_upto(1 + max(n for n, u in ada_units if (u["l"], u["c"]) == (0, 1)))
                ada_drain(("ada", 0, 1))
                h_rows(("n1", l), 0, (1,))
                turn_lo(("n1", l), HT, part=slice(2, 4))
            else:
                root_of_squares(("n1", l))
                h_rows(("n1", l), 0)
                turn_lo(("n1", l), HT)
            if l == 0:
                dve.wait_ge(act_side.sem, act_side.at("cos"))
            tmp = SM[:, :, :].rearrange("p a b -> p (a b)")

            def rope(col, n, l):
                for t in range(NT):
                    hv = PROJ[:, t, col:col + n * DH].rearrange("p (h d) -> p h d", d=DH)
                    x1, x2 = hv[:, :, 0:8], hv[:, :, 8:16]
                    cs = COS[:, 8 * t:8 * t + 8].unsqueeze(1).to_broadcast([P, n, 8])
                    sn = SIN[:, 8 * t:8 * t + 8].unsqueeze(1).to_broadcast([P, n, 8])
                    a, b, c, d = (tmp[:, 96 * i:96 * i + 8 * n].rearrange("p (h d) -> p h d", d=8) for i in range(4))
                    v.tensor_tensor(a, x1, cs, ALU.mult)
                    v.tensor_tensor(b, x2, sn, ALU.mult)
                    v.tensor_tensor(c, x2, cs, ALU.mult)
                    link(v.tensor_tensor(d, x1, sn, ALU.mult))
                    v.tensor_tensor(x1, a, b, ALU.subtract)
                    link(v.tensor_tensor(x2, c, d, ALU.add))

            for j in range(N_PROJ):
                key = ("proj", l, j)
                n = min(CW, PROJ_W - j * CW)
                before(key)
                b = vec_ready(dve, ("b_in", l, j))
                banks = product_ready(dve, key)
                v.tensor_tensor(PROJ[:, 0, j * CW:j * CW + n], banks[0][:, 0:n], b, ALU.add)
                tell(v.tensor_tensor(PROJ[:, 1, j * CW:j * CW + n], banks[1][:, 0:n], b, ALU.add), drained, key)
                if j == 1:
                    rope(QA, 2 * HA, l)
                if j == 3:
                    rope(QI, HI + 1, l)
                    wi = PROJ[:, :, WI:WI + HI]
                    link(v.tensor_scalar(wi, wi, float(np.float32(HI ** -0.5 * DH ** -0.5)), None, ALU.mult))
                after(key)
            z = PROJ[:, :, FC:FC + HC]
            as2 = lambda a: a.rearrange("p (t h) -> p t h", t=NT)
            link(v.tensor_scalar(as2(ZN), z, -1.0, None, ALU.mult))
            say(v.tensor_tensor(as2(ZA), as2(ZN), z, ALU.min), ("nabs", l))
            dve.wait_ge(act_side.sem, act_side.at(("ze", l)))
            say(v.tensor_scalar(ZU, ZE, 1.0, None, ALU.add), ("zu", l))
            dve.wait_ge(rows.sem, rows.at(("zu", l)))
            link(v.scalar_tensor_tensor(ZD, ZU, -1.0, ZE, ALU.add, ALU.subtract))
            link(v.reciprocal(ZA, ZU))
            link(v.tensor_tensor(ZD, ZD, ZA, ALU.mult))
            dve.wait_ge(act_side.sem, act_side.at(("zl", l)))
            link(v.tensor_tensor(ZL, ZL, ZD, ALU.subtract))
            say(v.scalar_tensor_tensor(LF, ZN, 0.0, ZL, ALU.max, ALU.add), ("logf", l))
            dve.wait_ge(rows.sem, rows.at(("logf", l)))

            def logf_wide(c, l=l):
                for t in range(NT):
                    ins = v.tensor_scalar(LB[:, t, :], con("ones"), LF[:, t * HC + c:t * HC + c + 1], None, ALU.mult)
                say(ins, ("logf_wide", l, c))

            def mask_of(hd, l=l):
                if hd["kind"] == "B":
                    return MB[:, hd["h"], ::-1], MB[:, hd["h"], 0:P][:, ::-1]
                if hd["kind"] == "C":
                    return CM[:, hd["h"], 0:S], CM[:, hd["h"], S:S + P]
                return IDX[:, 0:S], IDX[:, S:S + P]

            first = by_key[("gate", l, 0)]["units"][0]["index"]

            def weave(k, l=l, first=first):
                ada_upto(pos_in_stream[first + min(max(k - GATE_STEP, 0) + 4, 4 * N_GATE - 1)])
                if k == 2:
                    dve.wait_ge(forget.sem, forget.at((l, "cols")))
                    link(v.tensor_copy(F8, BANK[TP][:, 0:2 * HC]))
                    logf_wide(0)
                elif 3 <= k < 3 + HC:
                    c = k - 3
                    dve.wait_ge(forget.sem, forget.at((l, c)))
                    v.scalar_tensor_tensor(CM[:, c, 0:S], BANK[TP][:, 0:S], F8[:, HC + c:HC + c + 1], con("causal"), ALU.subtract, ALU.add)
                    link(v.scalar_tensor_tensor(CM[:, c, S:S + P], BANK[TP][:, 0:P], F8[:, c:c + 1], con("causal")[:, P:S], ALU.subtract, ALU.add))
                    if c + 1 < HC:
                        logf_wide(c + 1)
                if HI - HB <= k < HI:
                    h = k - (HI - HB)
                    dve.wait_ge(bias_in[h], 16 * (l + 1))
                    link(v.scalar_tensor_tensor(MB[:, h, :], MB[:, h, :], 1 / SCALE, con("band")[:, ::-1], ALU.mult, ALU.add))

            def late(k, l=l):
                u = k - GATE_STEP
                if u > 0 and u % 4 == 0:
                    key = ("gate", l, u // 4 - 1)
                    before(key)
                    b = vec_ready(dve, ("b_gate", l, u // 4 - 1))
                    banks = product_ready(dve, key)
                    j = u // 4 - 1
                    v.tensor_tensor(GATES[:, 0, j * CW:(j + 1) * CW], banks[0][:, :], b, ALU.add)
                    tell(v.tensor_tensor(GATES[:, 1, j * CW:(j + 1) * CW], banks[1][:, :], b, ALU.add), drained, key)
                    after(key)
                r = k - (HI + 2)
                if 0 <= r < TOPK // 8:
                    for a, cols in ((0, slice(0, S)), (8, slice(S, S + P))):
                        ins = v.max(MAX8[:, a:a + 8], IDX[:, cols])
                    link(ins)
                    for a, cols in ((0, slice(0, S)), (8, slice(S, S + P))):
                        ins = v.match_replace(IDX[:, cols], MAX8[:, a:a + 8], IDX[:, cols], PICKED)
                    link(ins)
                    if r == TOPK // 8 - 1:
                        link(v.tensor_scalar(IDX[:, :], IDX[:, :], PICKED, NEG, ALU.not_equal, ALU.mult))

            attention(l, heads_one(), mask_of, weave, ONE, scaled_output(l), late)

            def branch_out(cc, b):
                n = "ABC".index(b)
                key = ("branch", l, cc, b)
                banks = product_ready(dve, key)
                j = (n * D + cc * CW) // CW
                dve.wait_ge(act_side.sem, act_side.at(("gate", l, j)))
                for t in range(NT):
                    g = GATES[:, t, j * CW:(j + 1) * CW]
                    ins = v.scalar_tensor_tensor(O[:, t, cc * CW:(cc + 1) * CW] if b == "C" else g, g, 1.0, banks[t][:, :], ALU.add, ALU.mult)
                tell(ins, drained, key)
                if b != "C":
                    for t in range(NT):
                        ins = v.tensor_tensor(O[:, t, cc * CW:(cc + 1) * CW], O[:, t, cc * CW:(cc + 1) * CW],
                                              GATES[:, t, j * CW:(j + 1) * CW], ALU.add)
                    if b == "A":
                        say(ins, ("y", l, cc))
                    else:
                        link(ins)

            o_order = (3, 2, 1, 0)
            turn_lo(("o", l), HT, order=o_order, part=slice(0, 2))
            link(v.tensor_copy(HT[64:128, KT, :, :], HT[64:128, 5, :, :].bitcast(F32)))
            say(v.memset(HT[64:128, 5, :, :].bitcast(F32), 0.0), ("halves", l))
            turn_lo(("o", l), HT, order=o_order, part=slice(2, 4))
            for b in "CBA":
                branch_out(0, b)
            branch_out(1, "C")
            turn_lo(("y", l), AT, part=slice(0, 2))
            branch_out(1, "B")
            branch_out(1, "A")
            turn_lo(("y", l), AT, part=slice(2, 4))

            def add_to_x(key, gain, factor, tmp_of, event, coef):
                cc = key[-1]
                before(key)
                banks = product_ready(dve, key)
                for t in range(NT):
                    ins = v.scalar_tensor_tensor(tmp_of(t), banks[t][:, :], factor, MOD[:, gain + cc * CW:gain + (cc + 1) * CW], ALU.mult, ALU.mult)
                tell(ins, drained, key)
                for t in range(NT):
                    xs = X[:, t, cc * CW:(cc + 1) * CW]
                    ins = v.tensor_tensor(xs, xs, tmp_of(t), ALU.add)
                say(ins, ("x", event, cc))
                after(key)
                if coef is not None:
                    scaled(cc, coef)

            for cc in range(2):
                add_to_x(("wout", l, cc), 2 * D, 0.5, lambda t: GATES[:, t, D:D + CW], ("mid1", l), 4 * D)
            root_of_squares(("n2", l))
            h_rows(("n2", l), 3 * D)
            turn_lo(("n2", l), HT)
            n_ff = -(-FFN // CW)
            for j in range(n_ff):
                n = min(CW, FFN - j * CW)
                kg, ku = ("ffg", l, j), ("ffu", l, j)
                before(kg)
                banks = product_ready(dve, kg)
                dve.wait_ge(act_side.sem, act_side.at(("tg", l, j)))
                for t in range(NT):
                    ins = v.scalar_tensor_tensor(TG[:, j % 2, t, 0:n], TG[:, j % 2, t, 0:n], 1.0, banks[t][:, 0:n], ALU.add, ALU.mult)
                tell(ins, drained, kg)
                after(kg)
                if j:
                    turn_lo_ffn(("a", l), j - 1, CW // P)
                before(ku)
                banks = product_ready(dve, ku)
                for t in range(NT):
                    ins = v.scalar_tensor_tensor(O[:, t, (j % 2) * CW:(j % 2) * CW + n], TG[:, j % 2, t, 0:n], 0.5, banks[t][:, 0:n], ALU.mult, ALU.mult)
                tell(ins, drained, ku)
                after(ku)
            turn_lo_ffn(("a", l), n_ff - 1, (FFN - (n_ff - 1) * CW) // P)
            for cc in range(2):
                add_to_x(("ffo", l, cc), 5 * D, 1.0, lambda t: TG[:, 0, t, :], ("end", l), D if l + 1 < DEPTH else None)

        def vec_free(name, ins):
            tell(ins, vec_used, name)

        root_of_squares("final")
        for half in range(2):
            g = vec_ready(dve, ("final_g", half))
            for t in range(NT):
                xs = X[:, t, half * CW:(half + 1) * CW]
                ins = v.scalar_tensor_tensor(xs, xs, RR[:, t:t + 1], g, ALU.mult, ALU.mult)
            vec_free(("final_g", half), ins)

        stats = STAT.rearrange("p (t c s) -> p t c s", t=NT, c=2)

        def layer_norm(tag, names):
            g_name, b_name, i = names
            for t in range(NT):
                ins = v.bn_aggr(MV[:, 2 * t:2 * t + 2], STAT[:, 12 * t:12 * t + 12])
            say(ins, ("var", tag))
            dve.wait_ge(act_side.sem, act_side.at(("root", tag)))
            link(v.reciprocal(RR[:, 0:NT], RSTD))
            for half in range(2):
                for name, scalar, ops in ((g_name, MV[:, 0::2], (ALU.subtract, ALU.mult)), (b_name, RR[:, 0:NT], (ALU.mult, ALU.add))):
                    g = vec_ready(dve, (name, i, half))
                    for t in range(NT):
                        xs = X[:, t, half * CW:(half + 1) * CW]
                        ins = v.scalar_tensor_tensor(xs, xs, scalar[:, t:t + 1], g, *ops)
                    vec_free((name, i, half), ins)

        def residual(key):
            cc = key[-1]
            banks = product_ready(dve, key)
            for t in range(NT):
                xs = X[:, t, cc * CW:(cc + 1) * CW]
                ins = v.scalar_tensor_tensor(xs, xs, ALPHA, banks[t][:, :], ALU.mult, ALU.add)
            tell(ins, drained, key)
            for t in range(NT):
                ins = v.bn_stats(stats[:, t, cc, :], X[:, t, cc * CW:(cc + 1) * CW])
            link(ins)

        for i in range(2):
            heads = heads_two(i)
            nh = len(heads)
            turn_lo(("x", i), HT)
            w = 3 * nh * DH
            for j in range(-(-w // CW)):
                key = ("qkv", i, j)
                n = min(CW, w - j * CW)
                banks = product_ready(dve, key)
                rot = max(0, min(n, 2 * nh * DH - j * CW))
                for t in range(NT):
                    if rot:
                        r = rot // DH
                        four = lambda a: a.rearrange("p (h two d) -> p h two d", two=2, d=DH // 2)
                        wide = lambda name: con(name).rearrange("p (two d) -> p two d", two=2).unsqueeze(1).to_broadcast([P, r, 2, DH // 2])
                        px = banks[t][:, 0:rot]
                        v.tensor_tensor(four(RTMP[:, 0, 0:rot]), four(px), wide(f"cc{t}"), ALU.mult)
                        link(v.tensor_tensor(four(RTMP[:, 1, 0:rot]), four(px)[:, :, ::-1, :], wide(f"ss{t}"), ALU.mult))
                        ins = v.tensor_tensor(QKV[:, t, j * CW:j * CW + rot], RTMP[:, 0, 0:rot], RTMP[:, 1, 0:rot], ALU.add)
                    if rot < n:
                        if rot:
                            link(ins)
                        ins = v.tensor_copy(QKV[:, t, j * CW + rot:j * CW + n], banks[t][:, rot:n])
                    if t < NT - 1:
                        link(ins)
                tell(ins, drained, key)
            if i == 0:
                attention(("two", i), heads, lambda hd: (con("causal"), con("causal")[:, P:S]), lambda k: None, TWO,
                          scaled_output(("two", i)))
                dve.wait_ge(head_out.sem, head_out.at((("two", i), nh - 1)))
            else:
                dve.wait_ge(dil_in, 16)

                def raw_output(h, hd, bank):
                    dve.wait_ge(headed.sem, headed.at((("two", 1), h)))
                    tell(v.tensor_copy(O[:, :, hd["o"]:hd["o"] + DH], bank[:, 384:512].rearrange("p (t d) -> p t d", t=NT)),
                    head_out, (("two", 1), h))

                attention(("two", i), heads, lambda hd: (DILM[:, hd["h"] // 4, :], DILM[:, hd["h"] // 4, P:S]), lambda k: None,
                          TWO, raw_output)
                dve.wait_ge(head_out.sem, head_out.at((("two", i), nh - 1)))
                n2 = 4 * NT
                mx, rs, ww = MX[:, 0:3 * n2], RS[:, 0:3 * n2], NM[:, 0:3 * n2]
                gm = RR[:, 0:n2]
                link(v.tensor_tensor(gm, mx[:, 0:n2], mx[:, n2:2 * n2], ALU.max))
                link(v.tensor_tensor(gm, gm, mx[:, 2 * n2:3 * n2], ALU.max))
                for g in range(3):
                    ins = v.tensor_tensor(mx[:, g * n2:(g + 1) * n2], mx[:, g * n2:(g + 1) * n2], gm, ALU.subtract)
                say(ins, "group_max")
                dve.wait_ge(act_side.sem, act_side.at("group_exp"))
                link(v.tensor_tensor(rs, rs, ww, ALU.mult))
                link(v.tensor_tensor(gm, rs[:, 0:n2], rs[:, n2:2 * n2], ALU.add))
                link(v.tensor_tensor(gm, gm, rs[:, 2 * n2:3 * n2], ALU.add))
                link(v.reciprocal(gm, gm))
                for g in range(3):
                    ins = v.tensor_tensor(ww[:, g * n2:(g + 1) * n2], ww[:, g * n2:(g + 1) * n2], gm, ALU.mult)
                link(ins)
                for t in range(NT):
                    ot = O[:, t, 0:nh * DH].rearrange("p (h d) -> p h d", d=DH)
                    say(v.tensor_tensor(ot, ot, ww.rearrange("p (h t) -> p h t", t=NT)[:, :, t:t + 1].to_broadcast([P, nh, DH]), ALU.mult),
                        "weighted" if t == NT - 1 else "weighting")
            turn_lo(("o2", i), HT, nh * DH // P)
            for cc in range(2):
                residual(("wo", i, cc))
            layer_norm(("mid", i), ("ln_mix_g", "ln_mix_b", i))
            turn_lo(("m", i), HT)
            for j in range(DFF // CW):
                key = ("mi", i, j)
                dve.wait_ge(act_side.sem, act_side.at(("relu", i, j)))
                if j >= 2:
                    dve.wait_ge(turned.sem, turned.at((("a2", i), j - 2, 1)))
                for t in range(NT):
                    ins = v.tensor_tensor(O[:, t, (j % 2) * CW:(j % 2 + 1) * CW], RT[:, j % 2, t, :], RT[:, j % 2, t, :], ALU.mult)
                say(ins, ("a2", i, j))
                if j:
                    turn_lo_ffn(("a2", i), j - 1, CW // P)
            turn_lo_ffn(("a2", i), DFF // CW - 1, CW // P)
            for cc in range(2):
                residual(("mo", i, cc))
            layer_norm(("end2", i), ("ln_mlp_g", "ln_mlp_b", i))


def turn_ffn(pe, turned, turned_lo, rows, drained, tag, j, n, BANK, TQ, TP, O, con):
    signal_, event = (drained, ("ffu", tag[1], j)) if tag[0] == "a" else (rows, (*tag, j))
    pe.wait_ge(signal_.sem, signal_.at(event))
    for t in range(NT):
        if j:
            pe.wait_ge(turned_lo.sem, turned_lo.at((tag, j - 1, t)))
        for k in range(n):
            ins = pe.transpose(BANK[(TQ, TP)[t]][:, k * P:(k + 1) * P],
                               O[:, t, (j % 2) * CW + k * P:(j % 2) * CW + (k + 1) * P], con("ident"))
        ins.then_inc(turned.sem, turned.mark((tag, j, t)))


def unit_index(key):
    chunks, _ = plan()
    return next(c for c in chunks if c["key"] == key)["units"][0]["index"]


dil_at = unit_index(("mi", 0, 0))

_INS = ["x", "c", "positions", "ada_w", "ada_b", "norm1_g", "w_in", "b_in", "rel_bias", "w_branch", "w_out",
        "norm2_g", "w_ffn_in", "w_ffn_out", "final_g", "moba_w_qkv_2", "moba_w_o_2", "dil_w_qkv_2", "dil_w_o_2",
        "mlp_w_in_2", "mlp_w_out_2", "ln_mix_g_2", "ln_mix_b_2", "ln_mlp_g_2", "ln_mlp_b_2"]


def traced(nc, arrays, cat, book):
    dram = {}
    for name, a in arrays.items():
        short = name.removeprefix("in_").removesuffix("_2")
        dram[short] = nc.dram_tensor(name, a.shape, mybir.dt.from_np(a.dtype), kind="ExternalInput").ap()
    out = nc.dram_tensor("out_0_dram", (1, S, D), F32, kind="ExternalOutput").ap()
    build(nc, dram, out, cat, book)
    return nc


def kernel(**inputs):
    import concourse.bacc as bacc
    from concourse.bass_utils import run_bass_kernel_spmd

    const, cat = constants()
    arrays = {f"in_{name}": np.ascontiguousarray(inputs[name]) for name in _INS}
    arrays["in_constants"] = const
    values = {}
    traced(bacc.Bacc("TRN2", target_bir_lowering=False, num_devices=1), arrays, cat, ({}, values))
    nc = traced(bacc.Bacc("TRN2", target_bir_lowering=False, num_devices=1), arrays, cat, (values, {}))
    return run_bass_kernel_spmd(nc, [arrays], core_ids=[0]).results[0]["out_0_dram"]
```

```python
from contextlib import ExitStack

import numpy as np

import concourse.bass as bass
from concourse import mybir

F32 = mybir.dt.float32
F32R = mybir.dt.float32r
I32 = mybir.dt.int32
ALU = mybir.AluOpType
ACT = mybir.ActivationFunctionType
AX_X = mybir.AxisListType.X

P = 128
S = 256
NT = S // P
D = 1024
KT = D // P
CW = 512
DEPTH = 2
DH = 64
CHUNK = 64
HA, HB, HC, HI = 6, 5, 5, 8
FFN = 2816
DFF = 4096
REL = 128
MOBA_H, DIL_H = 16, 12
DIL = ((128, 1), (512, 4), (2048, 16))
TOPK = S // 4
ALPHA = (2.0 * DEPTH) ** 0.25
RMS_EPS, LN_EPS = 1e-6, 1e-5
SCALE = DH ** -0.5
NEG = -1e30
IDX_OUT = -1e38
PICKED = -3e38

QA, KA, VA = 0, HA * DH, 2 * HA * DH
QI = 3 * HA * DH
KI = QI + HI * DH
WI = KI + DH
QB = WI + HI
KB, VB = QB + HB * DH, QB + 2 * HB * DH
QC = QB + 3 * HB * DH
KC, VC = QC + HC * DH, QC + 2 * HC * DH
FC = QC + 3 * HC * DH
GATE = FC + HC
PROJ_W = GATE + 1
IN_W = GATE + 3 * D
N_PROJ = -(-PROJ_W // CW)
N_GATE = 3 * D // CW

NR = 5
NH = 5
NV = 5
UNIT_K = 2
SPLIT = 4


def constants():
    p = np.arange(P)[:, None]
    k = np.arange(S)[None, :]
    d = P + p - k
    parts = [("ident", np.eye(P)), ("ones", np.ones((P, P)))]
    parts += [("causal", np.where(d >= 0, 0.0, NEG))]
    parts += [("band", np.where(k // CHUNK <= (P + p) // CHUNK, 0.0, NEG))]
    parts.append(("tri", np.where(P + p <= np.arange(3 * P)[None, :], 1 / SCALE, 0.0)))
    rot = DH // 4
    inv = np.float32(500000.0) ** (-np.arange(0, rot, 2, dtype=np.float32) / np.float32(rot))
    parts.append(("inv", np.tile(inv.astype(np.float32)[None], (P, 1))))
    inv2 = (1.0 / (np.float32(10000.0) ** (np.arange(0, DH, 2, dtype=np.float32) / np.float32(DH)))).astype(np.float32)
    for t in range(NT):
        ang = ((t * P + p).astype(np.float32) * inv2[None]).astype(np.float32).astype(np.float64)
        parts.append((f"cc{t}", np.concatenate([np.cos(ang), np.cos(ang)], 1)))
        parts.append((f"ss{t}", np.concatenate([-np.sin(ang), np.sin(ang)], 1)))
    parts.append(("eps", np.tile(np.array([[RMS_EPS, LN_EPS]]), (P, 1))))
    for g, (window, dil) in enumerate(DIL):
        parts.append((f"dil{g}", np.where((d >= 0) & (d <= window) & (d % dil == 0), 0.0, NEG)))
    at, cols = {}, 0
    for name, a in parts:
        at[name] = (cols, cols + a.shape[1])
        cols += a.shape[1]
    return np.concatenate([a for _, a in parts], 1).astype(np.float32), at


class Signal:

    def __init__(self, sem, name, book):
        self.sem, self.name, self.known, self.new = sem, name, book[0], book[1]
        self.count = 0

    def mark(self, event):
        self.count += 1
        self.new[self.name, event] = self.count
        return 1

    def at(self, event):
        return self.known[self.name, event] if self.known else 1


def plan():
    chunks, stream = [], []
    count = {"w": 0, "ada": 0, "vec": 0}
    pair = [0]

    def chunk(key, src, row0, ktiles, col0, ncols, steps=None):
        c = dict(key=key, kind="gemm", pair=pair[0] % 2, ncols=ncols, units=[])
        pair[0] += 1
        for k0 in range(0, ktiles, UNIT_K):
            n = min(UNIT_K, ktiles - k0)
            u = dict(kind="w", index=count["w"], n=n, ncols=ncols, src=(src, row0 + k0 * P, n, col0, ncols))
            u["tiles"] = [[(k0 + i, i)] for i in range(n)] if steps is None else steps[k0 // UNIT_K]
            count["w"] += 1
            c["units"].append(u)
        chunks.append(c)
        return c

    def vec(name, src, col0, ncols=CW):
        v = dict(kind="vec", index=count["vec"], name=name, src=(src, col0, ncols), ncols=ncols)
        count["vec"] += 1
        return v

    def ada(l, c):
        units = []
        for i in range(KT // UNIT_K):
            units.append(dict(kind="ada", index=count["ada"], l=l, c=c, i=i))
            count["ada"] += 1
        return dict(key=("ada", l, c), kind="ada", units=units)

    def ada_vecs(l, c):
        vs = [vec(("ada_b", l, c), ("ada_b", l), c * CW)]
        if c in (2, 3):
            vs.append(vec(("norm1_g", l, c - 2), ("norm1_g", l), (c - 2) * CW))
        if c in (8, 9):
            vs.append(vec(("norm2_g", l, c - 8), ("norm2_g", l), (c - 8) * CW))
        return vs

    def put(c, vec_args=None):
        stream.extend(c["units"][:-1])
        if vec_args:
            stream.append(vec(*vec_args))
        stream.append(c["units"][-1])

    def phase(parts, adas, summed=True, lead=0, tail=0):
        units = [(l, c, n) for l, c in adas for n in range(KT // UNIT_K)]
        made = {}
        total = sum(-(-args[3] // UNIT_K) for _, args in parts) - lead - tail
        seen = sent = 0
        for vec_args, args in parts:
            done = []
            c = chunk(*args)
            for n, u in enumerate(c["units"]):
                if vec_args and n == len(c["units"]) - 1:
                    stream.append(vec(*vec_args))
                stream.append(u)
                seen += 1
                while sent * total < (seen - lead) * len(units) and sent < len(units):
                    l, a, i = units[sent]
                    if i == 0:
                        made[l, a] = ada(l, a)
                    last_ = i == KT // UNIT_K - 1
                    if last_ and summed:
                        stream.extend(ada_vecs(l, a))
                    stream.append(made[l, a]["units"][i])
                    if last_:
                        done.append(made[l, a])
                    sent += 1
            if summed:
                chunks.extend(done)
        return list(made.values())

    for c in (2, 3, 0):
        a = ada(0, c)
        chunks.append(a)
        stream.extend(a["units"])
        stream.extend(ada_vecs(0, c))
    last_shift = ada(0, 1)
    chunks.append(last_shift)
    for l in range(DEPTH):
        start = len(stream)
        parts = []
        for j in range(N_PROJ):
            n = min(CW, PROJ_W - j * CW)
            parts.append(((("b_in", l, j), ("b_in", l), j * CW, n), (("proj", l, j), ("w_in", l), 0, KT, j * CW, n)))
        phase(parts, [(l, c) for c in (4, 5, 6, 7)], lead=SPLIT)
        if l == 0:
            at = [n for n in range(start, len(stream)) if stream[n]["kind"] == "w"][1] + 1
            stream[at:at] = last_shift["units"] + ada_vecs(0, 1)
        parts = []
        for j in range(N_GATE):
            parts.append(((("b_gate", l, j), ("b_in", l), GATE + j * CW), (("gate", l, j), ("w_in", l), 0, KT, GATE + j * CW, CW)))
        late = phase(parts, [(l, 8), (l, 9)], summed=False)
        for cc in range(D // CW):
            for b, k0, kn, st in (("C", 5, 3, [[[(8, 0)], [(6, 1)]], [[(7, 0)]]]),
                                  ("B", 3, 3, [[[(3, 0)], [(4, 1)]], [[(5, 0)]]]),
                                  ("A", 0, 3, [[[(0, 0)], [(1, 1)]], [[(2, 0)]]])):
                put(chunk(("branch", l, cc, b), ("w_branch", l), k0 * P, kn, cc * CW, CW, steps=st))
        for a in late:
            stream.extend(ada_vecs(*a["key"][1:]))
        for cc in range(D // CW):
            put(chunk(("wout", l, cc), ("w_out", l), 0, KT, cc * CW, CW))
            if cc == 0:
                chunks.extend(late)
        parts = []
        for j in range(-(-FFN // CW)):
            n = min(CW, FFN - j * CW)
            parts.append((None, (("ffg", l, j), ("w_ffn_in", l), 0, KT, j * CW, n)))
            parts.append((None, (("ffu", l, j), ("w_ffn_in", l), 0, KT, FFN + j * CW, n)))
        phase(parts, [(l, 10), (l, 11)] + [(l + 1, c) for c in range(4) if l + 1 < DEPTH], lead=SPLIT, tail=8)
        for cc in range(D // CW):
            put(chunk(("ffo", l, cc), ("w_ffn_out", l), 0, FFN // P, cc * CW, CW))
    stream.extend(vec(("final_g", h), ("final_g",), h * CW) for h in range(2))
    for i in range(2):
        heads = (MOBA_H, DIL_H)[i]
        w = 3 * heads * DH
        for j in range(-(-w // CW)):
            n = min(CW, w - j * CW)
            put(chunk(("qkv", i, j), (("moba_w_qkv", "dil_w_qkv")[i],), 0, KT, j * CW, n))
        for cc in range(2):
            put(chunk(("wo", i, cc), (("moba_w_o", "dil_w_o")[i],), 0, heads * DH // P, cc * CW, CW))
        stream.extend(vec((v, i, h), (v, i), h * CW) for h in range(2) for v in ("ln_mix_g", "ln_mix_b"))
        for j in range(DFF // CW):
            put(chunk(("mi", i, j), ("mlp_w_in", i), 0, KT, j * CW, CW))
        for cc in range(2):
            put(chunk(("mo", i, cc), ("mlp_w_out", i), 0, DFF // P, cc * CW, CW))
        stream.extend(vec((v, i, h), (v, i), h * CW) for h in range(2) for v in ("ln_mlp_g", "ln_mlp_b"))
    for n, v in enumerate(v for v in stream if v["kind"] == "vec"):
        v["index"] = n
    for kind in ("ada", "w"):
        for n, u in enumerate(u for u in stream if u["kind"] == kind):
            u["index"] = n
    last = {}
    for c in chunks:
        place = c["pair"] if c["kind"] == "gemm" else ("ada", c["key"][2] % 2)
        c["before"] = last.get(place)
        last[place] = c["key"]
    return chunks, stream


def heads_one():
    out = [dict(kind="I", h=h, q=QI + h * DH, k=KI) for h in range(HI)]
    out += [dict(kind="B", h=h, q=QB + h * DH, k=KB + h * DH, v=VB + h * DH, o=(HA + h) * DH) for h in range(HB)]
    out += [dict(kind="C", h=h, q=QC + h * DH, k=KC + h * DH, v=VC + h * DH, o=(HA + HB + h) * DH) for h in range(HC)]
    out += [dict(kind="A", h=h, q=QA + h * DH, k=KA + h * DH, v=VA + h * DH, o=h * DH) for h in range(HA)]
    return out


def heads_two(i):
    n = (MOBA_H, DIL_H)[i]
    kind = "MD"[i]
    return [dict(kind=kind, h=h, q=h * DH, k=(n + h) * DH, v=(2 * n + h) * DH, o=h * DH) for h in range(n)]


def build(nc, dram, out, cat, book):
    with ExitStack() as ctx:
        program(nc, ctx, dram, out, cat, book)


def program(nc, ctx, dram, out, cat, book):
    chunks, stream = plan()
    by_key = {c["key"]: c for c in chunks}
    vec_of = {i["name"]: i for i in stream if i["kind"] == "vec"}
    ring = [i for i in stream if i["kind"] != "vec"]
    for n, i in enumerate(ring):
        i["slot"], i["turn"] = n % NR, n // NR
        i["evicts"] = ring[n - NR] if n >= NR else None

    plan_at = [-(-nc.sbuf_base // 64) * 64]
    top = []

    def place(name, shape, dt=F32, at=None):
        size = int(np.prod(shape[1:])) * 4
        offset = plan_at[0] if at is None else at
        if at is None:
            plan_at[0] += -(-size // 32) * 32
        top.append(offset + size)
        t = nc.alloc_sbuf_tensor_at(name, list(shape), dt, offset=offset)
        return t, offset

    X, _ = place("x_rows", [P, NT, D])
    O, _ = place("o_rows", [P, NT, D])
    HT, _ = place("turned", [P, KT + 1, 2, S], F32R)
    RAW, _ = place("raw_units", [P, NR, UNIT_K, CW])
    HI_, _ = place("hi_units", [P, NH, UNIT_K, CW], F32R)
    LO, _ = place("lo_units", [P, NH, UNIT_K, CW], F32R)
    VEC, _ = place("row_vectors", [P, NV, CW])
    PROJ, union = place("proj_rows", [P, NT, PROJ_W])
    GATES, _ = place("gate_rows", [P, NT, 3 * D])
    AT, _ = place("turned_wide", [P, DFF // P, 2, S], F32R, at=union)
    TG, _ = place("ffn_tanh", [P, 2, NT, CW], at=union + FFN // P * 2 * S * 4)
    RT, _ = place("mlp_relu", [P, 2, NT, CW], at=union + DFF // P * 2 * S * 4)
    one_end = union + max(FFN // P * 2 * S * 4 + 2 * NT * CW * 4, NT * (PROJ_W + 3 * D) * 4)
    MOD, mod_at = place("mod_rows", [P, 6 * D], at=-(-one_end // 64) * 64)
    free_at = [mod_at]

    def in_mod(name, shape):
        t, at = place(name, shape, at=free_at[0])
        free_at[0] = at + -(-int(np.prod(shape[1:])) * 4 // 32) * 32
        assert free_at[0] <= mod_at + 2 * D * 4
        return t

    QKT = in_mod("qk_turned", [DH, 2, 2 * S])
    KIT = in_mod("idx_keys_turned", [DH, S])
    IDX = in_mod("idx_scores", [P, 3 * P])
    LB = in_mod("logf_wide", [P, NT, P])
    QKV, _ = place("qkv_rows", [P, NT, 3 * D], at=union)
    RTMP, _ = place("rotary_tmp", [P, 2, CW], at=union + DFF // P * 2 * S * 4)
    QKV_END = union + NT * 3 * D * 4
    QKT2, _ = place("qk_turned_2", [DH, 3, 2 * S], at=QKV_END)
    PT2, _ = place("probs_turned_2", [P, 3, 3 * P], at=QKV_END + 3 * 2 * S * 4)
    plan_at[0] = -(-max(top) // 64) * 64
    SM, _ = place("scores", [P, 3, 3 * P])
    PT, _ = place("probs_turned", [P, 2, 3 * P])
    MB, _ = place("bias_masks", [P, HB, S])
    CM, cm_at = place("forget_masks", [P, HC, 3 * P])
    n_const = cat["eps"][1]
    CON, _ = place("constants", [P, n_const])
    DILM, _ = place("dilated_masks", [P, 3, S], at=cm_at)
    SMALL, _ = place("small", [P, 420])
    SQ = SM[:, :, :].rearrange("p a b -> p (a b)")[:, 0:NT * CW].rearrange("p (t n) -> p t n", t=NT)
    POS, _ = place("positions_int", [P, NT], I32)
    RB, _ = place("rel_rows", [DEPTH * HB, 2 * REL + 1], at=cm_at)
    RE, _ = place("rel_extended", [DEPTH * HB, 3 * P], at=cm_at + 2048)
    assert max(top) <= nc.sbuf_usable_end, (max(top), nc.sbuf_usable_end)
    scratch = nc.dram_tensor("rel_scratch", [DEPTH * HB, 3 * P], F32)

    def con(name):
        a, b = cat[name]
        return CON[:, a:b]

    used = [0]

    def small(n):
        used[0] += n
        assert used[0] <= 420
        return SMALL[:, used[0] - n:used[0]]

    COND, CT = small(KT), small(KT)
    POSF, ANG, KR, RED, COS, SIN = (small(NT), *(small(NT * 8) for _ in range(5)))
    MAX8 = small(16)
    ZN, ZA, ZE, ZU, ZL, ZD, LF, F8 = (small(NT * HC) for _ in range(8))
    MX, NM, RS, RR = (small(48) for _ in range(4))
    STAT = small(24)
    MV, RSTD, NMR = small(4), small(2), small(2)

    BANK = [ctx.enter_context(nc.psum_tensor(f"bank{i}", [P, CW], F32)) for i in range(8)]
    SB_ = (4, 5)
    TQ, TP = 6, 7

    ONE = dict(score=1, turn=3, weigh=4, qk=QKT, pt=PT, n_pt=2, n_qk=2, tq=(TQ,), tp=(TP,))
    TWO = dict(score=2, turn=4, weigh=6, qk=QKT2, pt=PT2, n_pt=3, n_qk=3, tq=(TQ, 2), tp=(TP, 3, 1))
    N_SM = 3
    GATE_STEP = 2

    def sem(name):
        return ctx.enter_context(nc.semaphore(name))

    def signal(name):
        return Signal(sem(name), name, book)

    raw_in = [sem(f"raw_in{i}") for i in range(NR)]
    vec_in = [sem(f"vec_in{i}") for i in range(NV)]
    x_in, c_in, pos_in, const_in, rel_in = (sem(n) for n in ("x_in", "c_in", "pos_in", "const_in", "rel_in"))
    scratch_in, dil_in, out_in = sem("scratch_in"), sem("dil_in"), sem("out_in")
    bias_in = [sem(f"bias_in{h}") for h in range(HB)]
    hi_ready = signal("hi_ready")
    lo_ready = signal("lo_ready")
    unit_used = signal("unit_used")
    ada_used = signal("ada_used")
    vec_used = signal("vec_used")
    product = signal("product")
    drained = signal("drained")
    turned = signal("turned")
    turned_hi = signal("turned_hi")
    turned_lo = signal("turned_lo")
    rows = signal("rows")
    act_side = signal("act_side")
    qk_in_psum = signal("qk_in_psum")
    qk_turned = signal("qk_turned")
    scored = signal("scored")
    masked = signal("masked")
    exped = signal("exped")
    p_in_psum = signal("p_in_psum")
    p_turned = signal("p_turned")
    headed = signal("headed")
    head_out = signal("head_out")
    forget = signal("forget")
    chain = signal("chain")
    act_chain = signal("act_chain")

    def tile_rows(src):
        name, *ix = src
        a = dram[name]
        return a[ix[0]] if ix else (a[0] if len(a.shape) == 3 else a)

    def raw_ready(e, u):
        e.wait_ge(raw_in[u["slot"]], 16 * (u["turn"] + 1))

    def vec_ready(e, name):
        v = vec_of[name]
        e.wait_ge(vec_in[v["index"] % NV], 16 * (v["index"] // NV + 1))
        return VEC[:, v["index"] % NV, 0:v["ncols"]]

    vectors = [i for i in stream if i["kind"] == "vec"]

    def freed_by(vec):
        what, *ix = vec["name"]
        if what in ("ada_b", "b_in", "b_gate"):
            return drained, ({"ada_b": "ada", "b_in": "proj", "b_gate": "gate"}[what], *ix)
        return vec_used, vec["name"]

    block = ctx.enter_context(nc.Block())

    @block.sync
    def _(sp):
        sp.dma_start(COND, dram["c"].rearrange("b (p k) -> (b p) k", p=P)).then_inc(c_in, 16)
        sp.dma_start(CON[:, :], dram["constants"][:, 0:n_const]).then_inc(const_in, 16)
        ada_seen = 0
        for item in stream:
            if item["kind"] == "vec":
                n = item["index"]
                if n >= NV:
                    signal_, event = freed_by(vectors[n - NV])
                    sp.wait_ge(signal_.sem, signal_.at(event))
                (name, *ix), col0, ncols = item["src"]
                a = dram[name]
                row = (a[ix[0]:ix[0] + 1, :] if ix else a.rearrange("(a n) -> a n", a=1))[:, col0:col0 + ncols]
                sp.dma_start(VEC[:, n % NV, 0:ncols], row.to_broadcast([P, ncols])).then_inc(vec_in[n % NV], 16)
                continue
            old = item["evicts"]
            if old is not None and old["kind"] == "w":
                sp.wait_ge(lo_ready.sem, lo_ready.at(old["index"]))
            elif old is not None:
                sp.wait_ge(ada_used.sem, ada_used.at(old["index"]))
            if item["kind"] == "ada":
                l, c, i = item["l"], item["c"], item["i"]
                ada_seen += 1
                if ada_seen == KT:
                    sp.dma_start(X[:, :, :], dram["x"][0].rearrange("(t p) d -> p t d", p=P)).then_inc(x_in, 16)
                src = dram["ada_w"][l].rearrange("(p k) n -> p k n", p=P)[:, i * UNIT_K:(i + 1) * UNIT_K, c * CW:(c + 1) * CW]
                sp.dma_start(RAW[:, item["slot"], :, :], src).then_inc(raw_in[item["slot"]], 16)
            else:
                src, row0, n, col0, ncols = item["src"]
                a = tile_rows(src)[row0:row0 + n * P, col0:col0 + ncols].rearrange("(k p) n -> p k n", p=P)
                key = item["index"]
                if key == dil_at:
                    sp.wait_ge(masked.sem, masked.at((DEPTH - 1, HI + HB + HC - 1)))
                    a0, b0 = cat["dil0"][0], cat["dil2"][1]
                    sp.dma_start(DILM[:, :, :], dram["constants"][:, a0:b0].rearrange("p (g k) -> p g k", g=3)).then_inc(dil_in, 16)
                sp.dma_start(RAW[:, item["slot"], 0:n, 0:ncols], a).then_inc(raw_in[item["slot"]], 16)
        for t in range(NT):
            if t == 0:
                sp.wait_ge(rows.sem, rows.at(("h", ("end2", 1), 0, 1)))
            else:
                sp.wait_ge(vec_used.sem, vec_used.at(("ln_mlp_b", 1, 1)))
            sp.dma_start(out[0, t * P:(t + 1) * P, :], X[:, t, :]).then_inc(out_in, 16)
        sp.wait_ge(out_in, 16 * NT)

    @block.gpsimd
    def _(pool):
        for u in (i for i in ring if i["kind"] == "w"):
            s, n, w = u["index"] % NH, u["n"], u["ncols"]
            pool.wait_ge(hi_ready.sem, hi_ready.at(u["index"]))
            pool.tensor_tensor(LO[:, s, 0:n, 0:w], RAW[:, u["slot"], 0:n, 0:w], HI_[:, s, 0:n, 0:w].bitcast(F32),
                               ALU.subtract).then_inc(lo_ready.sem, lo_ready.mark(u["index"]))

    @block.tensor
    def _(pe):
        todo = [c for c in chunks]

        def pair_free(c):
            if c["before"][0] == "mi":
                pe.wait_ge(act_side.sem, act_side.at(("relu", *c["before"][1:])))
            else:
                pe.wait_ge(drained.sem, drained.at(c["before"]))

        def unit(c, i, A, tiles=range(NT)):
            u = c["units"][i]
            if i == 0 and tiles[0] == 0 and c["before"] is not None:
                pair_free(c)
            pe.wait_ge(lo_ready.sem, lo_ready.at(u["index"]))
            s, w = u["index"] % NH, u["ncols"]
            nt = [(a, b) for tile in u["tiles"] for a, b in tile]
            for t in tiles:
                for m, (a, b) in enumerate(nt):
                    xs = A[:, a, :, t * P:(t + 1) * P]
                    passes = ((0, HI_), (0, LO), (1, HI_))
                    for q, (part, W) in enumerate(passes):
                        ins = pe.matmul(BANK[2 * c["pair"] + t][:, 0:w], xs[:, part, :], W[:, s, b, 0:w],
                                        start=(i == 0 and m == 0 and q == 0),
                                        stop=(i == len(c["units"]) - 1 and m == len(nt) - 1 and q == 2))
            if tiles[-1] == NT - 1:
                ins.then_inc(unit_used.sem, unit_used.mark(u["index"]))
            elif i == len(c["units"]) - 1:
                ins.then_inc(product.sem, product.mark(("first tile", c["key"])))

        def ending(A):
            c = todo.pop(0)
            n = len(c["units"])
            for i in range(n - SPLIT):
                unit(c, i, A)
            for t in range(NT):
                for i in range(max(0, n - SPLIT), n):
                    unit(c, i, A, (t,))

        def turn_tile(tag, src, n, ready):
            t, half = n // 2, n % 2
            if n >= 2:
                pe.wait_ge(turned_lo.sem, turned_lo.at((tag, "tile", n - 2)))
            signal_, event = ready(t, half)
            pe.wait_ge(signal_.sem, signal_.at(event))
            for j in range(4):
                ins = pe.transpose(BANK[(TQ, TP)[n % 2]][:, j * P:(j + 1) * P],
                                   src[:, t, (4 * half + j) * P:(4 * half + j + 1) * P], con("ident"))
            ins.then_inc(turned.sem, turned.mark((tag, "tile", n)))

        def beginning(tag, src, ready, A):
            c = todo.pop(0)
            assert len(c["units"]) == SPLIT
            turn_tile(tag, src, 0, ready)
            turn_tile(tag, src, 1, ready)
            for i in range(SPLIT):
                pe.wait_ge(turned_lo.sem, turned_lo.at((tag, "tile", i // 2)))
                unit(c, i, A, (0,))
                if i >= 2:
                    turn_tile(tag, src, i, ready)
            for i in range(SPLIT):
                pe.wait_ge(turned_lo.sem, turned_lo.at((tag, "tile", 2 + i // 2)))
                unit(c, i, A, (1,))

        def ada_sum(c):
            _, l, n = c["key"]
            if c["before"] is not None:
                pair_free(c)
            pe.wait_ge(ada_used.sem, ada_used.at(c["units"][-1]["index"]))
            pe.matmul(BANK[SB_[n % 2]][:, :], con("ones"), MOD[:, n * CW:(n + 1) * CW],
                      start=True, stop=True).then_inc(product.sem, product.mark(c["key"]))

        def gemms(A, n=None, until=None):
            while todo and (todo[0]["key"][0] in until or todo[0]["kind"] == "ada"):
                c = todo.pop(0)
                if c["kind"] == "ada":
                    ada_sum(c)
                else:
                    for i in range(len(c["units"])):
                        unit(c, i, A)

        def turn(tag, src, groups, n, ready, ntiles=KT):
            g = groups[n]
            if n >= 2:
                pe.wait_ge(turned_lo.sem, turned_lo.at((tag, groups[n - 2])))
            signal_, event = ready(g)
            pe.wait_ge(signal_.sem, signal_.at(event))
            for t in range(NT):
                for j in range(min(2, ntiles - 2 * g)):
                    ins = pe.transpose(BANK[(TQ, TP)[n % 2]][:, (j * NT + t) * P:(j * NT + t + 1) * P],
                                       src[:, t, (2 * g + j) * P:(2 * g + j + 1) * P], con("ident"))
            ins.then_inc(turned.sem, turned.mark((tag, g)))

        def sums():
            while todo and todo[0]["kind"] == "ada":
                ada_sum(todo.pop(0))

        def turn_and_start(tag, src, ready, A, ntiles=KT, turned_before=0, between=None):
            n_groups = -(-ntiles // 2)
            c = todo.pop(0)
            for n in range(n_groups + 1):
                if between and n == 2:
                    ada_sum(between)
                if turned_before <= n < n_groups:
                    turn(tag, src, range(n_groups), n, ready, ntiles)
                if n:
                    pe.wait_ge(turned_lo.sem, turned_lo.at((tag, n - 1)))
                    unit(c, n - 1, A)

        def wide(tag, n, name):
            c = todo.pop(0)
            last = n - 1
            width = (FFN - last * CW if name == "ffo" else CW) // P
            for i in range(len(c["units"])):
                if i == 2 * last - 2:
                    turn_ffn(pe, turned, turned_lo, rows, drained, tag, last, width, BANK, TQ, TP, O, con)
                pe.wait_ge(turned_lo.sem, turned_lo.at((tag, i // 2, 1)))
                unit(c, i, AT)
            ending(AT)

        def attention(tag, heads, src, weave, pipe):
            real = lambda h: 0 <= h < len(heads) and heads[h]["kind"] != "I"
            for k in range(len(heads) + pipe["weigh"]):
                h = k - pipe["score"]
                if 0 <= h < len(heads):
                    hd = heads[h]
                    pe.wait_ge(qk_turned.sem, qk_turned.at((tag, h)))
                    if h >= 2:
                        by = exped if heads[h - 2]["kind"] == "I" else masked
                        pe.wait_ge(by.sem, by.at((tag, h - 2)))
                    bank = BANK[SB_[h % 2]]
                    slot = h % pipe["n_qk"]
                    q = pipe["qk"][:, slot, 0:S]
                    kk = KIT[:, :] if hd["kind"] == "I" else pipe["qk"][:, slot, S:2 * S]
                    pe.matmul(bank[:, 0:S], q[:, P:S], kk, start=True, stop=True)
                    pe.matmul(bank[:, S:S + P], q[:, 0:P], kk[:, 0:P], start=True, stop=True)\
                        .then_inc(scored.sem, scored.mark((tag, h)))
                if k < len(heads):
                    hd = heads[k]
                    n_tq = len(pipe["tq"])
                    if k >= n_tq:
                        pe.wait_ge(qk_turned.sem, qk_turned.at((tag, k - n_tq)))
                    with_k = hd["kind"] != "I" or hd["h"] == 0
                    for col, at in ((hd["q"], 0), (hd["k"], S))[:2 if with_k else 1]:
                        for t in range(NT):
                            ins = pe.transpose(BANK[pipe["tq"][k % n_tq]][0:DH, at + t * P:at + (t + 1) * P],
                                               src[:, t, col:col + DH], con("ident"))
                    ins.then_inc(qk_in_psum.sem, qk_in_psum.mark((tag, k)))
                n_tp = len(pipe["tp"])
                h = k - pipe["weigh"]
                if real(h):
                    bank = BANK[pipe["tp"][h % n_tp]]
                    pe.wait_ge(p_turned.sem, p_turned.at((tag, h)))
                    v = heads[h]["v"]
                    pt = pipe["pt"][:, h % pipe["n_pt"], :]
                    pe.matmul(bank[:, 384:448], pt[:, 0:P], src[:, 0, v:v + DH], start=True, stop=True)
                    pe.matmul(bank[:, 448:512], pt[:, P:2 * P], src[:, 0, v:v + DH], start=True, stop=False)
                    pe.matmul(bank[:, 448:512], pt[:, 2 * P:3 * P], src[:, 1, v:v + DH], start=False, stop=True)\
                        .then_inc(headed.sem, headed.mark((tag, h)))
                weave(k)
                h = k - pipe["turn"]
                if real(h):
                    pe.wait_ge(exped.sem, exped.at((tag, h)))
                    if real(h - n_tp):
                        pe.wait_ge(head_out.sem, head_out.at((tag, h - n_tp)))
                    bank = BANK[pipe["tp"][h % n_tp]]
                    for at, cols in ((0, slice(S, S + P)), (P, slice(0, P)), (2 * P, slice(P, S))):
                        ins = pe.transpose(bank[:, at:at + P], SM[:, h % N_SM, cols], con("ident"))
                    ins.then_inc(p_in_psum.sem, p_in_psum.mark((tag, h)))

        pe.wait_ge(const_in, 16)
        for c in range(3):
            ada_sum(todo.pop(0))
        for l in range(DEPTH):
            if l == 0:
                turn_and_start(("n1", l), O, lambda g: (rows, ("h", ("n1", l), g // 2)), HT, between=todo.pop(0))
            else:
                beginning(("n1", l), O, lambda t, half: (rows, ("h", ("n1", l), t, half)), HT)
            gemms(HT, until=("proj",))
            heads = heads_one()
            pe.wait_ge(drained.sem, drained.at(("proj", l, N_PROJ - 1)))

            def weave(k, l=l):
                if 3 <= k < 3 + HC + 1:
                    forget_products(l, k - 3)
                if k >= GATE_STEP and todo[0]["key"][0:2] == ("gate", l):
                    c = todo[0]
                    unit(c, (k - GATE_STEP) % 4, HT)
                    if (k - GATE_STEP) % 4 == 3:
                        todo.pop(0)

            def forget_products(l, c):
                if c == 0:
                    pe.wait_ge(rows.sem, rows.at(("logf", l)))
                    lf = LF.rearrange("p (t h) -> p t h", t=NT)
                    pe.matmul(BANK[TP][:, 0:HC], con("tri")[:, P:2 * P], lf[:, 0, :], start=True, stop=True)
                    pe.matmul(BANK[TP][:, HC:2 * HC], con("tri")[:, S:3 * P], lf[:, 0, :], start=True, stop=False)
                    pe.matmul(BANK[TP][:, HC:2 * HC], con("tri")[:, P:S], lf[:, 1, :], start=False, stop=True)\
                        .then_inc(forget.sem, forget.mark((l, "cols")))
                    return
                pe.wait_ge(rows.sem, rows.at(("logf_wide", l, c - 1)))
                pe.matmul(BANK[TP][:, 0:S], LB[:, 0, :], con("tri")[:, P:3 * P], start=True, stop=False)
                pe.matmul(BANK[TP][:, 0:S], LB[:, 1, :], con("tri")[:, 0:S], start=False, stop=True)\
                    .then_inc(forget.sem, forget.mark((l, c - 1)))

            attention(l, heads, PROJ, weave, ONE)

            def branch(cc, b):
                assert todo[0]["key"] == ("branch", l, cc, b)
                c = todo.pop(0)
                for i in range(len(c["units"])):
                    unit(c, i, HT)

            tag, order = ("o", l), (3, 2, 1, 0)
            kinds = {3: HI + HB + HC - 1, 2: len(heads) - 1, 1: len(heads) - 1, 0: len(heads) - 1}
            ready = lambda g: (head_out, (l, kinds[g]))
            turn(tag, O, order, 0, ready)
            turn(tag, O, order, 1, ready)
            turn(tag, O, order, 2, ready)
            pe.wait_ge(rows.sem, rows.at(("halves", l)))
            branch(0, "C")
            turn(tag, O, order, 3, ready)
            pe.wait_ge(turned_lo.sem, turned_lo.at((tag, 1)))
            branch(0, "B")
            pe.wait_ge(turned_lo.sem, turned_lo.at((tag, 0)))
            branch(0, "A")
            branch(1, "C")
            ready = lambda g: (rows, ("y", l, g // 2))
            turn(("y", l), O, range(4), 0, ready)
            turn(("y", l), O, range(4), 1, ready)
            branch(1, "B")
            branch(1, "A")
            turn_and_start(("y", l), O, ready, AT, turned_before=2)
            sums()
            ending(AT)
            beginning(("n2", l), O, lambda t, half: (rows, ("h", ("n2", l), t, half)), HT)
            n_ff = -(-FFN // CW)
            for j in range(n_ff):
                if j < n_ff:
                    for what in ("ffg", "ffu"):
                        if (what, j) != ("ffg", 0):
                            c = todo.pop(0)
                            assert c["key"] == (what, l, j)
                            for i in range(len(c["units"])):
                                unit(c, i, HT)
                        sums()
                        if what == "ffg" and j:
                            turn_ffn(pe, turned, turned_lo, rows, drained, ("a", l), j - 1, min(CW, FFN - (j - 1) * CW) // P, BANK, TQ, TP, O, con)
            wide(("a", l), n_ff, "ffo")
        for i in range(2):
            heads = heads_two(i)
            def start(t, half, i=i):
                if t == 0:
                    return rows, ("h", "final" if i == 0 else ("end2", 0), 0, half)
                return vec_used, ("final_g", half) if i == 0 else ("ln_mlp_b", 0, half)

            beginning(("x", i), X, start, HT)
            gemms(HT, until=("qkv",))
            pe.wait_ge(drained.sem, drained.at(("qkv", i, -(-3 * len(heads) * DH // CW) - 1)))
            attention(("two", i), heads, QKV, lambda k: None, TWO)
            turn_and_start(("o2", i), O, lambda g: (rows, "weighted") if i else (head_out, (("two", 0), len(heads) - 1 if g else 3)),
                           HT, len(heads) * DH // P)
            ending(HT)
            beginning(("m", i), X, lambda t, half, i=i: (vec_used, ("ln_mix_b", i, half)) if t else
                      (rows, ("h", ("mid", i), 0, half)), HT)
            for j in range(DFF // CW):
                if j:
                    c = todo.pop(0)
                    for u in range(len(c["units"])):
                        unit(c, u, HT)
                    turn_ffn(pe, turned, turned_lo, rows, drained, ("a2", i), j - 1, CW // P, BANK, TQ, TP, O, con)
            wide(("a2", i), DFF // CW, "mo")
        assert not todo

    last_unit = {c["key"]: c["units"][-1]["index"] for c in chunks if c["kind"] == "gemm"}

    def product_ready(e, key):
        c = by_key[key]
        if c["kind"] == "ada":
            e.wait_ge(product.sem, product.at(key))
            return [BANK[SB_[key[2] % 2]]]
        e.wait_ge(unit_used.sem, unit_used.at(last_unit[key]))
        return [BANK[2 * c["pair"] + t] for t in range(NT)]

    def tile_ready(e, key, t):
        if t == 0:
            e.wait_ge(product.sem, product.at(("first tile", key)))
        else:
            e.wait_ge(unit_used.sem, unit_used.at(last_unit[key]))
        return BANK[2 * by_key[key]["pair"] + t]

    @block.scalar
    def _(act):
        w_units = [i for i in ring if i["kind"] == "w"]
        done = [0]

        def prep(upto):
            while done[0] < min(upto, len(w_units)):
                u = w_units[done[0]]
                s, n, w = u["index"] % NH, u["n"], u["ncols"]
                raw_ready(act, u)
                if u["index"] >= NH:
                    act.wait_ge(unit_used.sem, unit_used.at(u["index"] - NH))
                act.activation(HI_[:, s, 0:n, 0:w], RAW[:, u["slot"], 0:n, 0:w], ACT.Copy)\
                    .then_inc(hi_ready.sem, hi_ready.mark(u["index"]))
                done[0] += 1

        def prep_chunk(key, ahead=NH):
            prep(last_unit[key] + 1 + ahead)

        def turn_hi(tag, A, ntiles=KT, order=None, part=slice(None)):
            for m, g in list(enumerate(order or range(-(-ntiles // 2))))[part]:
                n = min(2, ntiles - 2 * g)
                act.wait_ge(turned.sem, turned.at((tag, g)))
                act.activation(A[:, 2 * g:2 * g + n, 0, :], BANK[(TQ, TP)[m % 2]][:, 0:n * S].rearrange("p (k s) -> p k s", k=n),
                               ACT.Copy).then_inc(turned_hi.sem, turned_hi.mark((tag, g)))

        def turn_hi_ffn(tag, j, n):
            for t in range(NT):
                act.wait_ge(turned.sem, turned.at((tag, j, t)))
                act.activation(AT[:, 4 * j:4 * j + n, 0, t * P:(t + 1) * P], BANK[(TQ, TP)[t]][:, 0:n * P].rearrange("p (k s) -> p k s", k=n),
                               ACT.Copy).then_inc(turned_hi.sem, turned_hi.mark((tag, j, t)))

        def turn_hi_tile(tag, A, n):
            t, half = n // 2, n % 2
            act.wait_ge(turned.sem, turned.at((tag, "tile", n)))
            act.activation(A[:, 4 * half:4 * half + 4, 0, t * P:(t + 1) * P],
                           BANK[(TQ, TP)[n % 2]][:, :].rearrange("p (k s) -> p k s", k=4), ACT.Copy)\
                .then_inc(turned_hi.sem, turned_hi.mark((tag, "tile", n)))

        def squares(tag, half, event, tiles=range(NT)):
            signal_, name = event
            act.wait_ge(signal_.sem, signal_.at(name))
            if half:
                act.wait_ge(act_side.sem, act_side.at(("squares", tag, 0)))
            for t in tiles:
                ins = act.activation(SQ[:, t, :], X[:, t, half * CW:(half + 1) * CW], ACT.Square,
                                     accum_out=STAT[:, 2 * half + t:2 * half + t + 1])
            ins.then_inc(act_side.sem, act_side.mark(("squares", tag, half) if len(tiles) == NT else ("squares", tag, half, *tiles)))

        def bring_root_table(tag):
            act.activation(NMR[:, 0:1], con("eps")[:, 0:1], ACT.Sqrt).then_inc(act_chain.sem, act_chain.mark(("table", tag)))

        def root(tag, dst, src, eps, scale):
            act.wait_ge(rows.sem, rows.at(("var", tag)))
            act.activation(dst, src, ACT.Sqrt, scale=scale, bias=con("eps")[:, eps:eps + 1])\
                .then_inc(act_side.sem, act_side.mark(("root", tag)))

        def across_norm(key, tag, event, next_tag):
            m = min(SPLIT, len(by_key[key]["units"]))
            upto = last_unit[key] + 1 + NH - m
            prep(upto)
            bring_root_table(tag)
            for t in range(NT):
                if event is not None:
                    squares(tag, 1, (rows, ("x", event, 1, t)), (t,))
                    root((tag, t), RSTD[:, t:t + 1], STAT[:, t:t + 1], 0, 1.0 / D)
                else:
                    root((tag, t), RSTD[:, t:t + 1], MV[:, 2 * t + 1:2 * t + 2], 1, 1.0)
                for half in range(2):
                    prep(upto + min(m, 2 * t + half + 1))
                    if next_tag is not None:
                        turn_hi_tile(next_tag, HT, 2 * t + half)

        def attention(tag, heads, weave, pipe):
            for k in range(len(heads) + pipe["score"]):
                weave(k)
                if k < len(heads):
                    hd = heads[k]
                    bank = BANK[pipe["tq"][k % len(pipe["tq"])]]
                    slot = pipe["qk"][:, k % pipe["n_qk"], :]
                    act.wait_ge(qk_in_psum.sem, qk_in_psum.at((tag, k)))
                    if k >= pipe["n_qk"]:
                        act.wait_ge(scored.sem, scored.at((tag, k - pipe["n_qk"])))
                    if hd["kind"] == "I":
                        if hd["h"] == 0:
                            act.activation(KIT[:, :], bank[0:DH, S:2 * S], ACT.Copy)\
                                .then_inc(act_chain.sem, act_chain.mark(("kit", tag)))
                        act.activation(slot[:, 0:S], bank[0:DH, 0:S], ACT.Copy)\
                            .then_inc(qk_turned.sem, qk_turned.mark((tag, k)))
                    else:
                        act.activation(slot, bank[0:DH, :], ACT.Copy)\
                            .then_inc(qk_turned.sem, qk_turned.mark((tag, k)))
                h = k - pipe["score"]
                if h >= 0 and heads[h]["kind"] == "I":
                    act.wait_ge(scored.sem, scored.at((tag, h)))
                    if h >= N_SM:
                        act.wait_ge(masked.sem, masked.at((tag, h - N_SM)))
                    act.activation(SM[:, h % N_SM, :], BANK[SB_[h % 2]][:, 0:3 * P], ACT.Relu)\
                        .then_inc(exped.sem, exped.mark((tag, h)))
                elif h >= 0:
                    act.wait_ge(masked.sem, masked.at((tag, h)))
                    m = 2 * h
                    act.activation(SM[:, h % N_SM, S:S + P], SM[:, h % N_SM, S:S + P], ACT.Exp, bias=NM[:, m:m + 1],
                                   accum_out=RS[:, m:m + 1])
                    act.activation(SM[:, h % N_SM, 0:S], SM[:, h % N_SM, 0:S], ACT.Exp, bias=NM[:, m + 1:m + 2],
                                   accum_out=RS[:, m + 1:m + 2]).then_inc(exped.sem, exped.mark((tag, h)))

        def bias_rows(l):
            for h in range(HB):
                rel = bass.AP(scratch, (l * HB + h) * 3 * P, [[1, P], [1, S]])
                act.dma_start(MB[:, h, :], rel).then_inc(bias_in[h], 16)

        act.dma_start(RB[:, :], dram["rel_bias"].rearrange("l h r -> (l h) r")).then_inc(rel_in, 16)
        act.dma_start(POS[:, :], dram["positions"].rearrange("b (t p) -> (b p) t", p=P),
                      allow_slow_non_contiguous=True).then_inc(pos_in, 16)
        act.wait_ge(c_in, 16)
        act.activation(CT, COND, ACT.Tanh, scale=0.5).then_inc(act_side.sem, act_side.mark("cond"))
        for what, dst in (("sin", SIN), ("cos", COS)):
            act.wait_ge(rows.sem, rows.at(what))
            act.activation(dst, dst, ACT.Sin).then_inc(act_side.sem, act_side.mark(what))
        act.wait_ge(rows.sem, rows.at("rel"))
        act.dma_start(scratch[:, :], RE[:, :]).then_inc(scratch_in, 16)
        act.wait_ge(x_in, 16)
        for half in range(2):
            squares(("n1", 0), half, (act_side, "cond"))
        bring_root_table(("n1", 0))
        root(("n1", 0), RSTD, STAT[:, 0:NT], 0, 1.0 / D)
        prep(2)
        for l in range(DEPTH):
            if l == 0:
                turn_hi(("n1", l), HT, part=slice(0, 2))
                prep(3)
                turn_hi(("n1", l), HT, part=slice(2, 4))
                prep(NH)
                act.wait_ge(scratch_in, 16)
                bias_rows(0)
            for j in range(N_PROJ):
                prep_chunk(("proj", l, j))
            first = by_key[("gate", l, 0)]["units"][0]["index"]

            def gate_tanh(j, l=l):
                act.wait_ge(drained.sem, drained.at(("gate", l, j)))
                act.activation(GATES[:, :, j * CW:(j + 1) * CW], GATES[:, :, j * CW:(j + 1) * CW], ACT.Tanh, scale=0.5)\
                    .then_inc(act_side.sem, act_side.mark(("gate", l, j)))

            def weave(k, l=l):
                if k == 1:
                    act.wait_ge(rows.sem, rows.at(("nabs", l)))
                    act.activation(ZE, ZA, ACT.Exp).then_inc(act_side.sem, act_side.mark(("ze", l)))
                if k == 2:
                    act.wait_ge(rows.sem, rows.at(("zu", l)))
                    act.activation(ZL, ZU, ACT.Ln).then_inc(act_side.sem, act_side.mark(("zl", l)))
                prep(first + min(max(k - GATE_STEP, 0) + 1, 4 * N_GATE) + 3)
                if k >= 6 + GATE_STEP and (k - 6 - GATE_STEP) % 4 == 0:
                    gate_tanh((k - 6 - GATE_STEP) // 4)

            attention(l, heads_one(), weave, ONE)
            prep_chunk(("gate", l, N_GATE - 1))
            if (len(heads_one()) + ONE["score"] - 1 - 6 - GATE_STEP) // 4 < N_GATE - 1:
                gate_tanh(N_GATE - 1)
            if l + 1 < DEPTH:
                act.wait_ge(masked.sem, masked.at((l, HI + HB - 1)))
                bias_rows(l + 1)
            turn_hi(("o", l), HT, order=(3, 2, 1, 0))
            for cc in range(2):
                for b in "CBA":
                    prep_chunk(("branch", l, cc, b), 3)
                    if (cc, b) == (1, "C"):
                        turn_hi(("y", l), AT, part=slice(0, 2))
            turn_hi(("y", l), AT, part=slice(2, 4))
            prep_chunk(("wout", l, 0))
            squares(("n2", l), 0, (rows, ("x", ("mid1", l), 0)))
            across_norm(("wout", l, 1), ("n2", l), ("mid1", l), ("n2", l))
            n_ff = -(-FFN // CW)
            for j in range(n_ff):
                n = min(CW, FFN - j * CW)
                prep_chunk(("ffg", l, j))
                banks = product_ready(act, ("ffg", l, j))
                for t in range(NT):
                    if j >= 2:
                        act.wait_ge(drained.sem, drained.at(("ffu", l, j - 2)))
                    ins = act.activation(TG[:, j % 2, t, 0:n], banks[t][:, 0:n], ACT.Tanh, scale=0.5)
                ins.then_inc(act_side.sem, act_side.mark(("tg", l, j)))
                if j:
                    turn_hi_ffn(("a", l), j - 1, CW // P)
                prep_chunk(("ffu", l, j))
            first = by_key[("ffo", l, 0)]["units"][0]["index"]
            prep(first + 2 * n_ff - 4 + NH)
            turn_hi_ffn(("a", l), n_ff - 1, (FFN - (n_ff - 1) * CW) // P)
            following = ("n1", l + 1) if l + 1 < DEPTH else "final"
            prep_chunk(("ffo", l, 0))
            squares(following, 0, (rows, ("x", ("end", l), 0)))
            across_norm(("ffo", l, 1), following, ("end", l), following if l + 1 < DEPTH else ("x", 0))
        for i in range(2):
            heads = heads_two(i)
            for j in range(-(-3 * len(heads) * DH // CW)):
                prep_chunk(("qkv", i, j))
            attention(("two", i), heads, lambda k: None, TWO)
            if i == 1:
                act.wait_ge(rows.sem, rows.at("group_max"))
                act.activation(NM[:, 0:3 * 4 * NT], MX[:, 0:3 * 4 * NT], ACT.Exp)\
                    .then_inc(act_side.sem, act_side.mark("group_exp"))
            turn_hi(("o2", i), HT, len(heads) * DH // P)
            prep_chunk(("wo", i, 0))
            across_norm(("wo", i, 1), ("mid", i), None, ("m", i))
            for j in range(DFF // CW):
                prep_chunk(("mi", i, j))
                banks = product_ready(act, ("mi", i, j))
                if j >= 2:
                    act.wait_ge(rows.sem, rows.at(("a2", i, j - 2)))
                for t in range(NT):
                    ins = act.activation(RT[:, j % 2, t, :], banks[t][:, :], ACT.Relu)
                ins.then_inc(act_side.sem, act_side.mark(("relu", i, j)))
                if j:
                    turn_hi_ffn(("a2", i), j - 1, CW // P)
            first = by_key[("mo", i, 0)]["units"][0]["index"]
            prep(first + 2 * (DFF // CW) - 4 + NH)
            turn_hi_ffn(("a2", i), DFF // CW - 1, CW // P)
            prep_chunk(("mo", i, 0))
            across_norm(("mo", i, 1), ("end2", i), None, ("x", 1) if i == 0 else None)

    @block.vector
    def _(dve):
        v = nc.vector
        step = [0]

        def link(ins):
            step[0] += 1
            ins.then_inc(chain.sem, chain.mark(step[0]))
            dve.wait_ge(chain.sem, step[0])

        def tell(ins, signal_, event):
            ins.then_inc(signal_.sem, signal_.mark(event))
            dve.wait_ge(signal_.sem, signal_.at(event))

        def say(ins, event):
            tell(ins, rows, event)

        pos_in_stream = {}
        for n, i in enumerate(ring):
            if i["kind"] == "w":
                pos_in_stream[i["index"]] = n
        ada_units = [(n, i) for n, i in enumerate(ring) if i["kind"] == "ada"]
        ada_done = [0]
        ada_pending = []

        def ada_upto(n):
            while ada_done[0] < len(ada_units) and ada_units[ada_done[0]][0] < n:
                _, u = ada_units[ada_done[0]]
                ada_done[0] += 1
                cols = slice(u["c"] * CW, (u["c"] + 1) * CW)
                raw_ready(dve, u)
                for k in range(UNIT_K):
                    kt = u["i"] * UNIT_K + k
                    if kt == 0:
                        link(v.tensor_scalar(MOD[:, cols], RAW[:, u["slot"], k, :], COND[:, kt:kt + 1], None, ALU.mult))
                        continue
                    ins = v.scalar_tensor_tensor(MOD[:, cols], RAW[:, u["slot"], k, :], COND[:, kt:kt + 1], MOD[:, cols], ALU.mult, ALU.add)
                    if k < UNIT_K - 1:
                        link(ins)
                tell(ins, ada_used, u["index"])

        def ada_drain(key):
            _, l, c = key
            cols = slice(c * CW, (c + 1) * CW)
            b = vec_ready(dve, ("ada_b", l, c))
            bank = product_ready(dve, key)[0]
            tell(v.tensor_tensor(MOD[:, cols], bank[:, :], b, ALU.add), drained, key)
            name = {2: "norm1_g", 3: "norm1_g", 8: "norm2_g", 9: "norm2_g"}.get(c)
            if name:
                name = (name, l, c - 2 if c < 6 else c - 8)
                g = vec_ready(dve, name)
                tell(v.scalar_tensor_tensor(MOD[:, cols], MOD[:, cols], 1.0, g, ALU.add, ALU.mult), vec_used, name)

        order = [c["key"] for c in chunks]

        def before(key):
            i = order.index(key)
            nxt = next((c for c in chunks[i + 1:] if c["kind"] == "gemm"), None)
            if nxt is not None:
                ada_upto(pos_in_stream[min(nxt["units"][-1]["index"] + 1, len(pos_in_stream) - 1)])

        def after(key):
            i = order.index(key) + 1
            while i < len(order) and order[i][0] == "ada":
                ada_upto(1 + max(n for n, u in ada_units if (u["l"], u["c"]) == order[i][1:]))
                ada_drain(order[i])
                i += 1

        def turn_lo(tag, A, ntiles=KT, order=None, part=slice(None)):
            for m, g in list(enumerate(order or range(-(-ntiles // 2))))[part]:
                n = min(2, ntiles - 2 * g)
                dve.wait_ge(turned_hi.sem, turned_hi.at((tag, g)))
                tell(v.tensor_tensor(A[:, 2 * g:2 * g + n, 1, :], BANK[(TQ, TP)[m % 2]][:, 0:n * S].rearrange("p (k s) -> p k s", k=n),
                                A[:, 2 * g:2 * g + n, 0, :].bitcast(F32), ALU.subtract),
                    turned_lo, (tag, g))

        def turn_lo_ffn(tag, j, n):
            for t in range(NT):
                dve.wait_ge(turned_hi.sem, turned_hi.at((tag, j, t)))
                tell(v.tensor_tensor(AT[:, 4 * j:4 * j + n, 1, t * P:(t + 1) * P], BANK[(TQ, TP)[t]][:, 0:n * P].rearrange("p (k s) -> p k s", k=n),
                                AT[:, 4 * j:4 * j + n, 0, t * P:(t + 1) * P].bitcast(F32), ALU.subtract),
                    turned_lo, (tag, j, t))

        def turn_lo_tile(tag, A, n):
            t, half = n // 2, n % 2
            dve.wait_ge(turned_hi.sem, turned_hi.at((tag, "tile", n)))
            part = A[:, 4 * half:4 * half + 4, :, t * P:(t + 1) * P]
            tell(v.tensor_tensor(part[:, :, 1, :], BANK[(TQ, TP)[n % 2]][:, :].rearrange("p (k s) -> p k s", k=4),
                                 part[:, :, 0, :].bitcast(F32), ALU.subtract), turned_lo, (tag, "tile", n))

        def scaled(half, coef, tiles=range(NT)):
            for t in tiles:
                cols = slice(half * CW, (half + 1) * CW)
                ins = v.tensor_tensor(O[:, t, cols], X[:, t, cols], MOD[:, coef + half * CW:coef + (half + 1) * CW], ALU.mult)
            link(ins)

        def root_of_squares(tag):
            for half in range(2):
                dve.wait_ge(act_side.sem, act_side.at(("squares", tag, half)))
            say(v.tensor_tensor(STAT[:, 0:NT], STAT[:, 0:NT], STAT[:, 2:2 + NT], ALU.add), ("var", tag))
            dve.wait_ge(act_side.sem, act_side.at(("root", tag)))
            link(v.reciprocal(RR[:, 0:NT], RSTD))

        def h_rows(tag, shift, halves=range(2)):
            for half in halves:
                for t in range(NT):
                    cols = slice(half * CW, (half + 1) * CW)
                    ins = v.scalar_tensor_tensor(O[:, t, cols], O[:, t, cols], RR[:, t:t + 1],
                                                 MOD[:, shift + half * CW:shift + (half + 1) * CW], ALU.mult, ALU.add)
                say(ins, ("h", tag, half))

        def across_norm(take, norm, next_tag):
            take(0, 0)
            take(0, 1)
            norm(0)
            if next_tag is not None:
                turn_lo_tile(next_tag, HT, 0)
            take(1, 0)
            if next_tag is not None:
                turn_lo_tile(next_tag, HT, 1)
            take(1, 1)
            norm(1)
            if next_tag is not None:
                turn_lo_tile(next_tag, HT, 2)
                turn_lo_tile(next_tag, HT, 3)

        def reciprocal_root(tag, t):
            dve.wait_ge(act_side.sem, act_side.at(("root", (tag, t))))
            link(v.reciprocal(RR[:, t:t + 1], RSTD[:, t:t + 1]))

        def across_rms(key, gain, factor, tmp_of, event, tag, coef, shift, next_tag):
            def take(t, step):
                if step == 0:
                    bank = tile_ready(dve, key, t)
                    ins = v.scalar_tensor_tensor(tmp_of(t), bank[:, :], factor, MOD[:, gain + CW:gain + 2 * CW], ALU.mult, ALU.mult)
                    if t:
                        tell(ins, drained, key)
                    else:
                        link(ins)
                    return
                xs = X[:, t, CW:2 * CW]
                say(v.tensor_tensor(xs, xs, tmp_of(t), ALU.add), ("x", event, 1, t))

            def norm(t):
                if coef is not None:
                    scaled(1, coef, (t,))
                if t == 0:
                    dve.wait_ge(act_side.sem, act_side.at(("squares", tag, 0)))
                dve.wait_ge(act_side.sem, act_side.at(("squares", tag, 1, t)))
                say(v.tensor_tensor(STAT[:, t:t + 1], STAT[:, t:t + 1], STAT[:, 2 + t:3 + t], ALU.add), ("var", (tag, t)))
                reciprocal_root(tag, t)
                for half in range(2):
                    cols = slice(half * CW, (half + 1) * CW)
                    if coef is not None:
                        say(v.scalar_tensor_tensor(O[:, t, cols], O[:, t, cols], RR[:, t:t + 1],
                                                   MOD[:, shift + half * CW:shift + (half + 1) * CW], ALU.mult, ALU.add),
                            ("h", tag, t, half))
                        continue
                    g = vec_ready(dve, ("final_g", half))
                    ins = v.scalar_tensor_tensor(X[:, t, cols], X[:, t, cols], RR[:, t:t + 1], g, ALU.mult, ALU.mult)
                    if t:
                        vec_free(("final_g", half), ins)
                    else:
                        say(ins, ("h", tag, t, half))

            across_norm(take, norm, next_tag)

        def vec_free(name, ins):
            tell(ins, vec_used, name)

        def attention(tag, heads, mask_of, weave, pipe, outputs, late=None):
            for k in range(len(heads) + pipe["weigh"]):
                weave(k)
                h = k - pipe["score"]
                if 0 <= h < len(heads):
                    hd = heads[h]
                    if hd["kind"] == "I":
                        dve.wait_ge(exped.sem, exped.at((tag, h)))
                        for t, cols in ((1, slice(0, S)), (0, slice(S, S + P))):
                            acc = IDX[:, cols]
                            if h == 0:
                                prev = con("band")[:, 0:S] if t else con("band")[:, P:S]
                            else:
                                prev = acc
                            ins = v.scalar_tensor_tensor(acc, SM[:, h % N_SM, cols], PROJ[:, t, WI + h:WI + h + 1], prev, ALU.mult, ALU.add)
                        tell(ins, masked, (tag, h))
                    else:
                        dve.wait_ge(scored.sem, scored.at((tag, h)))
                        if h >= N_SM and heads[h - N_SM]["kind"] != "I":
                            dve.wait_ge(p_in_psum.sem, p_in_psum.at((tag, h - N_SM)))
                        m1, m0 = mask_of(hd)
                        m = 2 * h
                        bank = BANK[SB_[h % 2]]
                        v.tensor_tensor_reduce(SM[:, h % N_SM, S:S + P], bank[:, S:S + P], m0, SCALE, PICKED, ALU.add, ALU.max, MX[:, m:m + 1])
                        link(v.tensor_tensor_reduce(SM[:, h % N_SM, 0:S], bank[:, 0:S], m1, SCALE, PICKED, ALU.add, ALU.max, MX[:, m + 1:m + 2]))
                        tell(v.tensor_scalar(NM[:, m:m + 2], MX[:, m:m + 2], -1.0, None, ALU.mult), masked, (tag, h))
                n_tp = len(pipe["tp"])
                h = k - pipe["weigh"]
                if 0 <= h < len(heads) and heads[h]["kind"] != "I":
                    outputs(h, heads[h], BANK[pipe["tp"][h % n_tp]])
                if late:
                    late(k)
                h = k - pipe["turn"]
                if 0 <= h < len(heads) and heads[h]["kind"] != "I":
                    dve.wait_ge(p_in_psum.sem, p_in_psum.at((tag, h)))
                    if h >= pipe["n_pt"] and heads[h - pipe["n_pt"]]["kind"] != "I":
                        dve.wait_ge(headed.sem, headed.at((tag, h - pipe["n_pt"])))
                    tell(v.tensor_copy(pipe["pt"][:, h % pipe["n_pt"], :], BANK[pipe["tp"][h % n_tp]][:, 0:3 * P]), p_turned, (tag, h))

        def scaled_output(tag):
            def put(h, hd, bank):
                m = 2 * h
                dve.wait_ge(exped.sem, exped.at((tag, h)))
                link(v.reciprocal(RR[:, m:m + 2], RS[:, m:m + 2]))
                dve.wait_ge(headed.sem, headed.at((tag, h)))
                tell(v.tensor_tensor(O[:, :, hd["o"]:hd["o"] + DH], bank[:, 384:512].rearrange("p (t d) -> p t d", t=NT),
                                RR[:, m:m + 2].unsqueeze(2).to_broadcast([P, NT, DH]), ALU.mult),
                    head_out, (tag, h))
            return put

        dve.wait_ge(c_in, 16)
        dve.wait_ge(act_side.sem, act_side.at("cond"))
        link(v.scalar_tensor_tensor(COND, CT, 1.0, COND, ALU.add, ALU.mult))
        link(v.tensor_scalar(COND, COND, 0.5, None, ALU.mult))
        dve.wait_ge(rel_in, 16)
        link(v.tensor_copy(RE[:, 0:S], RB[:, 1:S + 1]))
        say(v.tensor_copy(RE[:, S:3 * P], RB[:, 2 * REL:2 * REL + 1].to_broadcast([DEPTH * HB, P])), "rel")
        dve.wait_ge(pos_in, 16)
        dve.wait_ge(const_in, 16)
        link(v.tensor_copy(POSF, POS[:, :]))
        for t in range(NT):
            link(v.tensor_scalar(ANG[:, 8 * t:8 * t + 8], con("inv"), POSF[:, t:t + 1], None, ALU.mult))
        magic = float(1.5 * 2 ** 23)
        two_pi = 2 * np.pi
        c1 = float(np.float32(6.28125))
        c2 = float(np.float32(round((two_pi - c1) * 2 ** 21) / 2 ** 21))
        c3 = float(np.float32(two_pi - c1 - c2))
        link(v.tensor_scalar(KR, ANG, float(1 / two_pi), magic, ALU.mult, ALU.add))
        link(v.tensor_scalar(KR, KR, -magic, None, ALU.add))
        link(v.scalar_tensor_tensor(RED, KR, -c1, ANG, ALU.mult, ALU.add))
        link(v.scalar_tensor_tensor(RED, KR, -c2, RED, ALU.mult, ALU.add))
        link(v.scalar_tensor_tensor(RED, KR, -c3, RED, ALU.mult, ALU.add))
        pi_in = float(np.nextafter(np.float32(np.pi), np.float32(0)))
        say(v.tensor_scalar(SIN, RED, pi_in, -pi_in, ALU.min, ALU.max), "sin")
        link(v.tensor_scalar(KR, RED, float(np.pi / 2), -float(two_pi), ALU.is_gt, ALU.mult))
        link(v.scalar_tensor_tensor(RED, RED, float(np.pi / 2), KR, ALU.add, ALU.add))
        say(v.tensor_scalar(COS, RED, pi_in, -pi_in, ALU.min, ALU.max), "cos")
        v.memset(HT[0:64, KT, :, :].bitcast(F32), 0.0)
        for n, c in enumerate((2, 3, 0)):
            ada_upto(KT // UNIT_K * (n + 1))
            if n:
                ada_drain(("ada", 0, (2, 3, 0)[n - 1]))
                if n == 1:
                    dve.wait_ge(x_in, 16)
                scaled(n - 1, D)
                if n == 1:
                    root_of_squares(("n1", 0))
        ada_upto(ada_units[12][0] + 1)
        ada_drain(("ada", 0, 0))

        for l in range(DEPTH):
            if l == 0:
                h_rows(("n1", l), 0, (0,))
                ada_upto(ada_units[13][0] + 1)
                turn_lo(("n1", l), HT, part=slice(0, 1))
                ada_upto(ada_units[14][0] + 1)
                turn_lo(("n1", l), HT, part=slice(1, 2))
                ada_upto(ada_units[15][0] + 1)
                ada_drain(("ada", 0, 1))
                h_rows(("n1", l), 0, (1,))
                turn_lo(("n1", l), HT, part=slice(2, 4))
            if l == 0:
                dve.wait_ge(act_side.sem, act_side.at("cos"))
            tmp = SM[:, :, :].rearrange("p a b -> p (a b)")

            def rope(col, n, l):
                for t in range(NT):
                    hv = PROJ[:, t, col:col + n * DH].rearrange("p (h d) -> p h d", d=DH)
                    x1, x2 = hv[:, :, 0:8], hv[:, :, 8:16]
                    cs = COS[:, 8 * t:8 * t + 8].unsqueeze(1).to_broadcast([P, n, 8])
                    sn = SIN[:, 8 * t:8 * t + 8].unsqueeze(1).to_broadcast([P, n, 8])
                    a, b, c, d = (tmp[:, 96 * i:96 * i + 8 * n].rearrange("p (h d) -> p h d", d=8) for i in range(4))
                    v.tensor_tensor(a, x1, cs, ALU.mult)
                    v.tensor_tensor(b, x2, sn, ALU.mult)
                    v.tensor_tensor(c, x2, cs, ALU.mult)
                    link(v.tensor_tensor(d, x1, sn, ALU.mult))
                    v.tensor_tensor(x1, a, b, ALU.subtract)
                    link(v.tensor_tensor(x2, c, d, ALU.add))

            for j in range(N_PROJ):
                key = ("proj", l, j)
                n = min(CW, PROJ_W - j * CW)
                before(key)
                b = vec_ready(dve, ("b_in", l, j))
                banks = product_ready(dve, key)
                v.tensor_tensor(PROJ[:, 0, j * CW:j * CW + n], banks[0][:, 0:n], b, ALU.add)
                tell(v.tensor_tensor(PROJ[:, 1, j * CW:j * CW + n], banks[1][:, 0:n], b, ALU.add), drained, key)
                if j == 1:
                    rope(QA, 2 * HA, l)
                if j == 3:
                    rope(QI, HI + 1, l)
                    wi = PROJ[:, :, WI:WI + HI]
                    link(v.tensor_scalar(wi, wi, float(np.float32(HI ** -0.5 * DH ** -0.5)), None, ALU.mult))
                after(key)
            z = PROJ[:, :, FC:FC + HC]
            as2 = lambda a: a.rearrange("p (t h) -> p t h", t=NT)
            link(v.tensor_scalar(as2(ZN), z, -1.0, None, ALU.mult))
            say(v.tensor_tensor(as2(ZA), as2(ZN), z, ALU.min), ("nabs", l))

            def log_forget(step, l=l):
                if step == 0:
                    dve.wait_ge(act_side.sem, act_side.at(("ze", l)))
                    say(v.tensor_scalar(ZU, ZE, 1.0, None, ALU.add), ("zu", l))
                    link(v.scalar_tensor_tensor(ZD, ZU, -1.0, ZE, ALU.add, ALU.subtract))
                    link(v.reciprocal(ZA, ZU))
                    link(v.tensor_tensor(ZD, ZD, ZA, ALU.mult))
                else:
                    dve.wait_ge(act_side.sem, act_side.at(("zl", l)))
                    link(v.tensor_tensor(ZL, ZL, ZD, ALU.subtract))
                    say(v.scalar_tensor_tensor(LF, ZN, 0.0, ZL, ALU.max, ALU.add), ("logf", l))

            def logf_wide(c, l=l):
                for t in range(NT):
                    ins = v.tensor_scalar(LB[:, t, :], con("ones"), LF[:, t * HC + c:t * HC + c + 1], None, ALU.mult)
                say(ins, ("logf_wide", l, c))

            def mask_of(hd, l=l):
                if hd["kind"] == "B":
                    return MB[:, hd["h"], ::-1], MB[:, hd["h"], 0:P][:, ::-1]
                if hd["kind"] == "C":
                    return CM[:, hd["h"], 0:S], CM[:, hd["h"], S:S + P]
                return IDX[:, 0:S], IDX[:, S:S + P]

            first = by_key[("gate", l, 0)]["units"][0]["index"]

            def weave(k, l=l, first=first):
                ada_upto(pos_in_stream[first + min(max(k - GATE_STEP, 0) + 4, 4 * N_GATE - 1)])
                if k in (1, 2):
                    log_forget(k - 1)
                if k == 3:
                    dve.wait_ge(forget.sem, forget.at((l, "cols")))
                    link(v.tensor_copy(F8, BANK[TP][:, 0:2 * HC]))
                    logf_wide(0)
                elif 4 <= k < 4 + HC:
                    c = k - 4
                    dve.wait_ge(forget.sem, forget.at((l, c)))
                    v.scalar_tensor_tensor(CM[:, c, 0:S], BANK[TP][:, 0:S], F8[:, HC + c:HC + c + 1], con("causal"), ALU.subtract, ALU.add)
                    link(v.scalar_tensor_tensor(CM[:, c, S:S + P], BANK[TP][:, 0:P], F8[:, c:c + 1], con("causal")[:, P:S], ALU.subtract, ALU.add))
                    if c + 1 < HC:
                        logf_wide(c + 1)
                if HI - HB <= k < HI:
                    h = k - (HI - HB)
                    dve.wait_ge(bias_in[h], 16 * (l + 1))
                    link(v.scalar_tensor_tensor(MB[:, h, :], MB[:, h, :], 1 / SCALE, con("band")[:, ::-1], ALU.mult, ALU.add))

            def late(k, l=l):
                u = k - GATE_STEP
                if u > 0 and u % 4 == 0:
                    key = ("gate", l, u // 4 - 1)
                    before(key)
                    b = vec_ready(dve, ("b_gate", l, u // 4 - 1))
                    banks = product_ready(dve, key)
                    j = u // 4 - 1
                    v.tensor_tensor(GATES[:, 0, j * CW:(j + 1) * CW], banks[0][:, :], b, ALU.add)
                    tell(v.tensor_tensor(GATES[:, 1, j * CW:(j + 1) * CW], banks[1][:, :], b, ALU.add), drained, key)
                    after(key)
                r = k - (HI + 2)
                if 0 <= r < TOPK // 8:
                    for a, cols in ((0, slice(0, S)), (8, slice(S, S + P))):
                        ins = v.max(MAX8[:, a:a + 8], IDX[:, cols])
                    link(ins)
                    for a, cols in ((0, slice(0, S)), (8, slice(S, S + P))):
                        ins = v.match_replace(IDX[:, cols], MAX8[:, a:a + 8], IDX[:, cols], PICKED)
                    link(ins)
                    if r == TOPK // 8 - 1:
                        link(v.tensor_scalar(IDX[:, :], IDX[:, :], PICKED, NEG, ALU.not_equal, ALU.mult))

            attention(l, heads_one(), mask_of, weave, ONE, scaled_output(l), late)

            def branch_out(cc, b):
                n = "ABC".index(b)
                key = ("branch", l, cc, b)
                banks = product_ready(dve, key)
                j = (n * D + cc * CW) // CW
                dve.wait_ge(act_side.sem, act_side.at(("gate", l, j)))
                for t in range(NT):
                    g = GATES[:, t, j * CW:(j + 1) * CW]
                    ins = v.scalar_tensor_tensor(O[:, t, cc * CW:(cc + 1) * CW] if b == "C" else g, g, 1.0, banks[t][:, :], ALU.add, ALU.mult)
                tell(ins, drained, key)
                if b != "C":
                    for t in range(NT):
                        ins = v.tensor_tensor(O[:, t, cc * CW:(cc + 1) * CW], O[:, t, cc * CW:(cc + 1) * CW],
                                              GATES[:, t, j * CW:(j + 1) * CW], ALU.add)
                    if b == "A":
                        say(ins, ("y", l, cc))
                    else:
                        link(ins)

            o_order = (3, 2, 1, 0)
            turn_lo(("o", l), HT, order=o_order, part=slice(0, 2))
            link(v.tensor_copy(HT[64:128, KT, :, :], HT[64:128, 5, :, :].bitcast(F32)))
            say(v.memset(HT[64:128, 5, :, :].bitcast(F32), 0.0), ("halves", l))
            turn_lo(("o", l), HT, order=o_order, part=slice(2, 4))
            for b in "CBA":
                branch_out(0, b)
            branch_out(1, "C")
            turn_lo(("y", l), AT, part=slice(0, 2))
            branch_out(1, "B")
            branch_out(1, "A")
            turn_lo(("y", l), AT, part=slice(2, 4))

            def add_to_x(key, gain, factor, tmp_of, event, coef):
                cc = key[-1]
                before(key)
                banks = product_ready(dve, key)
                for t in range(NT):
                    ins = v.scalar_tensor_tensor(tmp_of(t), banks[t][:, :], factor, MOD[:, gain + cc * CW:gain + (cc + 1) * CW], ALU.mult, ALU.mult)
                tell(ins, drained, key)
                for t in range(NT):
                    xs = X[:, t, cc * CW:(cc + 1) * CW]
                    ins = v.tensor_tensor(xs, xs, tmp_of(t), ALU.add)
                say(ins, ("x", event, cc))
                after(key)
                if coef is not None:
                    scaled(cc, coef)

            wout_tmp = lambda t: GATES[:, t, D:D + CW]
            add_to_x(("wout", l, 0), 2 * D, 0.5, wout_tmp, ("mid1", l), 4 * D)
            across_rms(("wout", l, 1), 2 * D, 0.5, wout_tmp, ("mid1", l), ("n2", l), 4 * D, 3 * D, ("n2", l))
            n_ff = -(-FFN // CW)
            for j in range(n_ff):
                n = min(CW, FFN - j * CW)
                kg, ku = ("ffg", l, j), ("ffu", l, j)
                before(kg)
                banks = product_ready(dve, kg)
                dve.wait_ge(act_side.sem, act_side.at(("tg", l, j)))
                for t in range(NT):
                    ins = v.scalar_tensor_tensor(TG[:, j % 2, t, 0:n], TG[:, j % 2, t, 0:n], 1.0, banks[t][:, 0:n], ALU.add, ALU.mult)
                tell(ins, drained, kg)
                after(kg)
                if j:
                    turn_lo_ffn(("a", l), j - 1, CW // P)
                before(ku)
                banks = product_ready(dve, ku)
                for t in range(NT):
                    ins = v.scalar_tensor_tensor(O[:, t, (j % 2) * CW:(j % 2) * CW + n], TG[:, j % 2, t, 0:n], 0.5, banks[t][:, 0:n], ALU.mult, ALU.mult)
                tell(ins, drained, ku)
                after(ku)
            turn_lo_ffn(("a", l), n_ff - 1, (FFN - (n_ff - 1) * CW) // P)
            ffo_tmp = lambda t: TG[:, 0, t, :]
            more = l + 1 < DEPTH
            following = ("n1", l + 1) if more else "final"
            add_to_x(("ffo", l, 0), 5 * D, 1.0, ffo_tmp, ("end", l), D if more else None)
            across_rms(("ffo", l, 1), 5 * D, 1.0, ffo_tmp, ("end", l), following, D if more else None, 0,
                       following if more else ("x", 0))

        stats = STAT.rearrange("p (t c s) -> p t c s", t=NT, c=2)

        def residual(key):
            banks = product_ready(dve, key)
            for t in range(NT):
                xs = X[:, t, 0:CW]
                ins = v.scalar_tensor_tensor(xs, xs, ALPHA, banks[t][:, :], ALU.mult, ALU.add)
            tell(ins, drained, key)
            for t in range(NT):
                ins = v.bn_stats(stats[:, t, 0, :], X[:, t, 0:CW])
            link(ins)

        def across_ln(key, tag, names, next_tag):
            g_name, b_name, i = names

            def take(t, step):
                xs = X[:, t, CW:2 * CW]
                if step == 0:
                    bank = tile_ready(dve, key, t)
                    ins = v.scalar_tensor_tensor(xs, xs, ALPHA, bank[:, :], ALU.mult, ALU.add)
                    if t:
                        tell(ins, drained, key)
                    else:
                        link(ins)
                else:
                    link(v.bn_stats(stats[:, t, 1, :], xs))

            def norm(t):
                say(v.bn_aggr(MV[:, 2 * t:2 * t + 2], STAT[:, 12 * t:12 * t + 12]), ("var", (tag, t)))
                reciprocal_root(tag, t)
                for half in range(2):
                    xs = X[:, t, half * CW:(half + 1) * CW]
                    g = vec_ready(dve, (g_name, i, half))
                    ins = v.scalar_tensor_tensor(xs, xs, MV[:, 2 * t:2 * t + 1], g, ALU.subtract, ALU.mult)
                    if t:
                        vec_free((g_name, i, half), ins)
                    else:
                        link(ins)
                    b = vec_ready(dve, (b_name, i, half))
                    ins = v.scalar_tensor_tensor(xs, xs, RR[:, t:t + 1], b, ALU.mult, ALU.add)
                    if t:
                        vec_free((b_name, i, half), ins)
                    else:
                        say(ins, ("h", tag, 0, half))

            across_norm(take, norm, next_tag)

        for i in range(2):
            heads = heads_two(i)
            nh = len(heads)
            w = 3 * nh * DH
            for j in range(-(-w // CW)):
                key = ("qkv", i, j)
                n = min(CW, w - j * CW)
                banks = product_ready(dve, key)
                rot = max(0, min(n, 2 * nh * DH - j * CW))
                for t in range(NT):
                    if rot:
                        r = rot // DH
                        four = lambda a: a.rearrange("p (h two d) -> p h two d", two=2, d=DH // 2)
                        wide = lambda name: con(name).rearrange("p (two d) -> p two d", two=2).unsqueeze(1).to_broadcast([P, r, 2, DH // 2])
                        px = banks[t][:, 0:rot]
                        v.tensor_tensor(four(RTMP[:, 0, 0:rot]), four(px), wide(f"cc{t}"), ALU.mult)
                        link(v.tensor_tensor(four(RTMP[:, 1, 0:rot]), four(px)[:, :, ::-1, :], wide(f"ss{t}"), ALU.mult))
                        ins = v.tensor_tensor(QKV[:, t, j * CW:j * CW + rot], RTMP[:, 0, 0:rot], RTMP[:, 1, 0:rot], ALU.add)
                    if rot < n:
                        if rot:
                            link(ins)
                        ins = v.tensor_copy(QKV[:, t, j * CW + rot:j * CW + n], banks[t][:, rot:n])
                    if t < NT - 1:
                        link(ins)
                tell(ins, drained, key)
            if i == 0:
                attention(("two", i), heads, lambda hd: (con("causal"), con("causal")[:, P:S]), lambda k: None, TWO,
                          scaled_output(("two", i)))
                dve.wait_ge(head_out.sem, head_out.at((("two", i), nh - 1)))
            else:
                dve.wait_ge(dil_in, 16)

                def raw_output(h, hd, bank):
                    dve.wait_ge(headed.sem, headed.at((("two", 1), h)))
                    tell(v.tensor_copy(O[:, :, hd["o"]:hd["o"] + DH], bank[:, 384:512].rearrange("p (t d) -> p t d", t=NT)),
                    head_out, (("two", 1), h))

                attention(("two", i), heads, lambda hd: (DILM[:, hd["h"] // 4, :], DILM[:, hd["h"] // 4, P:S]), lambda k: None,
                          TWO, raw_output)
                dve.wait_ge(head_out.sem, head_out.at((("two", i), nh - 1)))
                n2 = 4 * NT
                mx, rs, ww = MX[:, 0:3 * n2], RS[:, 0:3 * n2], NM[:, 0:3 * n2]
                gm = RR[:, 0:n2]
                link(v.tensor_tensor(gm, mx[:, 0:n2], mx[:, n2:2 * n2], ALU.max))
                link(v.tensor_tensor(gm, gm, mx[:, 2 * n2:3 * n2], ALU.max))
                for g in range(3):
                    ins = v.tensor_tensor(mx[:, g * n2:(g + 1) * n2], mx[:, g * n2:(g + 1) * n2], gm, ALU.subtract)
                say(ins, "group_max")
                dve.wait_ge(act_side.sem, act_side.at("group_exp"))
                link(v.tensor_tensor(rs, rs, ww, ALU.mult))
                link(v.tensor_tensor(gm, rs[:, 0:n2], rs[:, n2:2 * n2], ALU.add))
                link(v.tensor_tensor(gm, gm, rs[:, 2 * n2:3 * n2], ALU.add))
                link(v.reciprocal(gm, gm))
                for g in range(3):
                    ins = v.tensor_tensor(ww[:, g * n2:(g + 1) * n2], ww[:, g * n2:(g + 1) * n2], gm, ALU.mult)
                link(ins)
                for t in range(NT):
                    ot = O[:, t, 0:nh * DH].rearrange("p (h d) -> p h d", d=DH)
                    say(v.tensor_tensor(ot, ot, ww.rearrange("p (h t) -> p h t", t=NT)[:, :, t:t + 1].to_broadcast([P, nh, DH]), ALU.mult),
                        "weighted" if t == NT - 1 else "weighting")
            turn_lo(("o2", i), HT, nh * DH // P)
            residual(("wo", i, 0))
            across_ln(("wo", i, 1), ("mid", i), ("ln_mix_g", "ln_mix_b", i), ("m", i))
            for j in range(DFF // CW):
                key = ("mi", i, j)
                dve.wait_ge(act_side.sem, act_side.at(("relu", i, j)))
                if j >= 2:
                    dve.wait_ge(turned.sem, turned.at((("a2", i), j - 2, 1)))
                for t in range(NT):
                    ins = v.tensor_tensor(O[:, t, (j % 2) * CW:(j % 2 + 1) * CW], RT[:, j % 2, t, :], RT[:, j % 2, t, :], ALU.mult)
                say(ins, ("a2", i, j))
                if j:
                    turn_lo_ffn(("a2", i), j - 1, CW // P)
            turn_lo_ffn(("a2", i), DFF // CW - 1, CW // P)
            residual(("mo", i, 0))
            across_ln(("mo", i, 1), ("end2", i), ("ln_mlp_g", "ln_mlp_b", i), ("x", 1) if i == 0 else None)


def turn_ffn(pe, turned, turned_lo, rows, drained, tag, j, n, BANK, TQ, TP, O, con):
    signal_, event = (drained, ("ffu", tag[1], j)) if tag[0] == "a" else (rows, (*tag, j))
    pe.wait_ge(signal_.sem, signal_.at(event))
    for t in range(NT):
        if j:
            pe.wait_ge(turned_lo.sem, turned_lo.at((tag, j - 1, t)))
        for k in range(n):
            ins = pe.transpose(BANK[(TQ, TP)[t]][:, k * P:(k + 1) * P],
                               O[:, t, (j % 2) * CW + k * P:(j % 2) * CW + (k + 1) * P], con("ident"))
        ins.then_inc(turned.sem, turned.mark((tag, j, t)))


def unit_index(key):
    chunks, _ = plan()
    return next(c for c in chunks if c["key"] == key)["units"][0]["index"]


dil_at = unit_index(("mi", 0, 0))

_INS = ["x", "c", "positions", "ada_w", "ada_b", "norm1_g", "w_in", "b_in", "rel_bias", "w_branch", "w_out",
        "norm2_g", "w_ffn_in", "w_ffn_out", "final_g", "moba_w_qkv_2", "moba_w_o_2", "dil_w_qkv_2", "dil_w_o_2",
        "mlp_w_in_2", "mlp_w_out_2", "ln_mix_g_2", "ln_mix_b_2", "ln_mlp_g_2", "ln_mlp_b_2"]


def traced(nc, arrays, cat, book):
    dram = {}
    for name, a in arrays.items():
        short = name.removeprefix("in_").removesuffix("_2")
        dram[short] = nc.dram_tensor(name, a.shape, mybir.dt.from_np(a.dtype), kind="ExternalInput").ap()
    out = nc.dram_tensor("out_0_dram", (1, S, D), F32, kind="ExternalOutput").ap()
    build(nc, dram, out, cat, book)
    return nc


def kernel(**inputs):
    import concourse.bacc as bacc
    from concourse.bass_utils import run_bass_kernel_spmd

    const, cat = constants()
    arrays = {f"in_{name}": np.ascontiguousarray(inputs[name]) for name in _INS}
    arrays["in_constants"] = const
    values = {}
    traced(bacc.Bacc("TRN2", target_bir_lowering=False, num_devices=1), arrays, cat, ({}, values))
    nc = traced(bacc.Bacc("TRN2", target_bir_lowering=False, num_devices=1), arrays, cat, (values, {}))
    return run_bass_kernel_spmd(nc, [arrays], core_ids=[0]).results[0]["out_0_dram"]
```
